# Optimizing a Trainium2 kernel written in Bass

```python
import jax, jax.numpy as jnp
from jax import lax
import numpy as np

D_MODEL = 1024
BATCH = 1
SEQ = 1024
DEPTH = 2
DEC_BATCH = 8
DEC_SEQ = 8
PAST_LEN = 1024
PAGE_SIZE = 128

N_A_LAYERS = DEPTH // 2
N_B_LAYERS = DEPTH - N_A_LAYERS
D_CONV = D_MODEL
CONV_W = 3
N_HEADS = 16
HEAD_DIM = 64
D_ATT = N_HEADS * HEAD_DIM
D_PLE = 256
Q_BLOCK = 128
EPS = 1e-6
NEG_INF = -1e30

kernel_name = "yoco_shortconv_forgetting_attention_step"

def rmsnorm(x, g):
    xf = x.astype(jnp.float32)
    y = xf * lax.rsqrt(jnp.mean(xf * xf, axis=-1, keepdims=True) + EPS)
    return (y * g.astype(jnp.float32)).astype(x.dtype)

def short_conv_layer(x, conv_state, g, w_in, conv_w, w_out):
    h = rmsnorm(x, g)
    b_gate, c_gate, xin, z = jnp.split(h @ w_in, 4, axis=-1)
    u = c_gate * xin
    u_pad = jnp.concatenate([conv_state.astype(u.dtype), u], axis=1)
    T = u.shape[1]
    conv = conv_w[0] * u_pad[:, 0:T]
    for j in range(1, CONV_W):
        conv = conv + conv_w[j] * u_pad[:, j:j + T]
    y = b_gate * conv * jax.nn.silu(z)
    return x + y @ w_out, u_pad[:, -(CONV_W - 1):]

def shared_kv(x, g, w_kv, b_f):
    Bg, T = x.shape[:2]
    h = rmsnorm(x, g)
    k, v, fl = jnp.split(h @ w_kv, [D_ATT, 2 * D_ATT], axis=-1)
    k = k.reshape(Bg, T, N_HEADS, HEAD_DIM)
    v = v.reshape(Bg, T, N_HEADS, HEAD_DIM)
    logf = jax.nn.log_sigmoid(fl.astype(jnp.float32) + b_f.astype(jnp.float32))
    return k, v, logf

def forgetting_attn_layer(x, g, w_in, w_out, attend):
    Bg, T = x.shape[:2]
    h = rmsnorm(x, g)
    q, z = jnp.split(h @ w_in, 2, axis=-1)
    o = attend(q.reshape(Bg, T, N_HEADS, HEAD_DIM))
    y = o.reshape(Bg, T, D_ATT) * jax.nn.silu(z)
    return x + y @ w_out

def prompt_attention(q, k, v, logf):
    B, S, H, dh = q.shape
    scale = HEAD_DIM ** -0.5
    c = jnp.cumsum(logf, axis=1)
    ck = jnp.swapaxes(c, 1, 2)
    kpos = jnp.arange(S)
    nb = S // Q_BLOCK

    def block(args):
        qb, cqb, i = args
        qpos = i * Q_BLOCK + jnp.arange(Q_BLOCK)
        s = jnp.einsum('bqhd,bkhd->bhqk', qb, k).astype(jnp.float32) * scale
        s = s + jnp.swapaxes(cqb, 1, 2)[..., None] - ck[:, :, None, :]
        s = jnp.where(kpos[None, :] <= qpos[:, None], s, NEG_INF)
        p = jax.nn.softmax(s, axis=-1)
        return jnp.einsum('bhqk,bkhd->bqhd', p.astype(v.dtype), v)

    qb = q.reshape(B, nb, Q_BLOCK, H, dh).transpose(1, 0, 2, 3, 4)
    cqb = c.reshape(B, nb, Q_BLOCK, H).transpose(1, 0, 2, 3)
    out = lax.map(block, (qb, cqb, jnp.arange(nb)))
    return out.transpose(1, 0, 2, 3, 4).reshape(B, S, H, dh)

def sample_attention(q, k_new, v_new, logf_new, k_past, v_past, logf_past):
    T = q.shape[1]
    scale = HEAD_DIM ** -0.5
    cp = jnp.cumsum(logf_past, axis=1)
    cn = jnp.cumsum(logf_new, axis=1)
    rest = cp[:, -1:, :] - cp
    cn_q = jnp.swapaxes(cn, 1, 2)[..., None]
    s_past = jnp.einsum('bqhd,bkhd->bhqk', q, k_past).astype(jnp.float32) * scale
    s_past = s_past + cn_q + jnp.swapaxes(rest, 1, 2)[:, :, None, :]
    s_new = jnp.einsum('bqhd,bkhd->bhqk', q, k_new).astype(jnp.float32) * scale
    s_new = s_new + cn_q - jnp.swapaxes(cn, 1, 2)[:, :, None, :]
    causal = jnp.arange(T)[None, :] <= jnp.arange(T)[:, None]
    s_new = jnp.where(causal, s_new, NEG_INF)
    P = k_past.shape[1]
    p = jax.nn.softmax(jnp.concatenate([s_past, s_new], axis=-1), axis=-1)
    o = jnp.einsum('bhqk,bkhd->bqhd', p[..., :P].astype(v_past.dtype), v_past)
    o = o + jnp.einsum('bhqk,bkhd->bqhd', p[..., P:].astype(v_new.dtype), v_new)
    return o.astype(q.dtype)

def trunk(x, p, conv_state, make_attend, norm_a, w_in_a, conv_w_a, w_out_a,
          norm_kv, w_kv, b_f, norm_b, w_in_b, w_out_b, w_ple_proj, w_ple_gate, norm_f):
    new_conv = []
    k = v = logf = None
    attend = None
    for i in range(DEPTH):
        if i < N_A_LAYERS:
            x, st = short_conv_layer(x, conv_state[i], norm_a[i], w_in_a[i], conv_w_a[i], w_out_a[i])
            new_conv.append(st)
        else:
            if i == N_A_LAYERS:
                k, v, logf = shared_kv(x, norm_kv, w_kv, b_f)
                attend = make_attend(k, v, logf)
            j = i - N_A_LAYERS
            x = forgetting_attn_layer(x, norm_b[j], w_in_b[j], w_out_b[j], attend)
        x = x + jax.nn.sigmoid(x @ w_ple_gate[i]) * (p[i].astype(x.dtype) @ w_ple_proj[i])
    y = rmsnorm(x, norm_f)
    return y, jnp.stack(new_conv), k, v, logf.astype(x.dtype)

def setup_inputs(seed: int = 0) -> dict:
    key = jax.random.key(seed)
    ks = jax.random.split(key, 24)
    f32 = jnp.float32
    n_pages = PAST_LEN // PAGE_SIZE
    n_pool = (5 * DEC_BATCH * n_pages) // 4
    nrm = lambda k, shape, s: jax.random.normal(k, shape, f32) * s

    x_prompt = nrm(ks[0], (BATCH, SEQ, D_MODEL), 1.0)
    x_sample = nrm(ks[1], (DEC_BATCH, DEC_SEQ, D_MODEL), 1.0)
    p_prompt = nrm(ks[2], (DEPTH, BATCH, SEQ, D_PLE), 1.0)
    p_sample = nrm(ks[3], (DEPTH, DEC_BATCH, DEC_SEQ, D_PLE), 1.0)
    state_conv = nrm(ks[4], (N_A_LAYERS, DEC_BATCH, CONV_W - 1, D_CONV), 1.0)
    cache_k = nrm(ks[5], (n_pool, PAGE_SIZE, N_HEADS, HEAD_DIM), 1.0)
    cache_v = nrm(ks[6], (n_pool, PAGE_SIZE, N_HEADS, HEAD_DIM), 1.0)
    head_bias = 2.0 + 4.0 * jax.random.uniform(ks[7], (N_HEADS,), f32)
    cache_logf = jax.nn.log_sigmoid(head_bias + nrm(ks[8], (n_pool, PAGE_SIZE, N_HEADS), 1.0))
    page_table = jax.random.permutation(ks[9], n_pool)[:DEC_BATCH * n_pages].reshape(
        DEC_BATCH, n_pages).astype(jnp.int32)

    norm_a = 1.0 + nrm(ks[10], (N_A_LAYERS, D_MODEL), 0.02)
    w_in_a = nrm(ks[11], (N_A_LAYERS, D_MODEL, 4 * D_CONV), D_MODEL ** -0.5)
    conv_w_a = nrm(ks[12], (N_A_LAYERS, CONV_W, D_CONV), CONV_W ** -0.5)
    w_out_a = nrm(ks[13], (N_A_LAYERS, D_CONV, D_MODEL), 0.5 * D_CONV ** -0.5)
    norm_kv = 1.0 + nrm(ks[14], (D_MODEL,), 0.02)
    w_kv = nrm(ks[15], (D_MODEL, 2 * D_ATT + N_HEADS), D_MODEL ** -0.5)
    b_f = 2.0 + 4.0 * jax.random.uniform(ks[16], (N_HEADS,), f32)
    norm_b = 1.0 + nrm(ks[17], (N_B_LAYERS, D_MODEL), 0.02)
    w_in_b = nrm(ks[18], (N_B_LAYERS, D_MODEL, 2 * D_ATT), D_MODEL ** -0.5)
    w_out_b = nrm(ks[19], (N_B_LAYERS, D_ATT, D_MODEL), 0.5 * D_ATT ** -0.5)
    w_ple_proj = nrm(ks[20], (DEPTH, D_PLE, D_MODEL), 0.5 * D_PLE ** -0.5)
    w_ple_gate = nrm(ks[21], (DEPTH, D_MODEL, D_MODEL), D_MODEL ** -0.5)
    norm_f = 1.0 + nrm(ks[22], (D_MODEL,), 0.02)
    return {
        "x_prompt": x_prompt, "x_sample": x_sample, "p_prompt": p_prompt, "p_sample": p_sample,
        "state_conv": state_conv, "cache_k": cache_k, "cache_v": cache_v, "cache_logf": cache_logf,
        "page_table": page_table,
        "norm_a": norm_a, "w_in_a": w_in_a, "conv_w_a": conv_w_a, "w_out_a": w_out_a,
        "norm_kv": norm_kv, "w_kv": w_kv, "b_f": b_f,
        "norm_b": norm_b, "w_in_b": w_in_b, "w_out_b": w_out_b,
        "w_ple_proj": w_ple_proj, "w_ple_gate": w_ple_gate, "norm_f": norm_f,
    }

def reference(x_prompt, x_sample, p_prompt, p_sample, state_conv, cache_k, cache_v, cache_logf,
              page_table, norm_a, w_in_a, conv_w_a, w_out_a, norm_kv, w_kv, b_f,
              norm_b, w_in_b, w_out_b, w_ple_proj, w_ple_gate, norm_f):
    weights = (norm_a, w_in_a, conv_w_a, w_out_a, norm_kv, w_kv, b_f,
               norm_b, w_in_b, w_out_b, w_ple_proj, w_ple_gate, norm_f)

    zero_conv = jnp.zeros((N_A_LAYERS, x_prompt.shape[0], CONV_W - 1, D_CONV), x_prompt.dtype)

    def make_prompt_attend(k, v, logf):
        return lambda q: prompt_attention(q, k, v, logf)

    y_prompt, conv_prompt, k_prompt, v_prompt, logf_prompt = trunk(
        x_prompt, p_prompt, zero_conv, make_prompt_attend, *weights)

    db = x_sample.shape[0]
    k_past = cache_k[page_table].reshape(db, -1, N_HEADS, HEAD_DIM)
    v_past = cache_v[page_table].reshape(db, -1, N_HEADS, HEAD_DIM)
    logf_past = cache_logf[page_table].reshape(db, -1, N_HEADS).astype(jnp.float32)

    def make_sample_attend(k, v, logf):
        return lambda q: sample_attention(q, k, v, logf, k_past, v_past, logf_past)

    y_sample, conv_sample, k_sample, v_sample, logf_sample = trunk(
        x_sample, p_sample, state_conv, make_sample_attend, *weights)

    return (y_prompt, y_sample, conv_prompt, k_prompt, v_prompt, logf_prompt,
            conv_sample, k_sample, v_sample, logf_sample)


_drawn_inputs = setup_inputs


def setup_inputs(seed=0):
    import zlib

    import numpy as np

    out = dict(_drawn_inputs(seed))
    spreads = {}
    factors = {'norm_kv': 2.871, 'norm_b': 8.0, 'norm_f': 2.824}
    for name, (base, spread) in spreads.items():
        noise = np.random.default_rng([zlib.crc32(name.encode()), seed]).standard_normal(out[name].shape)
        drawn = base * np.exp(spread * noise) if base else spread * noise
        out[name] = __import__('jax').numpy.asarray(drawn.astype(out[name].dtype))
    for name, factor in factors.items():
        out[name] = (out[name] * factor).astype(out[name].dtype)
    return out
```

```python
from contextlib import ExitStack

import numpy as np
import concourse.bass as bass
from concourse import mybir

F32 = mybir.dt.float32
F32R = mybir.dt.float32r
BF16 = mybir.dt.bfloat16
I32 = mybir.dt.int32
ALU = mybir.AluOpType
ACT = mybir.ActivationFunctionType
AXX = mybir.AxisListType.X

P = 128
D = 1024
KC = D // P
SEQ, DB, DS = 1024, 8, 8
NS = DB * DS
TT = SEQ + NS
PLE, PC = 256, 2
H, HD = 16, 64
NPAIR = H // 2
PAGES, PAGE = 8, 128
CW = 3
EPS = 1e-6
NEG = -1e30
SCALE = HD ** -0.5
BLK = [(0, 364), (364, 728), (728, TT)]
NB = len(BLK)
QG = 4
BACK = [(0, 1, 2, 8), (3, 4, 5, 6), (7,)]
AUG = 4

G_A, G_KV, G_B, G_F, G_CW, G_ST, G_N = 0, 1, 2, 3, 4, 7, 24

N_A1, N_A2, N_A3, N_F, N_B1, N_B2, N_B3, N_END = 0, 32, 40, 48, 49, 81, 89, 97
B_A1, B_A2, B_A3 = 0, 96, 120
B_F = B_A3 + 48
B_B1 = B_F + 3
B_B2 = B_B1 + 96
B_B3 = B_B2 + 24
B_END = B_B3 + 48
EA_A1, EA_A2, EA_A3, EA_F, EA_B1, EA_B2, EA_B3, EA_END = 0, 48, 48, 72, 75, 171, 171, 195
ED_A1, ED_A2, ED_A3, ED_F, ED_B1, ED_B2, ED_B3, ED_END = 0, 48, 72, 96, 96, 96, 120, 144
LEAD = {
    "tensor": {"block_done": 6, "score": 1, "turned": 1, "pv": 1, "s_kturn": 8, "s_score": 1, "s_pv": 1},
    "vector": {"w_split": 2, "x_sum": 2, "dve_evac": 6, "kq_lo": 1, "o_done": 1, "p_lo": 1, "s_kt1": 1, "s_st": 2,
               "s_out": 1},
    "scalar": {"exp": 1, "s_kt0": 1, "s_exp": 1, "s_pt": 1},
    "sync": {"kv_out": 16, "y_out": 16},
}
START = {name: n for per in LEAD.values() for name, n in per.items()}


def f(x):
    return x.bitcast(F32)


def program(nc, a, o, d):
    es = ExitStack()
    with es:
        def sb(ctx, name, shape, dt=F32):
            return ctx.enter_context(nc.sbuf_tensor(name, shape, dt))

        def sem(name):
            return es.enter_context(nc.semaphore(name))

        Hhi = sb(es, "Hhi", [P, KC, TT], F32R)
        Hlo = sb(es, "Hlo", [P, KC, TT], F32R)
        raw = sb(es, "w_raw", [P, 2, KC + PC, P])
        whi = sb(es, "w_hi", [P, 2, KC + PC, P], F32R)
        wlo = sb(es, "w_lo", [P, 2, KC + PC, P], F32R)
        ident = sb(es, "ident", [P, P])
        ones = sb(es, "ones", [P, P])
        tri = sb(es, "tri", [P, P])
        identb = sb(es, "identb", [P, P], BF16)
        maskb = sb(es, "maskb", [P, P], BF16)
        same = sb(es, "same", [NS, NS])
        maskS = sb(es, "maskS", [NS, NS])
        GT = sb(es, "GT", [P, KC, G_N])
        bf_col = sb(es, "bf_col", [H, 1])
        small = sb(es, "small", [P, 16])
        qd = sb(es, "qd", [P, NPAIR, DB, 2 * DS])
        knT = sb(es, "knT", [P, NPAIR, NS])
        zsS = sb(es, "zsS", [P, NPAIR, NS])
        vnew = sb(es, "vnew", [NS, D])
        lfn = sb(es, "lfn", [P, 9, H])

        sa = ExitStack()
        X = sb(sa, "X", [P, KC, TT])
        Y = sb(sa, "Y", [P, KC, TT])
        sA = sb(sa, "scrA", [P, TT])
        sU = sb(sa, "scrU", [P, 2 + SEQ + DB * (DS + 2)])
        sC = sb(sa, "scrC", [P, TT])
        sZ = sb(sa, "scrZ", [P, TT])
        uc = sb(sa, "uc", [P, KC, 18])
        sa.close()
        Up = sU[:, 0:2 + SEQ]
        Us = sU[:, 2 + SEQ:].rearrange("p (b t) -> p b t", b=DB)
        ss, sq = sC, [sA, sZ]
        rs = sC
        sp_ = ExitStack()
        Xp = sb(sp_, "X_again", [P, KC, TT])
        PTh = sb(sp_, "PTh", [P, PC, TT], F32R)
        PTl = sb(sp_, "PTl", [P, PC, TT], F32R)
        sg = sb(sp_, "sg", [P, 2, TT])
        sp_.close()
        pn = sA
        pn2 = sZ
        pnS = sU

        s1 = ExitStack()
        KA = sb(s1, "KA", [P, 2, SEQ], F32R)
        KB = sb(s1, "KB", [HD + AUG, 2, SEQ], F32R)
        QA = sb(s1, "QA", [P, 2, SEQ], F32R)
        QB = sb(s1, "QB", [HD + AUG, 2, SEQ], F32R)
        VS = sb(s1, "VS", [P, PAGES, 2, P], F32R)
        Pb = sb(s1, "Pb", [P, QG, SEQ])
        pTh = sb(s1, "pTh", [P, 2, 512], F32R)
        pTl = sb(s1, "pTl", [P, 2, 512], F32R)
        st = sb(s1, "stage", [P, TT])
        zf = sb(s1, "zf", [P, TT])
        yT = sb(s1, "yT", [P, TT])
        KN = sb(s1, "KN", [P, 9, P])
        oT = sb(s1, "oT", [P, 512])
        s1.close()
        s0 = ExitStack()
        fl = sb(s0, "fl", [H, TT])
        fe = sb(s0, "fe", [H, TT])
        fu = sb(s0, "fu", [H, TT])
        fm = sb(s0, "fm", [H, TT])
        lfT = sb(s0, "lfT", [H, TT])
        one16 = sb(s0, "one16", [H, SEQ])
        ch = sb(s0, "ch", [H, 5, SEQ], F32R)
        s0.close()

        s2 = ExitStack()
        Kr = sb(s2, "Kring", [P, 4, D])
        KT = sb(s2, "KT", [P, 2, D])
        Vb = sb(s2, "Vb", [P, PAGES, D])
        Ps = sb(s2, "Ps", [P, PAGES * PAGE + NS])
        PsT = sb(s2, "PsT", [P, 9, P])
        ST = sb(s2, "ST", [P, 2, P])
        bias = sb(s2, "bias", [P, 2, P])
        LFP = sb(s2, "LFP", [P, PAGES, DB, H])
        rest = sb(s2, "rest", [P, PAGES, DB, H])
        CQ = sb(s2, "CQ", [P, DB, H, DS])
        NBs = sb(s2, "NBs", [NS, DB, H, DS])
        cn = sb(s2, "cn", [NS, H])
        pt = sb(s2, "pt", [1, DB * PAGES], I32)
        s2.close()
        Rq = Ps[0:NS, 0:DB * H * DS]

        PS = es.enter_context(nc.psum_tensor("PS", [P, 8, 512], F32))
        flat = PS[:, :, :].rearrange("p b n -> p (b n)")
        S = flat[:, 3 * 512:6 * 512]

        names = (
            "const_ready sp_step in_rows in_x0 in_x1 in_x2 w_in0 w_in1 w_gained w_hi w_split block_done act_evac dve_evac "
            "h_hi h_ready g_turned g_ready x_turned x_act x_dve x_sum x_parked x_back y_back y_merged out_dma "
            "uc_turned uc_act uc_out f_raw f_abs f_exp f_ln f_lf f_turned f_nat f_aug f_augdma "
            "aug_in staged kv_turned kv_nat kv_out kq_hi kq_lo v_hi v_lo z_exp z_done "
            "score rowmax exp rinv p_begun p_norm turned p_hi p_lo pv o_up o_done y_out "
            "s_table s_logf s_cn s_cnsb s_rq s_cq s_cqsb s_rest s_restsb s_bias s_kturn s_kt0 s_kt1 s_score "
            "s_st s_new s_newst s_all s_max s_exp s_norm s_back s_pt s_pv s_out "
            "y_norm y_turned y_act y_dve y_dma0 y_dma1").split()
        names += [f"{k}{i}" for i in range(4) for k in ("k_in",)] + [f"v_in{i}" for i in range(PAGES)]
        names += [f"n{r}_{k}" for r in range(3) for k in ("sq", "acc", "ps", "rt", "tmp")]
        names += [f"ple{r}_{k}" for r in range(2) for k in ("in", "turned", "hi", "lo")]
        sems = {k: sem(k) for k in names}

        def loaded(n0, per=2, i=0):
            return 32 * (n0 // 2 + 1) + 16 * per * i

        block = es.enter_context(nc.Block())

        wv = lambda w: w.rearrange("(k p) n -> p k n", p=P)
        row = lambda w: w.rearrange("(a n) -> a n", a=1)
        w_in_a, w_out_a = wv(a["w_in_a"][0]), wv(a["w_out_a"][0])
        w_kv, w_in_b, w_out_b = wv(a["w_kv"]), wv(a["w_in_b"][0]), wv(a["w_out_b"][0])
        w_gate = [wv(a["w_ple_gate"][i]) for i in range(2)]
        w_proj = [wv(a["w_ple_proj"][i]) for i in range(2)]
        x_p = a["x_prompt"][0].rearrange("(t p) c -> p t c", p=P)
        x_s = a["x_sample"].rearrange("b t c -> (b t) c")
        p_p = [a["p_prompt"][i, 0].rearrange("(t p) c -> p t c", p=P) for i in range(2)]
        p_s = [a["p_sample"][i].rearrange("b t c -> (b t) c") for i in range(2)]
        ck = a["cache_k"].rearrange("n s h d -> (n s) (h d)")
        cv = a["cache_v"].rearrange("n s h d -> (n s) (h d)")
        cl = a["cache_logf"].rearrange("n s h -> (n s) h")
        last_page = a["cache_k"].shape[0] - 1
        o_yp = o["y_prompt"][0].rearrange("(t p) c -> p t c", p=P)
        o_ys = o["y_sample"].rearrange("b t c -> (b t) c")
        o_kv = [(o[f"{x}_prompt"][0].rearrange("(t p) h d -> p t (h d)", p=P),
                 o[f"{x}_sample"].rearrange("b t h d -> (b t) (h d)")) for x in "kv"]
        A1_COLS = [D, 2 * D, 3 * D, 0]

        def peeled(eng, n, body):
            with eng.Fori(0, n - 1) as i:
                body(i, False)
            body(n - 1, True)

        def at_pair(t, j):
            return t[:, bass.ds(j, 1)]

        @block.sync
        def _(sp):
            for k, n in LEAD["sync"].items():
                sp.sem_inc(sems[k], n)
            sp.dma_start(Y[:, 0:4, 0:D], x_p[:, 0:4, :]).then_inc(sems["in_x0"], 16)
            for src, r, n in ((a["norm_a"][0:1, :], G_A, 1), (row(a["norm_kv"]), G_KV, 1),
                              (a["norm_b"][0:1, :], G_B, 1), (row(a["norm_f"]), G_F, 1),
                              (a["conv_w_a"][0], G_CW, CW), (a["state_conv"][0].rearrange("b w c -> (b w) c"), G_ST, 16),
                              (row(a["norm_f"]), G_N - 1, 1)):
                sp.dma_start(sZ[r:r + n, 0:D], src).then_inc(sems["in_rows"], 16)
            sp.dma_start(Y[:, 4:8, 0:D], x_p[:, 4:8, :]).then_inc(sems["in_x1"], 16)
            sp.dma_start(sA[0:NS, 0:D], x_s).then_inc(sems["in_x2"], 16)
            with nc.allow_non_contiguous_dma(reason="16 values, one per partition"):
                sp.dma_start(bf_col[:, :], a["b_f"].rearrange("(n a) -> n a", a=1)).then_inc(sems["in_rows"], 16)

            def load(n, par, src, proj=None, cols=P):
                sp.wait_ge(sems["w_split"], START["w_split"] + n - 1)
                sp.sem_inc(sems["sp_step"], 1)
                if proj is None:
                    for c in (0, 4):
                        sp.dma_start(raw[:, par, c:c + 4, 0:cols], src[:, c:c + 4, :]).then_inc(sems[f"w_in{par}"], 16)
                else:
                    sp.dma_start(raw[:, par, 0:KC, :], src).then_inc(sems[f"w_in{par}"], 16)
                    sp.dma_start(raw[:, par, KC:, :], proj).then_inc(sems[f"w_in{par}"], 16)

            def load_out(n0, w):
                with sp.Fori(0, KC // 2) as i:
                    for u in range(2):
                        load(n0 + 2 * i + u, (n0 + u) % 2, w[:, :, bass.ds(2 * P * i + P * u, P)])

            def load_feed(n0, r):
                for dst, src in ((sA[:, 0:D], p_p[r][:, 0:4, :]), (sZ[:, 0:D], p_p[r][:, 4:8, :])):
                    sp.dma_start(dst.rearrange("p (t c) -> p t c", c=PLE), src).then_inc(sems[f"ple{r}_in"], 16)
                sp.dma_start(sU[0:NS, 0:PLE], p_s[r]).then_inc(sems[f"ple{r}_in"], 16)
                with sp.Fori(0, KC // 2) as i:
                    for u in range(2):
                        c = bass.ds(2 * P * i + P * u, P)
                        load(n0 + 2 * i + u, (n0 + u) % 2, w_gate[r][:, :, c], w_proj[r][:, :, c])

            with sp.Fori(0, KC) as j:
                for t in range(4):
                    load(4 * j + t, t % 2, w_in_a[:, :, bass.ds(A1_COLS[t] + P * j, P)])
            load_out(N_A2, w_out_a)
            sp.wait_ge(sems["dve_evac"], START["dve_evac"] + ED_A2)
            load_feed(N_A3, 0)
            sp.wait_ge(sems["uc_act"], 2)
            sp.dma_start(o["conv_prompt"][0, 0], sC[0:2, 0:D]).then_inc(sems["uc_out"], 16)
            sp.dma_start(o["conv_sample"][0].rearrange("b w c -> (b w) c"), sC[2:18, 0:D]).then_inc(sems["uc_out"], 16)
            with nc.allow_non_contiguous_dma(reason="the last 16 columns of w_kv"):
                load(N_F, N_F % 2, w_kv[:, :, 2 * D:2 * D + H], cols=H)
            sp.wait_ge(sems["x_sum"], START["x_sum"] + 8)
            for k in range(KC):
                sp.dma_start(d["x"][k], X[:, k, :]).then_inc(sems["x_parked"], 16)
            sp.wait_ge(sems["f_nat"], 1)
            sp.dma_start(o["logf_prompt"][0].rearrange("(t p) h -> p t h", p=P), lfn[:, 0:8, :]).then_inc(sems["out_dma"], 16)
            sp.dma_start(o["logf_sample"].rearrange("b t h -> (b t) h"), lfn[0:NS, 8, :]).then_inc(sems["out_dma"], 16)
            sp.wait_ge(sems["f_aug"], 1)
            for r, (sk, sq_) in enumerate(((2, 4), (3, 4), (4, 0), (4, 1))):
                sp.dma_start(d["augk"][:, r, :], f(ch[:, sk, :])).then_inc(sems["f_augdma"], 16)
                sp.dma_start(d["augq"][:, r, :], f(ch[:, sq_, :])).then_inc(sems["f_augdma"], 16)
            sp.wait_ge(sems["f_augdma"], 128)

            with sp.Fori(0, NPAIR) as j:
                for t, (w, c0) in enumerate(((w_kv, 0), (w_kv, D), (w_in_b, 0), (w_in_b, D))):
                    load(N_B1 + 4 * j + t, (N_B1 + t) % 2, w[:, :, bass.ds(c0 + P * j, P)])
                    if t == 0:
                        sp.wait_ge(sems["score"], START["score"] + 16 * j)
                        sp.sem_inc(sems["sp_step"], 1)
                        for hh in range(2):
                            for dst, src in ((KB, d["augk"]), (QB, d["augq"])):
                                sp.dma_start(f(dst[HD:, hh, :]), src[bass.ds(2 * j + hh, 1)].rearrange("a r n -> (a r) n")).then_inc(sems["aug_in"], 16)
                for t, (o_p, o_s) in enumerate(o_kv):
                    sp.wait_ge(sems["kv_nat"], 2 * j + t + 1)
                    sp.sem_inc(sems["sp_step"], 1)
                    sp.dma_start(o_p[:, :, bass.ds(P * j, P)], KN[:, 0:8, :]).then_inc(sems["kv_out"], 16)
                    sp.dma_start(o_s[:, bass.ds(P * j, P)], KN[0:NS, 8, :]).then_inc(sems["kv_out"], 16)
                sp.wait_ge(sems["o_done"], START["o_done"] + 4 * j + 4)
                sp.sem_inc(sems["sp_step"], 1)
                sp.dma_start(d["y"][bass.ds(j, 1)].rearrange("a p n -> (a p) n"), yT[:, 0:SEQ]).then_inc(sems["y_out"], 16)

            sp.wait_ge(sems["y_out"], START["y_out"] + 16 * NPAIR)
            sp.wait_ge(sems["kv_out"], START["kv_out"] + 64 * NPAIR)
            sp.dma_start(pt[:, :], a["page_table"].rearrange("b (a n) -> a b n", a=1)).then_inc(sems["s_table"], 16)
            sp.wait_ge(sems["s_table"], 16)

            def page(b, pg):
                v = sp.value_load(pt[0:1, bass.ds(PAGES * b + pg, 1)], min_val=0, max_val=last_page)
                return bass.ds(v * PAGE, PAGE)
            with nc.allow_non_contiguous_dma(reason="16 log forget values per row"):
                with sp.Fori(0, DB) as b:
                    for pg in range(PAGES):
                        sp.dma_start(at_pair(LFP[:, pg], b).rearrange("p b h -> p (b h)"), cl[page(b, pg), :]).then_inc(sems["s_logf"], 16)
            with sp.Fori(0, DB) as b:
                for pg in range(PAGES):
                    rows = page(b, pg)
                    sp.wait_ge(sems["s_kturn"], START["s_kturn"] + 2 * PAGES * b + 2 * pg - 6)
                    sp.sem_inc(sems["sp_step"], 1)
                    sp.dma_start(Kr[:, pg % 4, :], ck[rows, :]).then_inc(sems[f"k_in{pg % 4}"], 16)
                for pg in range(PAGES):
                    rows = page(b, pg)
                    if pg == 0:
                        sp.wait_ge(sems["s_pv"], START["s_pv"] + b)
                        sp.sem_inc(sems["sp_step"], 1)
                    sp.dma_start(Vb[:, pg, :], cv[rows, :]).then_inc(sems[f"v_in{pg}"], 16)

            sp.wait_ge(sems["s_out"], START["s_out"] + DB)
            for k in range(KC):
                sp.dma_start(Y[:, k, 0:SEQ], d["y"][k]).then_inc(sems["y_back"], 16)
                sp.dma_start(X[:, k, :], d["x"][k]).then_inc(sems["x_back"], 16)
            load_out(N_B2, w_out_b)
            load_feed(N_B3, 1)
            for tt in range(9):
                n = P if tt < 8 else NS
                sp.wait_ge(sems["y_act"], tt + 1)
                sp.wait_ge(sems["y_dve"], tt + 1)
                sp.dma_start(o_yp[:, tt, :] if tt < 8 else o_ys, Y[0:n, tt % 2, 0:D]).then_inc(sems[f"y_dma{tt % 2}"], 16)
            sp.wait_ge(sems["y_dma0"], 80)
            sp.wait_ge(sems["y_dma1"], 64)
            sp.wait_ge(sems["out_dma"], 32)
            sp.wait_ge(sems["uc_out"], 32)

        @block.gpsimd
        def _(g):
            g.memset(ones[:, :], 1.0)
            g.memset(ident[:, :], 0.0)
            g.memset(tri[:, :], 0.0)
            g.memset(maskb[:, :], 0.0)
            g.memset(same[:, :], 1.0)
            g.memset(maskS[:, :], 0.0)
            g.memset(small[:, 15:16], EPS)
            g.memset(qd[:, :, :, :].rearrange("p a b c -> p (a b c)"), 0.0)
            g.drain()
            g.affine_select(out=ident[:, :], in_=ident[:, :], compare_op=ALU.not_equal, fill=1.0, base=0,
                            pattern=[[-1, P]], channel_multiplier=1)
            g.affine_select(out=tri[:, :], in_=tri[:, :], compare_op=ALU.is_ge, fill=1.0, base=0,
                            pattern=[[1, P]], channel_multiplier=-1)
            g.affine_select(out=maskb[:, :], in_=maskb[:, :], compare_op=ALU.is_ge, fill=NEG, base=0,
                            pattern=[[-1, P]], channel_multiplier=1)
            for m, fill in ((same, 0.0), (maskS, NEG)):
                g.affine_select(out=m[:, :], in_=m[:, :], compare_op=ALU.is_ge, fill=fill, base=0,
                                pattern=[[1, NS]], channel_multiplier=-1)
            g.drain()
            for m, fill in ((same, 0.0), (maskS, NEG)):
                v = m[:, :].rearrange("p (b t) -> p b t", b=DB)
                g.affine_select(out=v, in_=v, compare_op=ALU.is_ge, fill=fill, base=0,
                                pattern=[[-DS, DB], [0, DS]], channel_multiplier=1)
            g.tensor_copy(identb[:, :], ident[:, :])
            g.drain().then_inc(sems["const_ready"], 1)

            def gain(par, r, count, done=None):
                g.wait_ge(sems[f"w_in{par}"], count)
                w = raw[:, par, 0:KC, :]
                g.tensor_tensor(w, w, GT[:, :, r:r + 1].to_broadcast([P, KC, P]), ALU.mult).then_inc(sems["w_gained"], 1)
            g.wait_ge(sems["g_ready"], 1)
            gain(N_F % 2, G_KV, loaded(N_F))
            with g.Fori(0, NPAIR) as j:
                for t, r in enumerate((G_KV, G_KV, G_B, G_B)):
                    gain((N_B1 + t) % 2, r, loaded(N_B1 + t, 4, j))
                for c in range(16):
                    qb = c % 8
                    g.wait_ge(sems["rinv"], 16 * j + c + 1)
                    g.sem_inc(sems["p_begun"], 1)
                    pb = Pb[:, qb % QG, 0:(qb + 1) * P]
                    g.tensor_scalar(pb, pb, small[:, 8 + qb % QG:9 + qb % QG], 1.0, ALU.mult, ALU.mult).then_inc(sems["p_norm"], 1)
            g.wait_ge(sems["s_restsb"], 1)
            g.wait_ge(sems["s_cqsb"], 1)
            with g.Fori(0, DB) as b:
                for pg in range(PAGES):
                    g.wait_ge(sems["s_st"], START["s_st"] + PAGES * b + pg - 1)
                    g.tensor_tensor(bias[:, pg % 2, :].rearrange("p (h q) -> p h q", h=H),
                                    at_pair(CQ, b).rearrange("p b h q -> p (b h) q"),
                                    at_pair(rest[:, pg], b).rearrange("p b h -> p (b h)").unsqueeze(2).to_broadcast([P, H, DS]),
                                    ALU.add).then_inc(sems["s_bias"], 1)

        @block.tensor
        def _(pe):
            for k, n in LEAD["tensor"].items():
                pe.sem_inc(sems[k], n)
            mm, tp = pe.matmul, pe.transpose

            def tile(n, par, bank, free, hr=None, k0=0, nk=KC, hi=Hhi, lo=Hlo):
                pe.wait_ge(sems["w_split"], START["w_split"] + n + 1)
                for b, (s, e) in enumerate(BLK):
                    free(b)
                    for k in range(nk):
                        if hr is not None and b == 0:
                            pe.wait_ge(sems["h_ready"], hr + k + 1)
                        out = PS[:, bank + b, 0:e - s]
                        wh, wl = whi[:, par, k0 + k, :], wlo[:, par, k0 + k, :]
                        mm(out, wh, hi[:, k, s:e], start=(k == 0), stop=False)
                        mm(out, wh, lo[:, k, s:e], start=False, stop=False)
                        last = mm(out, wl, hi[:, k, s:e], start=False, stop=(k == nk - 1))
                    last.then_inc(sems["block_done"], 1)

            pe.wait_ge(sems["const_ready"], 1)
            pe.wait_ge(sems["in_rows"], 128)
            for k in range(KC):
                last = tp(PS[:, 7, k * G_N:(k + 1) * G_N], sZ[0:G_N, k * P:(k + 1) * P], ident[0:G_N, 0:G_N])
            last.then_inc(sems["g_turned"], 1)
            for k in range(KC):
                for h_ in range(2):
                    if k == 0:
                        pe.wait_ge(sems[f"in_x{h_}"], 16)
                    else:
                        pe.wait_ge(sems[("x_act", "x_dve")[h_]], (k, 2 * k - 1)[h_])
                    for i in range(4):
                        last = tp(PS[:, h_, i * P:(i + 1) * P], Y[:, 4 * h_ + i, k * P:(k + 1) * P], ident[:, :])
                    last.then_inc(sems["x_turned"], 1)
                pe.wait_ge(sems["in_x2"], 16) if k == 0 else pe.wait_ge(sems["x_dve"], 2 * k)
                tp(PS[:, 2, 0:NS], sA[0:NS, k * P:(k + 1) * P], ident[0:NS, 0:NS]).then_inc(sems["x_turned"], 1)

            def norm_sum(r):
                pe.wait_ge(sems[f"n{r}_acc"], KC - 1)
                for b, (s, e) in enumerate(BLK):
                    mm(PS[:, 3 + b, 0:e - s], ones[:, :], ss[:, s:e], start=True, stop=True).then_inc(sems[f"n{r}_ps"], 1)
            norm_sum(0)

            with pe.Fori(0, KC) as j:
                for t in range(4):
                    free = [lambda b: pe.wait_ge(sems["dve_evac"], START["dve_evac"] + 6 * j - 3 + b + 1), lambda b: pe.wait_ge(sems["act_evac"], 6 * j + b + 1),
                            lambda b: pe.wait_ge(sems["dve_evac"], START["dve_evac"] + 6 * j + b + 1), lambda b: pe.wait_ge(sems["act_evac"], 6 * j + 3 + b + 1)][t]
                    tile(4 * j + t, t % 2, 0, free, hr=0)

            def out_tiles(n0, ed0, hr):
                with pe.Fori(0, KC // 2) as i:
                    for u in range(2):
                        tile(n0 + 2 * i + u, (n0 + u) % 2, 0,
                             lambda b: pe.wait_ge(sems["dve_evac"], START["dve_evac"] + ed0 + 6 * i + 3 * u - 3 + b + 1), hr=hr)

            def feed(r, n0, ea0, ed0, hr):
                pe.wait_ge(sems[f"ple{r}_in"], 48)
                for c in range(PC):
                    for h_, src in enumerate((sA, sZ, sU)):
                        if c:
                            pe.wait_ge(sems[f"ple{r}_lo"], h_ + 1)
                        if h_ < 2:
                            for i in range(4):
                                last = tp(PS[:, 3 + h_, i * P:(i + 1) * P], src[:, i * PLE + c * P:i * PLE + (c + 1) * P], ident[:, :])
                        else:
                            last = tp(PS[:, 5, 0:NS], src[0:NS, c * P:(c + 1) * P], ident[0:NS, 0:NS])
                        last.then_inc(sems[f"ple{r}_turned"], 1)
                pe.wait_ge(sems[f"ple{r}_lo"], 6)
                pe.wait_ge(sems["dve_evac"], START["dve_evac"] + ed0)
                with pe.Fori(0, KC // 2) as i:
                    for u in range(2):
                        n, par = n0 + 2 * i + u, (n0 + u) % 2
                        tile(n, par, 0, lambda b: pe.wait_ge(sems["act_evac"], ea0 + 6 * i + 3 * u - 3 + b + 1), hr=hr)
                        tile(n, par, 3, lambda b: pe.wait_ge(sems["dve_evac"], START["dve_evac"] + ed0 + 6 * i + 3 * u - 3 + b + 1),
                             k0=KC, nk=PC, hi=PTh, lo=PTl)

            out_tiles(N_A2, ED_A2, 8)
            for c in range(2):
                for i in range(4):
                    last = tp(PS[0:18, 6 + c, i * P:(i + 1) * P], uc[:, 4 * c + i, :], ident[:, :])
                last.then_inc(sems["uc_turned"], 1)
            feed(0, N_A3, EA_A3, ED_A3, 16)
            norm_sum(1)
            pe.wait_ge(sems["act_evac"], EA_F)
            tile(N_F, N_F % 2, 0, lambda b: None, hr=24)
            pe.wait_ge(sems["f_lf"], 1)
            for t in range(9):
                n = P if t < 8 else NS
                last = tp(PS[0:n, 6, t * H:(t + 1) * H], lfT[:, t * P:t * P + n], ident[0:H, 0:H])
            last.then_inc(sems["f_turned"], 1)

            def turn_tile(j, t):
                pe.wait_ge(sems["staged"], 3 * j + t + 1)
                if t == 0:
                    pe.wait_ge(sems["exp"], START["exp"] + 16 * j)
                    pe.wait_ge(sems["p_lo"], START["p_lo"] + 24 * j)
                else:
                    pe.wait_ge(sems["kv_nat"], 2 * j + 1)
                for i in range(9):
                    n = P if i < 8 else NS
                    last = tp(PS[0:n, 3 + i // 4, (i % 4) * P:(i % 4 + 1) * P], st[:, i * P:i * P + n], ident[:, :])
                last.then_inc(sems["kv_turned"], 1)

            def scores(j, hh, qb):
                c = 8 * hh + qb
                n = (qb + 1) * P
                pe.wait_ge(sems["exp"], START["exp"] + 16 * j + c)
                if c == 0:
                    pe.wait_ge(sems["kv_nat"], 2 * j + 2)
                    pe.wait_ge(sems["kq_lo"], START["kq_lo"] + 2 * j + 2)
                    pe.wait_ge(sems["aug_in"], 64 * j + 64)
                q = slice(qb * P, (qb + 1) * P)
                for c0 in range(0, n, 512):
                    w = min(512, n - c0)
                    mm(S[:, c0:c0 + w], QA[:, hh, q], KA[:, hh, c0:c0 + w], start=True, stop=False)
                    mm(S[:, c0:c0 + w], QB[:, hh, q], KB[:, hh, c0:c0 + w], start=False, stop=(c0 + 512 < n))
                mm(S[:, qb * P:n], identb[:, :], maskb[:, :], start=False, stop=True).then_inc(sems["score"], 1)

            def turn_p(j, hh, grp, kb):
                u = 12 * hh + 4 * grp + kb
                q0 = max(0, kb - QG * grp)
                if kb == 0:
                    pe.wait_ge(sems["p_norm"], 16 * j + 8 * hh + QG * (grp + 1))
                pe.wait_ge(sems["p_lo"], START["p_lo"] + 24 * j + u - 1)
                for qi in range(q0, QG):
                    last = tp(PS[:, 5 + kb % 2, qi * P:(qi + 1) * P], Pb[:, qi, kb * P:(kb + 1) * P], ident[:, :])
                last.then_inc(sems["turned"], 1)

            def pv_step(j, hh, grp, kb):
                u = 12 * hh + 4 * grp + kb
                q0 = max(0, kb - QG * grp)
                nkb = QG * (grp + 1)
                if kb == 0:
                    pe.wait_ge(sems["o_done"], START["o_done"] + 4 * j + 2 * hh + grp)
                    pe.wait_ge(sems["v_lo"], j + 1)
                pe.wait_ge(sems["p_lo"], START["p_lo"] + 24 * j + u + 1)
                for x in (pTh, pTl):
                    last = mm(PS[:, 7, q0 * P:512], VS[:, kb, hh, :], x[:, kb % 2, q0 * P:512],
                              start=(kb == 0 and x is pTh), stop=(kb == nkb - 1 and x is pTl))
                last.then_inc(sems["pv"], 1)

            with pe.Fori(0, NPAIR) as j:
                for t in range(4):
                    tile(N_B1 + 4 * j + t, (N_B1 + t) % 2, 0,
                         lambda b: pe.wait_ge(sems["act_evac"], EA_B1 + 12 * j + 3 * t - 3 + b + 1))
                    if t < 2:
                        turn_tile(j, t)
                for hh in range(2):
                    for grp in range(2):
                        for qi in range(QG):
                            scores(j, hh, QG * grp + qi)
                        turn_p(j, hh, grp, 0)
                        for kb in range(QG * (grp + 1)):
                            if kb + 1 < QG * (grp + 1):
                                turn_p(j, hh, grp, kb + 1)
                            pv_step(j, hh, grp, kb)

            pe.wait_ge(sems["act_evac"], EA_B2)
            pe.wait_ge(sems["exp"], START["exp"] + 16 * NPAIR)
            pe.wait_ge(sems["p_lo"], START["p_lo"] + 24 * NPAIR)
            pe.wait_ge(sems["o_done"], START["o_done"] + 4 * NPAIR)
            mm(PS[0:NS, 6, 0:H], same[:, :], lfn[0:NS, 8, :], start=True, stop=True).then_inc(sems["s_cn"], 1)
            pe.wait_ge(sems["s_rq"], 1)
            for c in range(2):
                last = mm(PS[:, c, :], ones[0:NS, :], Rq[:, c * 512:(c + 1) * 512], start=True, stop=True)
            last.then_inc(sems["s_cq"], 1)
            pe.wait_ge(sems["s_logf"], 16 * DB * PAGES)
            for pg in range(PAGES):
                out = S[:, pg * P:(pg + 1) * P]
                for x in range(pg, PAGES):
                    last = mm(out, (tri if x == pg else ones)[:, :], LFP[:, x, :, :].rearrange("p b h -> p (b h)"),
                              start=(x == pg), stop=(x == PAGES - 1))
            last.then_inc(sems["s_rest"], 1)
            pe.wait_ge(sems["s_cqsb"], 1)
            pe.wait_ge(sems["s_restsb"], 1)

            def k_turn(b, pg):
                pe.wait_ge(sems[f"k_in{pg % 4}"], 32 * b + 16 * (pg // 4) + 16)
                for c in range(2):
                    pe.wait_ge(sems[f"s_kt{c}"], 1 + PAGES * b + pg)
                    for i in range(4 * c, 4 * c + 4):
                        last = tp(PS[:, c, (i % 4) * P:(i % 4 + 1) * P], Kr[:, pg % 4, i * P:(i + 1) * P], ident[:, :])
                    last.then_inc(sems["s_kturn"], 1)

            def q_of(b, i):
                return at_pair(qd[:, i], b).rearrange("p b n -> p (b n)")

            def s_turn(b, pg):
                pe.wait_ge(sems["s_st"], START["s_st"] + PAGES * b + pg + 1)
                tp(S[:, pg * P:(pg + 1) * P], ST[:, pg % 2, :], ident[:, :])

            with pe.Fori(0, DB) as b:
                k_turn(b, 0)
                for pg in range(PAGES):
                    if pg < PAGES - 1:
                        k_turn(b, pg + 1)
                    pe.wait_ge(sems["s_kt0"], START["s_kt0"] + PAGES * b + pg + 1)
                    pe.wait_ge(sems["s_kt1"], START["s_kt1"] + PAGES * b + pg + 1)
                    pe.wait_ge(sems["s_st"], START["s_st"] + PAGES * b + pg)
                    if pg == PAGES - 1:
                        pe.wait_ge(sems["s_out"], START["s_out"] + b)
                    for i in range(NPAIR):
                        last = mm(PS[:, 2, 16 * i:16 * i + 16], KT[:, pg % 2, i * P:(i + 1) * P], q_of(b, i), start=True, stop=True)
                    last.then_inc(sems["s_score"], 1)
                    if pg == 0:
                        pe.wait_ge(sems["s_exp"], START["s_exp"] + b)
                    else:
                        s_turn(b, pg - 1)
                for i in range(NPAIR):
                    last = mm(PS[0:NS, 6, 16 * i:16 * i + 16], knT[:, i, :], q_of(b, i), start=True, stop=True)
                last.then_inc(sems["s_new"], 1)
                pe.wait_ge(sems["s_newst"], b + 1)
                s_turn(b, PAGES - 1)
                tp(S[:, PAGES * PAGE:PAGES * PAGE + NS], PsT[0:NS, 8, :], ident[0:NS, 0:NS]).then_inc(sems["s_all"], 1)
                pe.wait_ge(sems["s_norm"], b + 1)
                for c in range(3):
                    pe.wait_ge(sems["s_pt"], START["s_pt"] + 3 * b + c)
                    for x, i in enumerate(BACK[c]):
                        n = P if i < 8 else NS
                        last = tp(PS[0:n, 7, x * P:(x + 1) * P], Ps[:, i * P:i * P + n], ident[:, :])
                    last.then_inc(sems["s_back"], 1)
                pe.wait_ge(sems["s_pt"], START["s_pt"] + 3 * b + 3)
                for pg in range(PAGES):
                    pe.wait_ge(sems[f"v_in{pg}"], 16 * b + 16)
                for i in range(NPAIR):
                    c = slice(i * P, (i + 1) * P)
                    for pg in range(PAGES):
                        mm(PS[:, 6, 16 * i:16 * i + 16], Vb[:, pg, c], PsT[:, pg, 16 * i:16 * i + 16], start=(pg == 0), stop=False)
                    last = mm(PS[:, 6, 16 * i:16 * i + 16], vnew[:, c], PsT[0:NS, 8, 16 * i:16 * i + 16], start=False, stop=True)
                last.then_inc(sems["s_pv"], 1)

            out_tiles(N_B2, ED_B2, 32)
            feed(1, N_B3, EA_B3, ED_B3, 40)
            norm_sum(2)
            pe.wait_ge(sems["y_norm"], KC)
            pe.wait_ge(sems["dve_evac"], START["dve_evac"] + ED_END)
            pe.wait_ge(sems["act_evac"], EA_END)
            for tt in range(9):
                n = P if tt < 8 else NS
                for c in range(2):
                    if tt:
                        pe.wait_ge(sems[("y_act", "y_dve")[c]], tt)
                    for i in range(4):
                        last = tp(PS[0:n, c, i * P:(i + 1) * P], X[:, 4 * c + i, tt * P:tt * P + n], ident[:, :])
                    last.then_inc(sems["y_turned"], 1)

        @block.scalar
        def _(act):
            for k, n in LEAD["scalar"].items():
                act.sem_inc(sems[k], n)
            af = act.activation

            def w_hi(par, blocks, count=None, gained=None, nk=KC):
                if gained is None:
                    act.wait_ge(sems[f"w_in{par}"], count)
                else:
                    act.wait_ge(sems["w_gained"], gained)
                act.wait_ge(sems["block_done"], START["block_done"] + blocks)
                af(whi[:, par, 0:nk, :], raw[:, par, 0:nk, :], ACT.Copy).then_inc(sems["w_hi"], 1)

            for k in range(KC):
                act.wait_ge(sems["x_turned"], 3 * k + 1)
                af(X[:, k, 0:512], PS[:, 0, :], ACT.Copy).then_inc(sems["x_act"], 1)
            w_hi(0, -3, loaded(0))

            def squares(r, x_ok):
                for k in range(KC):
                    x_ok(k)
                    if k >= 3:
                        act.wait_ge(sems[f"n{r}_acc"], k - 2)
                    af(ss[:, :] if k == 0 else sq[k % 2][:, :], X[:, k, :], ACT.Square).then_inc(sems[f"n{r}_sq"], 1)

            def roots(r):
                for b, (s, e) in enumerate(BLK):
                    act.wait_ge(sems[f"n{r}_ps"], b + 1)
                    af(rs[:, s:e], PS[:, 3 + b, 0:e - s], ACT.Sqrt, scale=1.0 / D, bias=small[:, 15:16]).then_inc(sems[f"n{r}_rt"], 1)

            def normed_hi(r):
                for k in range(KC):
                    act.wait_ge(sems[f"n{r}_tmp"], k + 1)
                    af(Hhi[:, k, :], sq[k % 2][:, :], ACT.Copy).then_inc(sems["h_hi"], 1)

            def split_hi(src):
                for k in range(KC):
                    af(Hhi[:, k, :], src[:, k, :], ACT.Copy).then_inc(sems["h_hi"], 1)

            act.wait_ge(sems["const_ready"], 1)
            act.wait_ge(sems["x_turned"], 3 * KC)
            act.drain()
            squares(0, lambda k: act.wait_ge(sems["x_dve"], 2 * k + 2))
            roots(0)
            normed_hi(0)

            def conv_layer(j, last):
                for t in range(4):
                    act.drain()
                    if last and t == 3:
                        w_hi(N_A2 % 2, 3 * (N_A2 - 1), loaded(N_A2))
                    else:
                        w_hi((t + 1) % 2, 12 * j + 3 * t, loaded(t + 1, 4, j))
                    if t in (0, 2):
                        act.wait_ge(sems["dve_evac"], START["dve_evac"] + 6 * j)
                        for b, (s, e) in enumerate(BLK):
                            act.wait_ge(sems["block_done"], START["block_done"] + 12 * j + 3 * t + b + 1)
                            if t == 0:
                                af(sA[:, s:e], PS[:, b, 0:e - s], ACT.Copy).then_inc(sems["act_evac"], 1)
                            else:
                                af(sZ[:, s:e], PS[:, b, 0:e - s], ACT.Silu).then_inc(sems["act_evac"], 1)
            peeled(act, KC, conv_layer)
            act.wait_ge(sems["dve_evac"], START["dve_evac"] + ED_A2)
            act.wait_ge(sems["block_done"], START["block_done"] + B_A2)
            split_hi(Y)

            def out_tiles(n0, b0):
                def body(i, last):
                    for u in range(2):
                        n = n0 + u + 1
                        if last and u == 1:
                            w_hi(n % 2, b0 + 21, loaded(n, 2, 3), nk=KC + PC)
                        else:
                            w_hi(n % 2, b0 + 6 * i + 3 * u, loaded(n, 2, i))
                peeled(act, KC // 2, body)

            def feed(r, n0, b0, ed0, next_hi):
                for g_ in range(6):
                    act.wait_ge(sems[f"ple{r}_turned"], g_ + 1)
                    c, h_ = divmod(g_, 3)
                    n = 512 if h_ < 2 else NS
                    af(PTh[:, c, h_ * 512:h_ * 512 + n], PS[:, 3 + h_, 0:n], ACT.Copy).then_inc(sems[f"ple{r}_hi"], 1)
                act.wait_ge(sems["dve_evac"], START["dve_evac"] + ed0)
                act.wait_ge(sems["block_done"], START["block_done"] + b0)
                split_hi(X)

                def body(i, last):
                    for u in range(2):
                        if last and u == 1:
                            if next_hi:
                                next_hi(b0 + 42)
                        else:
                            w_hi((n0 + u + 1) % 2, b0 + 12 * i + 6 * u, loaded(n0 + u + 1, 2, i), nk=KC + PC)
                        act.wait_ge(sems["x_sum"], START["x_sum"] + 8 * r + 2 * i + u - 1)
                        for b, (s, e) in enumerate(BLK):
                            act.wait_ge(sems["block_done"], START["block_done"] + b0 + 12 * i + 6 * u + b + 1)
                            af(sg[:, u, s:e], PS[:, b, 0:e - s], ACT.Sigmoid).then_inc(sems["act_evac"], 1)
                peeled(act, KC // 2, body)

            out_tiles(N_A2, B_A2)
            for c in range(2):
                act.wait_ge(sems["uc_turned"], c + 1)
                af(sC[0:18, c * 512:(c + 1) * 512], PS[0:18, 6 + c, :], ACT.Copy).then_inc(sems["uc_act"], 1)
            act.drain()
            feed(0, N_A3, B_A3, ED_A3, lambda blocks: w_hi(N_F % 2, blocks, gained=1))
            act.drain()
            act.wait_ge(sems["uc_out"], 32)
            squares(1, lambda k: act.wait_ge(sems["x_sum"], START["x_sum"] + k + 1))
            roots(1)
            act.wait_ge(sems["block_done"], START["block_done"] + B_F)
            normed_hi(1)

            act.wait_ge(sems["x_parked"], 16 * KC)
            for b, (s, e) in enumerate(BLK):
                act.wait_ge(sems["block_done"], START["block_done"] + B_F + b + 1)
                af(fl[:, s:e], PS[0:H, b, 0:e - s], ACT.Identity, bias=bf_col[:, 0:1]).then_inc(sems["act_evac"], 1)
            act.drain().then_inc(sems["f_raw"], 1)
            act.wait_ge(sems["f_abs"], 1)
            af(fe[:, :], fu[:, :], ACT.Exp)
            act.drain()
            af(fm[:, :], fe[:, :], ACT.Ln, bias=1.0).then_inc(sems["f_ln"], 1)
            act.wait_ge(sems["f_turned"], 1)
            af(lfn[:, 0:8, :].rearrange("p t h -> p (t h)"), PS[:, 6, 0:8 * H], ACT.Copy)
            af(lfn[0:NS, 8, :], PS[0:NS, 6, 8 * H:9 * H], ACT.Copy)
            act.drain().then_inc(sems["f_nat"], 1)
            w_hi(N_B1 % 2, B_F, gained=2)

            def attention(j, hh):
                for grp in range(2):
                    for qi in range(QG):
                        qb = QG * grp + qi
                        n = (qb + 1) * P
                        act.wait_ge(sems["rowmax"], 16 * j + 8 * hh + qb + 1)
                        af(Pb[:, qi, 0:n], S[:, 0:n], ACT.Exp, bias=small[:, qi:qi + 1],
                           accum_out=small[:, 4 + qi:5 + qi])
                        act.drain().then_inc(sems["exp"], 1)
                    for kb in range(QG * (grp + 1)):
                        u = 12 * hh + 4 * grp + kb
                        q0 = max(0, kb - QG * grp)
                        act.wait_ge(sems["turned"], START["turned"] + 24 * j + u + 1)
                        act.wait_ge(sems["pv"], START["pv"] + 24 * j + u - 1)
                        af(pTh[:, kb % 2, q0 * P:512], PS[:, 5 + kb % 2, q0 * P:512], ACT.Copy).then_inc(sems["p_hi"], 1)
                    act.wait_ge(sems["pv"], START["pv"] + 24 * j + 12 * hh + (4, 12)[grp])
                    act.wait_ge(sems["o_done"], START["o_done"] + 4 * j + 2 * hh + grp)
                    af(oT[64 * hh:64 * hh + 64, :], PS[64:128, 7, :], ACT.Copy).then_inc(sems["o_up"], 1)

            def pair(j, last):
                for t in range(4):
                    act.drain()
                    if t < 3:
                        w_hi((N_B1 + t + 1) % 2, B_B1 + 12 * j + 3 * t, gained=3 + 4 * j + t)
                    if t == 0:
                        act.wait_ge(sems["kq_lo"], START["kq_lo"] + 2 * j)
                    elif t < 3:
                        act.wait_ge(sems["kv_turned"], 2 * j + t)
                        act.wait_ge(sems["kq_lo"], START["kq_lo"] + 2 * j + 1)
                    else:
                        act.wait_ge(sems["o_done"], START["o_done"] + 4 * j)
                        act.wait_ge(sems["y_out"], START["y_out"] + 16 * j)
                    for b, (s, e) in enumerate(BLK):
                        act.wait_ge(sems["block_done"], START["block_done"] + B_B1 + 12 * j + 3 * t + b + 1)
                        af((st, st, st, zf)[t][:, s:e], PS[:, b, 0:e - s], ACT.Copy,
                           scale=SCALE if t == 2 else 1.0).then_inc(sems["act_evac"], 1)
                    if t < 3:
                        act.drain().then_inc(sems["staged"], 1)
                    else:
                        act.drain()
                    if t == 0:
                        act.wait_ge(sems["score"], START["score"] + 16 * j)
                        for hh in range(2):
                            for half in range(2):
                                af(KA[64 * half:64 * half + 64, hh, :], st[64 * hh:64 * hh + 64, 0:SEQ], ACT.Copy)
                        act.drain().then_inc(sems["kq_hi"], 1)
                    if t == 1:
                        act.wait_ge(sems["kv_nat"], 2 * j + 2)
                        act.wait_ge(sems["pv"], START["pv"] + 24 * j)
                        af(VS[:, :, :, 0:HD], KN[:, 0:8, :].rearrange("p t (h n) -> p t h n", h=2), ACT.Copy).then_inc(sems["v_hi"], 1)
                    if t == 2:
                        for hh in range(2):
                            rows = st[64 * hh:64 * hh + 64, 0:SEQ]
                            af(QA[64 * hh:64 * hh + 64, hh, :], rows, ACT.Copy)
                            af(QB[0:HD, hh, :], rows, ACT.Copy)
                        act.drain().then_inc(sems["kq_hi"], 1)
                    if t == 3:
                        af(yT[:, :], zf[:, :], ACT.Exp, scale=-1.0).then_inc(sems["z_exp"], 1)
                attention(j, 0)
                attention(j, 1)
                if not last:
                    w_hi((N_B1 + 4) % 2, B_B1 + 12 * j + 9, gained=3 + 4 * j + 3)
            peeled(act, NPAIR, pair)

            act.drain()
            with act.Fori(0, DB) as b:
                for pg in range(PAGES):
                    act.wait_ge(sems["s_kturn"], START["s_kturn"] + 2 * PAGES * b + 2 * pg + 1)
                    act.wait_ge(sems["s_score"], START["s_score"] + PAGES * b + pg - 1)
                    af(KT[:, pg % 2, 0:512], PS[:, 0, :], ACT.Copy).then_inc(sems["s_kt0"], 1)
                act.wait_ge(sems["s_max"], b + 1)
                af(Ps[:, :], S[:, 0:PAGES * PAGE + NS], ACT.Exp, bias=small[:, 0:1], accum_out=small[:, 4:5])
                act.drain().then_inc(sems["s_exp"], 1)
                for c in range(3):
                    act.wait_ge(sems["s_back"], 3 * b + c + 1)
                    if c == 0:
                        af(PsT[0:NS, 8, :], PS[0:NS, 7, 3 * P:], ACT.Copy)
                    k0, nk = BACK[c][0], len(BACK[c]) - (c == 0)
                    af(PsT[:, k0:k0 + nk, :].rearrange("p t n -> p (t n)"), PS[:, 7, 0:nk * P], ACT.Copy)
                    act.drain().then_inc(sems["s_pt"], 1)

            act.drain()
            act.wait_ge(sems["y_back"], 16 * KC)
            act.wait_ge(sems["y_merged"], 1)
            w_hi(N_B2 % 2, B_B2 - 3, loaded(N_B2))
            split_hi(Y)
            out_tiles(N_B2, B_B2)
            feed(1, N_B3, B_B3, ED_B3, None)
            act.drain()
            squares(2, lambda k: act.wait_ge(sems["x_sum"], START["x_sum"] + 8 + k + 1))
            roots(2)
            act.drain()
            for tt in range(9):
                n = P if tt < 8 else NS
                act.wait_ge(sems["y_turned"], 2 * tt + 1)
                if tt >= 2:
                    act.wait_ge(sems[f"y_dma{tt % 2}"], 16 * (tt // 2))
                af(Y[0:n, tt % 2, 0:512], PS[0:n, 0, :], ACT.Copy).then_inc(sems["y_act"], 1)

        @block.vector
        def _(ve):
            for k, n in LEAD["vector"].items():
                ve.sem_inc(sems[k], n)
            tt_, ts_, stt = ve.tensor_tensor, ve.tensor_scalar, ve.scalar_tensor_tensor

            def w_lo(par, n, nk=KC):
                ve.wait_ge(sems["w_hi"], n + 1)
                tt_(wlo[:, par, 0:nk, :], raw[:, par, 0:nk, :], f(whi[:, par, 0:nk, :]), ALU.subtract).then_inc(sems["w_split"], 1)

            ve.wait_ge(sems["g_turned"], 1)
            ve.tensor_copy(GT[:, :, :].rearrange("p k n -> p (k n)"), PS[:, 7, 0:KC * G_N]).then_inc(sems["g_ready"], 1)
            for k in range(KC):
                ve.wait_ge(sems["x_turned"], 3 * k + 2)
                ve.tensor_copy(X[:, k, 512:SEQ], PS[:, 1, :]).then_inc(sems["x_dve"], 1)
                ve.wait_ge(sems["x_turned"], 3 * k + 3)
                ve.tensor_copy(X[:, k, SEQ:], PS[:, 2, 0:NS]).then_inc(sems["x_dve"], 1)
            w_lo(0, 0)

            def sum_squares(r):
                for k in range(1, KC):
                    ve.wait_ge(sems[f"n{r}_sq"], k + 1)
                    tt_(ss[:, :], ss[:, :], sq[k % 2][:, :], ALU.add).then_inc(sems[f"n{r}_acc"], 1)
                    ve.drain()

            def reciprocals(r):
                ve.wait_ge(sems[f"n{r}_rt"], NB)
                ve.reciprocal(rs[:, :], rs[:, :])
                ve.drain()

            def h_lo(src, k, h0):
                ve.wait_ge(sems["h_hi"], h0 + k + 1)
                tt_(Hlo[:, k, :], src, f(Hhi[:, k, :]), ALU.subtract).then_inc(sems["h_ready"], 1)

            def normed(r, gain, h0):
                reciprocals(r)
                for k in range(KC + 1):
                    ve.drain()
                    if k < KC:
                        if gain is None:
                            tt_(sq[k % 2][:, :], X[:, k, :], rs[:, :], ALU.mult).then_inc(sems[f"n{r}_tmp"], 1)
                        else:
                            stt(out=sq[k % 2][:, :], in0=X[:, k, :], scalar=GT[:, k, gain:gain + 1], in1=rs[:, :],
                                op0=ALU.mult, op1=ALU.mult).then_inc(sems[f"n{r}_tmp"], 1)
                    if k:
                        ve.drain()
                        h_lo(sq[(k - 1) % 2][:, :], k - 1, h0)

            ve.memset(Up[:, 0:2], 0.0)
            ve.drain()
            sum_squares(0)
            normed(0, G_A, 0)

            def conv_layer(j, last):
                for t in range(4):
                    if last and t == 3:
                        w_lo(N_A2 % 2, N_A2)
                    else:
                        w_lo((t + 1) % 2, 4 * j + t + 1)
                    ve.drain()
                    if t == 1:
                        for b, (s, e) in enumerate(BLK):
                            ve.wait_ge(sems["act_evac"], 6 * j + b + 1)
                            ve.wait_ge(sems["block_done"], START["block_done"] + 12 * j + 3 + b + 1)
                            m = min(e, SEQ)
                            ins = tt_(Up[:, 2 + s:2 + m], PS[:, b, 0:m - s], sA[:, s:m], ALU.mult)
                            if e > SEQ:
                                ins = tt_(Us[:, :, 2:], PS[:, b, SEQ - s:e - s].rearrange("p (b t) -> p b t", b=DB),
                                          sA[:, SEQ:e].rearrange("p (b t) -> p b t", b=DB), ALU.mult)
                            ins.then_inc(sems["dve_evac"], 1)
                        g = lambda r, n=1: GT[:, bass.ds(j, 1), r:r + n].rearrange("p a n -> p (a n)")
                        ve.tensor_copy(Us[:, :, 0:2], g(G_ST, 16).rearrange("p (b w) -> p b w", b=DB))
                        ve.drain()
                        cs = sC[:, SEQ:].rearrange("p (b t) -> p b t", b=DB)
                        for w in range(CW):
                            for dst, src in ((sC[:, 0:SEQ], Up[:, w:w + SEQ]), (cs, Us[:, :, w:w + DS])):
                                if w == 0:
                                    ts_(dst, src, g(G_CW), None, ALU.mult)
                                else:
                                    stt(out=dst, in0=src, scalar=g(G_CW + w), in1=dst, op0=ALU.mult, op1=ALU.add)
                            ve.drain()
                        ucj = at_pair(uc, j).rearrange("p a n -> p (a n)")
                        ve.tensor_copy(ucj[:, 0:2], Up[:, SEQ:SEQ + 2])
                        ve.tensor_copy(ucj[:, 2:18].rearrange("p (b w) -> p b w", b=DB), Us[:, :, DS:])
                    if t == 2:
                        ve.wait_ge(sems["act_evac"], 6 * j + 6)
                        tt_(sC[:, :], sC[:, :], sZ[:, :], ALU.mult)
                        ve.drain()
                    if t == 3:
                        for b, (s, e) in enumerate(BLK):
                            ve.wait_ge(sems["block_done"], START["block_done"] + 12 * j + 9 + b + 1)
                            tt_(at_pair(Y, j).rearrange("p a n -> p (a n)")[:, s:e], PS[:, b, 0:e - s], sC[:, s:e],
                                ALU.mult).then_inc(sems["dve_evac"], 1)
            peeled(ve, KC, conv_layer)

            def split_lo(src, h0):
                for k in range(KC):
                    h_lo(src[:, k, :], k, h0)

            def add_x(m, ps_, s, e):
                x = at_pair(X, m).rearrange("p a n -> p (a n)")[:, s:e] if not isinstance(m, int) else X[:, m, s:e]
                return tt_(x, x, ps_, ALU.add)

            def out_tiles(n0, b0):
                def body(i, last):
                    for u in range(2):
                        n = n0 + u + 1
                        w_lo(n % 2, n + 2 * i, nk=KC + PC if last and u == 1 else KC)
                        for b, (s, e) in enumerate(BLK):
                            ve.wait_ge(sems["block_done"], START["block_done"] + b0 + 6 * i + 3 * u + b + 1)
                            add_x(2 * i + u, PS[:, b, 0:e - s], s, e).then_inc(sems["dve_evac"], 1)
                peeled(ve, KC // 2, body)

            def feed(r, n0, b0, ea0, h0):
                for g_ in range(6):
                    ve.wait_ge(sems[f"ple{r}_hi"], g_ + 1)
                    c, h_ = divmod(g_, 3)
                    n = 512 if h_ < 2 else NS
                    tt_(PTl[:, c, h_ * 512:h_ * 512 + n], PS[:, 3 + h_, 0:n], f(PTh[:, c, h_ * 512:h_ * 512 + n]),
                        ALU.subtract).then_inc(sems[f"ple{r}_lo"], 1)
                split_lo(X, h0)

                def body(i, last):
                    for u in range(2):
                        n = n0 + u + 1
                        if last and u == 1:
                            if r == 0:
                                w_lo(n % 2, N_F)
                        else:
                            w_lo(n % 2, n + 2 * i, nk=KC + PC)
                        for b, (s, e) in enumerate(BLK):
                            ve.wait_ge(sems["act_evac"], ea0 + 6 * i + 3 * u + b + 1)
                            ve.wait_ge(sems["block_done"], START["block_done"] + b0 + 12 * i + 6 * u + 3 + b + 1)
                            tt_(sg[:, u, s:e], sg[:, u, s:e], PS[:, 3 + b, 0:e - s], ALU.mult).then_inc(sems["dve_evac"], 1)
                        ve.drain()
                        add_x(2 * i + u, sg[:, u, :], 0, TT).then_inc(sems["x_sum"], 1)
                peeled(ve, KC // 2, body)

            split_lo(Y, 8)
            out_tiles(N_A2, B_A2)
            ve.drain()
            feed(0, N_A3, B_A3, EA_A3, 16)
            ve.drain()
            sum_squares(1)
            normed(1, None, 24)

            ve.wait_ge(sems["f_raw"], 1)
            stt(out=fu[:, :], in0=fl[:, :], scalar=-1.0, in1=fl[:, :], op0=ALU.mult, op1=ALU.min).then_inc(sems["f_abs"], 1)
            ve.memset(one16[:, :], 1.0)
            ve.wait_ge(sems["f_ln"], 1)
            stt(out=lfT[:, :], in0=fl[:, :], scalar=0.0, in1=fm[:, :], op0=ALU.min, op1=ALU.subtract)
            ve.drain().then_inc(sems["f_lf"], 1)
            ve.tensor_tensor_scan(fe[:, 0:SEQ], one16[:, :], lfT[:, 0:SEQ], 0.0, ALU.mult, ALU.add)
            ve.tensor_copy(ch[:, 4, :], one16[:, :])
            ve.drain()
            ve.tensor_copy(ch[:, 0, :], fe[:, 0:SEQ])
            ve.drain()
            tt_(ch[:, 1, :], fe[:, 0:SEQ], f(ch[:, 0, :]), ALU.subtract)
            ve.drain()
            ts_(ch[:, 2:4, :], f(ch[:, 0:2, :]), -1.0, None, ALU.mult)
            ve.drain().then_inc(sems["f_aug"], 1)
            w_lo(N_B1 % 2, N_B1)

            def attention(j, hh):
                for grp in range(2):
                    def rinv(qi):
                        ve.wait_ge(sems["exp"], START["exp"] + 16 * j + 8 * hh + QG * grp + qi + 1)
                        ve.reciprocal(small[:, 8 + qi:9 + qi], small[:, 4 + qi:5 + qi]).then_inc(sems["rinv"], 1)
                    for qi in range(QG):
                        qb = QG * grp + qi
                        n = (qb + 1) * P
                        ve.wait_ge(sems["score"], START["score"] + 16 * j + 8 * hh + qb + 1)
                        ve.reduce_max(small[:, qi:qi + 1], S[:, 0:n], AXX, negate=True).then_inc(sems["rowmax"], 1)
                        rinv(qi)
                    for kb in range(QG * (grp + 1)):
                        u = 12 * hh + 4 * grp + kb
                        q0 = max(0, kb - QG * grp)
                        ve.wait_ge(sems["p_hi"], 24 * j + u + 1)
                        tt_(pTl[:, kb % 2, q0 * P:512], PS[:, 5 + kb % 2, q0 * P:512], f(pTh[:, kb % 2, q0 * P:512]),
                            ALU.subtract).then_inc(sems["p_lo"], 1)
                    hs = slice(64 * hh, 64 * hh + 64)
                    ve.wait_ge(sems["o_up"], 4 * j + 2 * hh + grp + 1)
                    tt_(oT[hs, :], PS[0:64, 7, :], oT[hs, :], ALU.add)
                    ve.drain()
                    tt_(yT[hs, 512 * grp:512 * grp + 512], oT[hs, :], zf[hs, 512 * grp:512 * grp + 512],
                        ALU.mult).then_inc(sems["o_done"], 1)

            def pair(j, last):
                for t in range(4):
                    n = N_B1 + t + 1
                    if t < 3:
                        w_lo(n % 2, n + 4 * j)
                    ve.drain()
                    if t < 2:
                        ve.wait_ge(sems["kv_turned"], 2 * j + t + 1)
                        ve.wait_ge(sems["kv_out"], START["kv_out"] + 64 * j + 32 * t)
                        for c in range(2):
                            ve.tensor_copy(KN[:, 4 * c:4 * c + 4, :].rearrange("p t n -> p (t n)"), PS[:, 3 + c, :])
                        ve.tensor_copy(KN[0:NS, 8, :], PS[0:NS, 5, 0:P])
                        if t == 1:
                            ve.tensor_copy(vnew[:, bass.ds(P * j, P)], PS[0:NS, 5, 0:P])
                        ve.drain().then_inc(sems["kv_nat"], 1)
                    if t == 0:
                        ve.wait_ge(sems["kq_hi"], 2 * j + 1)
                        for hh in range(2):
                            hs = slice(64 * hh, 64 * hh + 64)
                            tt_(KB[0:HD, hh, :], st[hs, 0:SEQ], f(KA[hs, hh, :]), ALU.subtract)
                        ve.tensor_copy(at_pair(knT, j).rearrange("p a n -> p (a n)"), st[:, SEQ:])
                        ve.drain().then_inc(sems["kq_lo"], 1)
                    if t == 1:
                        ve.wait_ge(sems["v_hi"], j + 1)
                        tt_(VS[:, :, :, HD:], KN[:, 0:8, :].rearrange("p t (h n) -> p t h n", h=2),
                            f(VS[:, :, :, 0:HD]), ALU.subtract).then_inc(sems["v_lo"], 1)
                    if t == 2:
                        ve.wait_ge(sems["kq_hi"], 2 * j + 2)
                        for hh in range(2):
                            hs, other = slice(64 * hh, 64 * hh + 64), slice(64 - 64 * hh, 128 - 64 * hh)
                            tt_(QA[other, hh, :], st[hs, 0:SEQ], f(QA[hs, hh, :]), ALU.subtract)
                            ve.tensor_copy(qd[hs, bass.ds(j, 1), :, DS * hh:DS * hh + DS].rearrange("p a b t -> p (a b) t"),
                                           st[hs, SEQ:].rearrange("p (b t) -> p b t", b=DB))
                        ve.drain().then_inc(sems["kq_lo"], 1)
                    if t == 3:
                        ve.wait_ge(sems["z_exp"], j + 1)
                        ts_(yT[:, :], yT[:, :], 1.0, None, ALU.add)
                        ve.drain()
                        ve.reciprocal(yT[:, :], yT[:, :])
                        ve.drain()
                        tt_(zf[:, :], zf[:, :], yT[:, :], ALU.mult)
                        ve.drain()
                        ve.tensor_copy(at_pair(zsS, j).rearrange("p a n -> p (a n)"), zf[:, SEQ:])
                attention(j, 0)
                attention(j, 1)
                if not last:
                    w_lo((N_B1 + 4) % 2, N_B1 + 4 + 4 * j)
            peeled(ve, NPAIR, pair)

            ve.drain()
            ve.wait_ge(sems["y_out"], START["y_out"] + 16 * NPAIR)
            ve.wait_ge(sems["kv_out"], START["kv_out"] + 64 * NPAIR)
            ve.wait_ge(sems["s_cn"], 1)
            ve.tensor_copy(cn[:, :], PS[0:NS, 6, 0:H]).then_inc(sems["s_cnsb"], 1)
            ve.drain()
            shape = [NS, DB, H, DS]
            bq = lambda m: m.rearrange("p (b q) -> p b q", b=DB).unsqueeze(2).to_broadcast(shape)
            bh = cn[:, :].unsqueeze(1).unsqueeze(3).to_broadcast(shape)
            tt_(Rq.rearrange("p (b h q) -> p b h q", b=DB, h=H), bq(ident[0:NS, 0:NS]), bh, ALU.mult).then_inc(sems["s_rq"], 1)
            ve.wait_ge(sems["s_cq"], 1)
            for c in range(2):
                ve.tensor_copy(CQ[:, :, :, :].rearrange("p b h q -> p (b h q)")[:, 512 * c:512 * c + 512], PS[:, c, :])
            ve.drain().then_inc(sems["s_cqsb"], 1)
            tt_(NBs[:, :, :, :], CQ[0:NS, :, :, :], bh, ALU.subtract)
            ve.drain()
            tt_(NBs[:, :, :, :], NBs[:, :, :, :], bq(maskS[:, :]), ALU.add)
            ve.wait_ge(sems["s_rest"], 1)
            for c in range(2):
                ve.tensor_copy(rest[:, 4 * c:4 * c + 4, :, :].rearrange("p a b h -> p (a b h)"), S[:, 512 * c:512 * c + 512])
            ve.drain().then_inc(sems["s_restsb"], 1)

            with ve.Fori(0, DB) as b:
                ve.drain()
                for pg in range(PAGES):
                    ve.wait_ge(sems["s_kturn"], START["s_kturn"] + 2 * PAGES * b + 2 * pg + 2)
                    ve.wait_ge(sems["s_score"], START["s_score"] + PAGES * b + pg - 1)
                    ve.tensor_copy(KT[:, pg % 2, 512:D], PS[:, 1, :]).then_inc(sems["s_kt1"], 1)
                    ve.wait_ge(sems["s_score"], START["s_score"] + PAGES * b + pg + 1)
                    ve.wait_ge(sems["s_bias"], PAGES * b + pg + 1)
                    tt_(ST[:, pg % 2, :], PS[:, 2, 0:P], bias[:, pg % 2, :], ALU.add).then_inc(sems["s_st"], 1)
                ve.wait_ge(sems["s_new"], b + 1)
                tt_(PsT[0:NS, 8, :], PS[0:NS, 6, 0:P], at_pair(NBs, b).rearrange("p b h q -> p (b h q)"), ALU.add).then_inc(sems["s_newst"], 1)
                ve.wait_ge(sems["s_all"], b + 1)
                ve.reduce_max(small[:, 0:1], S[:, 0:PAGES * PAGE + NS], AXX, negate=True).then_inc(sems["s_max"], 1)
                ve.wait_ge(sems["s_exp"], START["s_exp"] + b + 1)
                ve.reciprocal(small[:, 8:9], small[:, 4:5])
                ve.drain()
                ts_(Ps[:, :], Ps[:, :], small[:, 8:9], None, ALU.mult).then_inc(sems["s_norm"], 1)
                ve.wait_ge(sems["s_pv"], START["s_pv"] + b + 1)
                for hh in range(2):
                    hs = slice(64 * hh, 64 * hh + 64)
                    z = zsS[hs, :, bass.ds(DS * b, DS)]
                    ins = tt_(z, PS[hs, 6, 0:P].rearrange("p (i n) -> p i n", n=2 * DS)[:, :, DS * hh:DS * hh + DS], z, ALU.mult)
                ins.then_inc(sems["s_out"], 1)

            ve.drain()
            ve.tensor_copy(Y[:, :, SEQ:], zsS[:, :, :])
            ve.drain().then_inc(sems["y_merged"], 1)
            w_lo(N_B2 % 2, N_B2)
            split_lo(Y, 32)
            ve.wait_ge(sems["x_back"], 16 * KC)
            out_tiles(N_B2, B_B2)
            ve.drain()
            feed(1, N_B3, B_B3, EA_B3, 40)
            ve.drain()
            sum_squares(2)
            reciprocals(2)
            ve.drain()
            for k in range(KC):
                stt(out=X[:, k, :], in0=X[:, k, :], scalar=GT[:, k, G_F:G_F + 1], in1=rs[:, :],
                    op0=ALU.mult, op1=ALU.mult).then_inc(sems["y_norm"], 1)
            for tt in range(9):
                n = P if tt < 8 else NS
                ve.wait_ge(sems["y_turned"], 2 * tt + 2)
                if tt >= 2:
                    ve.wait_ge(sems[f"y_dma{tt % 2}"], 16 * (tt // 2))
                ve.tensor_copy(Y[0:n, tt % 2, 512:D], PS[0:n, 1, :]).then_inc(sems["y_dve"], 1)


INS = ["x_prompt", "x_sample", "p_prompt", "p_sample", "state_conv", "cache_k", "cache_v", "cache_logf",
       "page_table", "norm_a", "w_in_a", "conv_w_a", "w_out_a", "norm_kv", "w_kv", "b_f", "norm_b",
       "w_in_b", "w_out_b", "w_ple_proj", "w_ple_gate", "norm_f"]
OUTS = [("y_prompt", (1, SEQ, D)), ("y_sample", (DB, DS, D)), ("conv_prompt", (1, 1, CW - 1, D)),
        ("k_prompt", (1, SEQ, H, HD)), ("v_prompt", (1, SEQ, H, HD)), ("logf_prompt", (1, SEQ, H)),
        ("conv_sample", (1, DB, CW - 1, D)), ("k_sample", (DB, DS, H, HD)), ("v_sample", (DB, DS, H, HD)),
        ("logf_sample", (DB, DS, H))]


def kernel(**inputs):
    import concourse.bacc as bacc
    from concourse.bass_utils import run_bass_kernel_spmd

    nc = bacc.Bacc("TRN2", target_bir_lowering=False, num_devices=1)
    arrays, a, o = {}, {}, {}
    for name in INS:
        x = np.ascontiguousarray(inputs[name])
        arrays[f"in_{name}"] = x
        a[name] = nc.dram_tensor(f"in_{name}", x.shape, mybir.dt.from_np(x.dtype), kind="ExternalInput").ap()
    for name, shape in OUTS:
        o[name] = nc.dram_tensor(f"out_{name}", shape, F32, kind="ExternalOutput").ap()
    d = {"x": nc.dram_tensor("parked_x", (KC, P, TT), F32, kind="Internal").ap(),
         "y": nc.dram_tensor("parked_y", (KC, P, SEQ), F32, kind="Internal").ap(),
         "augk": nc.dram_tensor("aug_k", (H, AUG, SEQ), F32, kind="Internal").ap(),
         "augq": nc.dram_tensor("aug_q", (H, AUG, SEQ), F32, kind="Internal").ap()}
    program(nc, a, o, d)
    r = run_bass_kernel_spmd(nc, [arrays], core_ids=[0])
    return tuple(r.results[0][f"out_{name}"] for name, _ in OUTS)
```

```python
from contextlib import ExitStack

import numpy as np
import concourse.bass as bass
from concourse import mybir

F32 = mybir.dt.float32
F32R = mybir.dt.float32r
BF16 = mybir.dt.bfloat16
I32 = mybir.dt.int32
ALU = mybir.AluOpType
ACT = mybir.ActivationFunctionType
AXX = mybir.AxisListType.X

P = 128
D = 1024
KC = D // P
SEQ, DB, DS = 1024, 8, 8
NS = DB * DS
TT = SEQ + NS
PLE, PC = 256, 2
H, HD = 16, 64
NPAIR = H // 2
PAGES, PAGE = 8, 128
CW = 3
EPS = 1e-6
NEG = -1e30
SCALE = HD ** -0.5
BLK = [(0, 364), (364, 728), (728, TT)]
NB = len(BLK)
QG = 4
KEYS = PAGES * PAGE
AUG = 4

G_A, G_KV, G_B, G_F, G_CW, G_ST, G_N = 0, 1, 2, 3, 4, 7, 24

N_A1, N_A2, N_A3, N_F, N_B1, N_B2, N_B3, N_END = 0, 32, 40, 48, 49, 81, 89, 97
B_A1, B_A2, B_A3 = 0, 96, 120
B_F = B_A3 + 48
B_B1 = B_F + 3
B_B2 = B_B1 + 96
B_B3 = B_B2 + 24
B_END = B_B3 + 48
EA_A1, EA_A2, EA_A3, EA_F, EA_B1, EA_B2, EA_B3, EA_END = 0, 48, 48, 72, 75, 171, 171, 195
ED_A1, ED_A2, ED_A3, ED_F, ED_B1, ED_B2, ED_B3, ED_END = 0, 48, 72, 96, 96, 96, 120, 144
STEPS = [("S", 0), ("D", 2), ("N", 0), ("N", 1), ("D", 1), ("S", 1), ("D", 2), ("N", 2), ("D", 1), ("S", 2), ("D", 3),
         ("S", 3), ("D", 4), ("S", 4), ("D", 5), ("T", 0, 0), ("T", 0, 1), ("S", 5), ("D", 4), ("V", 0, 0), ("T", 0, 2),
         ("S", 6), ("D", 4), ("V", 0, 1), ("T", 0, 3), ("S", 7), ("D", 3), ("V", 0, 2), ("D", 1), ("V", 0, 3), ("D", 3),
         ("T", 1, 0), ("T", 1, 1)]
for _kb in range(8):
    STEPS += [("D", 2 if _kb < 7 else 1), ("V", 1, _kb)] + ([("T", 1, _kb + 2)] if _kb < 6 else [])
TURN_PARTS = [(0, 1, 2, 3), (4, 5, 6), (7, 8)]
PIECES = 48
assert sum(x[1] for x in STEPS if x[0] == "D") == PIECES
P_OFF = [sum((x + 1) * P for x in range(qb)) for qb in range(2 * QG + 1)]
P_ROUNDS = [(2, 0, 0), (3, 0, 4), (4, 0, PAGES), (5, 1, 0), (7, 1, 4)]
LEAD = {
    "tensor": {"block_done": 6, "score": 1, "turned": 1, "pv": 1, "s_score": 2, "s_pv": 1},
    "vector": {"w_split": 2, "x_sum": 2, "dve_evac": 6, "o_done": 1, "p_lo": 1, "s_kt1": 1, "s_pt1": 1, "s_osb": 1,
               "s_out": 1},
    "scalar": {"exp": 1, "s_kt0": 1, "s_exp": 1, "s_pt0": 1},
    "sync": {"kv_out": 16, "y_out": 16},
}
START = {name: n for per in LEAD.values() for name, n in per.items()}


def f(x):
    return x.bitcast(F32)


def program(nc, a, o, d):
    es = ExitStack()
    with es:
        def sb(ctx, name, shape, dt=F32):
            return ctx.enter_context(nc.sbuf_tensor(name, shape, dt))

        def sem(name):
            return es.enter_context(nc.semaphore(name))

        raw = sb(es, "w_raw", [P, 2, KC + PC, P])
        whi = sb(es, "w_hi", [P, 2, KC + PC, P], F32R)
        wlo = sb(es, "w_lo", [P, 2, KC + PC, P], F32R)
        ident = sb(es, "ident", [P, P])
        ones = sb(es, "ones", [P, P])
        tri = sb(es, "tri", [P, P])
        identb = sb(es, "identb", [P, P], BF16)
        maskb = sb(es, "maskb", [P, P], BF16)
        same = sb(es, "same", [NS, NS])
        maskQ = sb(es, "maskQ", [NS, NS], BF16)
        GT = sb(es, "GT", [P, KC, G_N])
        bf_col = sb(es, "bf_col", [H, 1])
        pt = sb(es, "pt", [1, DB * PAGES], I32)
        small = sb(es, "small", [P, 32])
        sl = ExitStack()
        LFP = sb(sl, "LFP", [P, PAGES, DB, H])
        sl.close()
        qd = sb(es, "qd", [P, NPAIR, DB, 2 * DS])
        knT = sb(es, "knT", [P, NPAIR, NS])
        zsS = sb(es, "zsS", [P, NPAIR, NS])
        vnew = sb(es, "vnew", [NS, D])
        lfn = sb(es, "lfn", [P, 9, H])

        cn = sb(es, "cn", [NS, H])

        sh = ExitStack()
        Hhi = sb(sh, "Hhi", [P, KC, TT], F32R)
        Hlo = sb(sh, "Hlo", [P, KC, TT], F32R)

        sa = ExitStack()
        X = sb(sa, "X", [P, KC, TT])
        Y = sb(sa, "Y", [P, KC, TT])
        sA = sb(sa, "scrA", [P, TT])
        sU = sb(sa, "scrU", [P, 2 + SEQ + DB * (DS + 2)])
        sC = sb(sa, "scrC", [P, TT])
        sZ = sb(sa, "scrZ", [P, TT])
        uc = sb(sa, "uc", [P, KC, 18])
        sa.close()
        Up = sU[:, 0:2 + SEQ]
        Us = sU[:, 2 + SEQ:].rearrange("p (b t) -> p b t", b=DB)
        ss, sq = sC, [sA, sZ]
        rs = sC
        sp_ = ExitStack()
        Xp = sb(sp_, "X_again", [P, KC, TT])
        PTh = sb(sp_, "PTh", [P, PC, TT], F32R)
        PTl = sb(sp_, "PTl", [P, PC, TT], F32R)
        sg = sb(sp_, "sg", [P, 2, TT])
        sp_.close()
        pn = sA
        pn2 = sZ
        pnS = sU

        s1 = ExitStack()
        KA = sb(s1, "KA", [P, 2, SEQ], F32R)
        KB = sb(s1, "KB", [HD + AUG, 2, SEQ], F32R)
        QA = sb(s1, "QA", [P, 2, SEQ], F32R)
        QB = sb(s1, "QB", [HD + AUG, 2, SEQ], F32R)
        VS = sb(s1, "VS", [P, PAGES, 2, P], F32R)
        Pb = sb(s1, "Pb", [P, P_OFF[-1]])
        pTh = sb(s1, "pTh", [P, 2, 512], F32R)
        pTl = sb(s1, "pTl", [P, 2, 512], F32R)
        stK = sb(s1, "stageK", [P, TT])
        stQ = sb(s1, "stageQ", [P, TT])
        zf = sb(s1, "zf", [P, TT])
        yT = sb(s1, "yT", [P, TT])
        KN = sb(s1, "KN", [P, 9, P])
        s1.close()
        s0 = ExitStack()
        fl = sb(s0, "fl", [H, TT])
        fe = sb(s0, "fe", [H, TT])
        fu = sb(s0, "fu", [H, TT])
        fm = sb(s0, "fm", [H, TT])
        lfT = sb(s0, "lfT", [H, TT])
        one16 = sb(s0, "one16", [H, SEQ])
        ch = sb(s0, "ch", [H, 5, SEQ], F32R)
        RTs = sb(s0, "RT_first", [P, 2, KEYS + NS], F32R)
        lf8 = sb(s0, "lf8", [NS, DB, H])
        s0.close()
        sh.close()

        s2 = ExitStack()
        Kr = sb(s2, "Kpages", [P, PAGES, D])
        Vb = sb(s2, "Vpages", [P, PAGES, D])
        KT = sb(s2, "KT", [P, 2, NPAIR, 2 * PAGE])
        Ps = sb(s2, "Ps", [P, 2, KEYS + NS])
        PsT = sb(s2, "PsT", [P, 2, 9, P])
        RT = sb(s2, "RT", [P, 2, KEYS + NS], F32R)
        pick = sb(s2, "pick", [P, NPAIR, 32], F32R)
        qc = sb(s2, "qc", [P, NPAIR, 32])
        cq = sb(s2, "cq", [NS, NPAIR, 32])
        cqh = sb(s2, "cqh", [NS, NPAIR, 32], F32R)
        cql = sb(s2, "cql", [NS, NPAIR, 32], F32R)
        mq = sb(s2, "mq", [NS, 4, 32], BF16)
        onesr = sb(s2, "onesr", [NS, 512], F32R)
        Osb = sb(s2, "Osb", [P, 2, P])
        s2.close()

        PS = es.enter_context(nc.psum_tensor("PS", [P, 8, 512], F32))
        flat = PS[:, :, :].rearrange("p b n -> p (b n)")
        S = flat[:, 3 * 512:6 * 512]

        def score_bank(qb):
            return PS[:, 3 + qb % 2, :] if qb < 4 else S

        names = (
            "const_ready sp_step in_rows in_x0 in_x1 in_x2 w_in0 w_in1 w_gained w_hi w_split block_done act_evac dve_evac "
            "h_hi h_ready g_turned g_ready x_turned x_act x_dve x_sum x_parked x_back y_back y_merged out_dma "
            "uc_turned uc_act uc_out f_raw f_abs f_exp f_ln f_lf f_turned f_nat f_aug f_augdma "
            "staged kv_turned kv_nat kv_out kq_hi kq_lo v_hi v_lo z_exp z_done y_used "
            "score rowmax exp rinv p_begun p_norm turned p_hi p_lo pv o_up o_done y_out "
            "s_table s_logf s_rest s_lf8 s_cn s_cnsb s_restsb s_restout s_restin qd_zero s_prep s_kturn s_kt0 s_kt1 s_score "
            "s_all s_max s_exp s_back s_pt0 s_pt1 s_pv s_osb s_yturn s_out aug_in0 aug_in1 "
                        "y_norm y_turned y_act y_dve y_dma0 y_dma1").split()
        names += [f"{k}{i}" for i in range(PAGES) for k in ("k_in", "v_in")]
        names += [f"n{r}_{k}" for r in range(3) for k in ("sq", "acc", "ps", "rt", "tmp")]
        names += [f"ple{r}_{k}" for r in range(2) for k in ("in", "turned", "hi", "lo")]
        sems = {k: sem(k) for k in names}

        def loaded(n0, per=2, i=0):
            return 32 * (n0 // 2 + 1) + 16 * per * i

        block = es.enter_context(nc.Block())

        wv = lambda w: w.rearrange("(k p) n -> p k n", p=P)
        row = lambda w: w.rearrange("(a n) -> a n", a=1)
        w_in_a, w_out_a = wv(a["w_in_a"][0]), wv(a["w_out_a"][0])
        w_kv, w_in_b, w_out_b = wv(a["w_kv"]), wv(a["w_in_b"][0]), wv(a["w_out_b"][0])
        w_gate = [wv(a["w_ple_gate"][i]) for i in range(2)]
        w_proj = [wv(a["w_ple_proj"][i]) for i in range(2)]
        x_p = a["x_prompt"][0].rearrange("(t p) c -> p t c", p=P)
        x_s = a["x_sample"].rearrange("b t c -> (b t) c")
        p_p = [a["p_prompt"][i, 0].rearrange("(t p) c -> p t c", p=P) for i in range(2)]
        p_s = [a["p_sample"][i].rearrange("b t c -> (b t) c") for i in range(2)]
        ck = a["cache_k"].rearrange("n s h d -> (n s) (h d)")
        cv = a["cache_v"].rearrange("n s h d -> (n s) (h d)")
        cl = a["cache_logf"].rearrange("n s h -> (n s) h")
        last_page = a["cache_k"].shape[0] - 1
        o_yp = o["y_prompt"][0].rearrange("(t p) c -> p t c", p=P)
        o_ys = o["y_sample"].rearrange("b t c -> (b t) c")
        o_kv = [(o[f"{x}_prompt"][0].rearrange("(t p) h d -> p t (h d)", p=P),
                 o[f"{x}_sample"].rearrange("b t h d -> (b t) (h d)")) for x in "kv"]
        A1_COLS = [D, 2 * D, 3 * D, 0]

        def peeled(eng, n, body):
            with eng.Fori(0, n - 1) as i:
                body(i, False)
            body(n - 1, True)

        def at_pair(t, j):
            return t[:, bass.ds(j, 1)]

        @block.sync
        def _(sp):
            for k, n in LEAD["sync"].items():
                sp.sem_inc(sems[k], n)
            sp.dma_start(Y[:, 0:4, 0:D], x_p[:, 0:4, :]).then_inc(sems["in_x0"], 16)
            for src, r, n in ((a["norm_a"][0:1, :], G_A, 1), (row(a["norm_kv"]), G_KV, 1),
                              (a["norm_b"][0:1, :], G_B, 1), (row(a["norm_f"]), G_F, 1),
                              (a["conv_w_a"][0], G_CW, CW), (a["state_conv"][0].rearrange("b w c -> (b w) c"), G_ST, 16),
                              (row(a["norm_f"]), G_N - 1, 1)):
                sp.dma_start(sZ[r:r + n, 0:D], src).then_inc(sems["in_rows"], 16)
            sp.dma_start(Y[:, 4:8, 0:D], x_p[:, 4:8, :]).then_inc(sems["in_x1"], 16)
            sp.dma_start(sA[0:NS, 0:D], x_s).then_inc(sems["in_x2"], 16)
            with nc.allow_non_contiguous_dma(reason="16 values, one per partition"):
                sp.dma_start(bf_col[:, :], a["b_f"].rearrange("(n a) -> n a", a=1)).then_inc(sems["in_rows"], 16)

            sp.dma_start(pt[:, :], a["page_table"].rearrange("b (a n) -> a b n", a=1)).then_inc(sems["s_table"], 16)
            sp.wait_ge(sems["s_table"], 16)

            def page(b, pg):
                v = sp.value_load(pt[0:1, bass.ds(PAGES * b + pg, 1)], min_val=0, max_val=last_page)
                return bass.ds(v * PAGE, PAGE)

            def load(n, par, src, proj=None, cols=P):
                sp.wait_ge(sems["w_split"], START["w_split"] + n - 1)
                sp.sem_inc(sems["sp_step"], 1)
                if proj is None:
                    for c in (0, 4):
                        sp.dma_start(raw[:, par, c:c + 4, 0:cols], src[:, c:c + 4, :]).then_inc(sems[f"w_in{par}"], 16)
                else:
                    sp.dma_start(raw[:, par, 0:KC, :], src).then_inc(sems[f"w_in{par}"], 16)
                    sp.dma_start(raw[:, par, KC:, :], proj).then_inc(sems[f"w_in{par}"], 16)

            def load_out(n0, w):
                with sp.Fori(0, KC // 2) as i:
                    for u in range(2):
                        load(n0 + 2 * i + u, (n0 + u) % 2, w[:, :, bass.ds(2 * P * i + P * u, P)])

            def load_feed(n0, r):
                for dst, src in ((sA[:, 0:D], p_p[r][:, 0:4, :]), (sZ[:, 0:D], p_p[r][:, 4:8, :])):
                    sp.dma_start(dst.rearrange("p (t c) -> p t c", c=PLE), src).then_inc(sems[f"ple{r}_in"], 16)
                sp.dma_start(sU[0:NS, 0:PLE], p_s[r]).then_inc(sems[f"ple{r}_in"], 16)
                with sp.Fori(0, KC // 2) as i:
                    for u in range(2):
                        c = bass.ds(2 * P * i + P * u, P)
                        load(n0 + 2 * i + u, (n0 + u) % 2, w_gate[r][:, :, c], w_proj[r][:, :, c])

            with sp.Fori(0, KC) as j:
                for t in range(4):
                    load(4 * j + t, t % 2, w_in_a[:, :, bass.ds(A1_COLS[t] + P * j, P)])
                    with nc.allow_non_contiguous_dma(reason="16 log forget values per row"):
                        for pg in (2 * t, 2 * t + 1):
                            sp.dma_start(at_pair(LFP[:, pg], j).rearrange("p b h -> p (b h)"), cl[page(j, pg), :]).then_inc(sems["s_logf"], 16)
            load_out(N_A2, w_out_a)
            sp.wait_ge(sems["dve_evac"], START["dve_evac"] + ED_A2)
            load_feed(N_A3, 0)
            sp.wait_ge(sems["uc_act"], 2)
            sp.dma_start(o["conv_prompt"][0, 0], sC[0:2, 0:D]).then_inc(sems["uc_out"], 16)
            sp.dma_start(o["conv_sample"][0].rearrange("b w c -> (b w) c"), sC[2:18, 0:D]).then_inc(sems["uc_out"], 16)
            with nc.allow_non_contiguous_dma(reason="the last 16 columns of w_kv"):
                load(N_F, N_F % 2, w_kv[:, :, 2 * D:2 * D + H], cols=H)
            sp.wait_ge(sems["x_sum"], START["x_sum"] + 8)
            for k in range(KC):
                sp.dma_start(d["x"][k], X[:, k, :]).then_inc(sems["x_parked"], 16)
            load(N_B1, N_B1 % 2, w_kv[:, :, 0:P])
            sp.wait_ge(sems["f_nat"], 1)
            sp.dma_start(o["logf_prompt"][0].rearrange("(t p) h -> p t h", p=P), lfn[:, 0:8, :]).then_inc(sems["out_dma"], 16)
            sp.dma_start(o["logf_sample"].rearrange("b t h -> (b t) h"), lfn[0:NS, 8, :]).then_inc(sems["out_dma"], 16)
            sp.wait_ge(sems["f_aug"], 1)
            for r, (sk, sq_) in enumerate(((2, 4), (3, 4), (4, 0), (4, 1))):
                sp.dma_start(d["augk"][:, r, :], f(ch[:, sk, :])).then_inc(sems["f_augdma"], 16)
                sp.dma_start(d["augq"][:, r, :], f(ch[:, sq_, :])).then_inc(sems["f_augdma"], 16)
            sp.wait_ge(sems["f_augdma"], 128)

            def load_b1(j, t, back=0):
                w, c0 = ((w_kv, 0), (w_in_b, 0), (w_kv, D), (w_in_b, D))[t]
                n = N_B1 + 4 * (j + back) + t
                load(n, (N_B1 + t) % 2, w[:, :, bass.ds(c0 + P * (j + back), P)])

            def load_aug(j, hh):
                for dst, src in ((KB, d["augk"]), (QB, d["augq"])):
                    sp.dma_start(f(dst[HD:, hh, :]), src[bass.ds(2 * j + hh, 1)].rearrange("a r n -> (a r) n")).then_inc(sems[f"aug_in{hh}"], 16)

            def store_kv(j, t):
                sp.wait_ge(sems["kv_nat"], 6 * j + 3 * t + 3)
                sp.sem_inc(sems["sp_step"], 1)
                o_p, o_s = o_kv[t]
                sp.dma_start(o_p[:, :, bass.ds(P * j, P)], KN[:, 0:8, :]).then_inc(sems["kv_out"], 16)
                sp.dma_start(o_s[:, bass.ds(P * j, P)], KN[0:NS, 8, :]).then_inc(sems["kv_out"], 16)

            def half0(j, more):
                if more:
                    load_b1(j, 0, 1)
                store_kv(j, 1)
                if more:
                    load_b1(j, 1, 1)
                    load_b1(j, 2, 1)
                    sp.wait_ge(sems["score"], START["score"] + 16 * j + 8)
                    sp.sem_inc(sems["sp_step"], 1)
                    load_aug(j + 1, 0)
                    load_b1(j, 3, 1)

            def half1(j, more):
                if more:
                    store_kv(j + 1, 0)
                    sp.wait_ge(sems["score"], START["score"] + 16 * j + 16)
                    sp.sem_inc(sems["sp_step"], 1)
                    load_aug(j + 1, 1)
                sp.wait_ge(sems["o_done"], START["o_done"] + 4 * j + 4)
                sp.sem_inc(sems["sp_step"], 1)
                sp.dma_start(d["y"][bass.ds(j, 1)].rearrange("a p n -> (a p) n"), yT[:, 0:SEQ]).then_inc(sems["y_out"], 16)

            sp.wait_ge(sems["s_restsb"], 1)
            sp.dma_start(d["rest"], f(RTs[:, :, :])).then_inc(sems["s_restout"], 16)
            sp.wait_ge(sems["s_restout"], 16)
            load_aug(0, 0)
            load_aug(0, 1)
            load_b1(0, 1)
            load_b1(0, 2)
            load_b1(0, 3)
            store_kv(0, 0)
            with sp.Fori(0, NPAIR - 1) as j:
                half0(j, True)
                half1(j, True)
            half0(NPAIR - 1, False)
            half1(NPAIR - 1, False)

            sp.wait_ge(sems["y_out"], START["y_out"] + 16 * NPAIR)
            sp.wait_ge(sems["kv_out"], START["kv_out"] + 64 * NPAIR)
            sp.dma_start(f(RT[:, :, :]), d["rest"]).then_inc(sems["s_restin"], 16)
            for pg in range(PAGES):
                sp.dma_start(Kr[:, pg, :], ck[page(0, pg), :]).then_inc(sems[f"k_in{pg}"], 16)

            def value_pages(b):
                for pg in range(PAGES):
                    rows = page(b, pg)
                    if pg == 0:
                        sp.wait_ge(sems["s_pv"], START["s_pv"] + b)
                        sp.sem_inc(sems["sp_step"], 1)
                    sp.dma_start(Vb[:, pg, :], cv[rows, :]).then_inc(sems[f"v_in{pg}"], 16)

            with sp.Fori(0, DB - 1) as b:
                value_pages(b)
                for pg in range(PAGES):
                    rows = page(b + 1, pg)
                    sp.wait_ge(sems["s_kturn"], 16 * b + 2 * pg + 2)
                    sp.sem_inc(sems["sp_step"], 1)
                    sp.dma_start(Kr[:, pg, :], ck[rows, :]).then_inc(sems[f"k_in{pg}"], 16)
            value_pages(DB - 1)

            sp.wait_ge(sems["s_out"], START["s_out"] + DB)
            for k in range(KC):
                sp.dma_start(Y[:, k, 0:SEQ], d["y"][k]).then_inc(sems["y_back"], 16)
            for k in range(KC):
                sp.dma_start(X[:, k, :], d["x"][k]).then_inc(sems["x_back"], 16)
            load_out(N_B2, w_out_b)
            load_feed(N_B3, 1)
            for tt in range(9):
                n = P if tt < 8 else NS
                sp.wait_ge(sems["y_act"], tt + 1)
                sp.wait_ge(sems["y_dve"], tt + 1)
                sp.dma_start(o_yp[:, tt, :] if tt < 8 else o_ys, Y[0:n, tt % 2, 0:D]).then_inc(sems[f"y_dma{tt % 2}"], 16)
            sp.wait_ge(sems["y_dma0"], 80)
            sp.wait_ge(sems["y_dma1"], 64)
            sp.wait_ge(sems["out_dma"], 32)
            sp.wait_ge(sems["uc_out"], 32)

        @block.gpsimd
        def _(g):
            g.memset(ones[:, :], 1.0)
            g.memset(ident[:, :], 0.0)
            g.memset(tri[:, :], 0.0)
            g.memset(maskb[:, :], 0.0)
            g.memset(same[:, :], 1.0)
            g.memset(maskQ[:, :], 0.0)
            g.memset(small[:, 31:32], EPS)
            g.drain()
            g.affine_select(out=ident[:, :], in_=ident[:, :], compare_op=ALU.not_equal, fill=1.0, base=0,
                            pattern=[[-1, P]], channel_multiplier=1)
            g.affine_select(out=tri[:, :], in_=tri[:, :], compare_op=ALU.is_ge, fill=1.0, base=0,
                            pattern=[[1, P]], channel_multiplier=-1)
            g.affine_select(out=maskb[:, :], in_=maskb[:, :], compare_op=ALU.is_ge, fill=NEG, base=0,
                            pattern=[[-1, P]], channel_multiplier=1)
            g.affine_select(out=same[:, :], in_=same[:, :], compare_op=ALU.is_ge, fill=0.0, base=0,
                            pattern=[[1, NS]], channel_multiplier=-1)
            g.affine_select(out=maskQ[:, :], in_=maskQ[:, :], compare_op=ALU.is_ge, fill=NEG, base=0,
                            pattern=[[-1, NS]], channel_multiplier=1)
            g.drain()
            v = same[:, :].rearrange("p (b t) -> p b t", b=DB)
            g.affine_select(out=v, in_=v, compare_op=ALU.is_ge, fill=0.0, base=0,
                            pattern=[[-DS, DB], [0, DS]], channel_multiplier=1)
            v = maskQ[:, :].rearrange("p (b t) -> p b t", b=DB)
            g.affine_select(out=v, in_=v, compare_op=ALU.is_ge, fill=NEG, base=DS - 1,
                            pattern=[[DS, DB], [0, DS]], channel_multiplier=-1)
            g.tensor_copy(identb[:, :], ident[:, :])
            g.drain().then_inc(sems["const_ready"], 1)

            def gain(par, r, count, done=None):
                g.wait_ge(sems[f"w_in{par}"], count)
                w = raw[:, par, 0:KC, :]
                g.tensor_tensor(w, w, GT[:, :, r:r + 1].to_broadcast([P, KC, P]), ALU.mult).then_inc(sems["w_gained"], 1)
            g.wait_ge(sems["g_ready"], 1)
            gain(N_F % 2, G_KV, loaded(N_F))
            def gain_b1(j, t, back=0):
                gain((N_B1 + t) % 2, (G_KV, G_B, G_KV, G_B)[t], loaded(N_B1 + 4 * back + t, 4, j))

            def normalise(c, j):
                qb = c % 8
                g.wait_ge(sems["rinv"], 16 * j + c + 1)
                g.sem_inc(sems["p_begun"], 1)
                pb = Pb[:, P_OFF[qb]:P_OFF[qb + 1]]
                g.tensor_scalar(pb, pb, small[:, 16 + qb:17 + qb], 1.0, ALU.mult, ALU.mult).then_inc(sems["p_norm"], 1)

            def iteration(j, more):
                for hh in range(2):
                    if more and hh == 0:
                        gain_b1(j, 0, 1)
                    for qb in range(4):
                        normalise(8 * hh + qb, j)
                    if more:
                        gain_b1(j, (1, 3)[hh], 1)
                    for qb in range(4, 8):
                        normalise(8 * hh + qb, j)
                    if more and hh == 0:
                        gain_b1(j, 2, 1)

            gain_b1(0, 0)
            g.wait_ge(sems["s_rest"], 1)
            g.memset(qd[:, :, :, :].rearrange("p a b c -> p (a b c)"), 0.0).then_inc(sems["qd_zero"], 1)
            for t in range(1, 4):
                gain_b1(0, t)
            with g.Fori(0, NPAIR - 1) as j:
                iteration(j, True)
            iteration(NPAIR - 1, False)
        @block.tensor
        def _(pe):
            for k, n in LEAD["tensor"].items():
                pe.sem_inc(sems[k], n)
            mm, tp = pe.matmul, pe.transpose

            def tile(n, par, bank, free, hr=None, k0=0, nk=KC, hi=Hhi, lo=Hlo):
                pe.wait_ge(sems["w_split"], START["w_split"] + n + 1)
                for b, (s, e) in enumerate(BLK):
                    free(b)
                    for k in range(nk):
                        if hr is not None and b == 0:
                            pe.wait_ge(sems["h_ready"], hr + k + 1)
                        out = PS[:, bank + b, 0:e - s]
                        wh, wl = whi[:, par, k0 + k, :], wlo[:, par, k0 + k, :]
                        mm(out, wh, hi[:, k, s:e], start=(k == 0), stop=False)
                        mm(out, wh, lo[:, k, s:e], start=False, stop=False)
                        last = mm(out, wl, hi[:, k, s:e], start=False, stop=(k == nk - 1))
                    last.then_inc(sems["block_done"], 1)

            pe.wait_ge(sems["const_ready"], 1)
            pe.wait_ge(sems["in_rows"], 128)
            for k in range(KC):
                last = tp(PS[:, 7, k * G_N:(k + 1) * G_N], sZ[0:G_N, k * P:(k + 1) * P], ident[0:G_N, 0:G_N])
            last.then_inc(sems["g_turned"], 1)
            for k in range(KC):
                for h_ in range(2):
                    if k == 0:
                        pe.wait_ge(sems[f"in_x{h_}"], 16)
                    else:
                        pe.wait_ge(sems[("x_act", "x_dve")[h_]], (k, 2 * k - 1)[h_])
                    for i in range(4):
                        last = tp(PS[:, h_, i * P:(i + 1) * P], Y[:, 4 * h_ + i, k * P:(k + 1) * P], ident[:, :])
                    last.then_inc(sems["x_turned"], 1)
                pe.wait_ge(sems["in_x2"], 16) if k == 0 else pe.wait_ge(sems["x_dve"], 2 * k)
                tp(PS[:, 2, 0:NS], sA[0:NS, k * P:(k + 1) * P], ident[0:NS, 0:NS]).then_inc(sems["x_turned"], 1)

            def norm_sum(r):
                pe.wait_ge(sems[f"n{r}_acc"], KC - 1)
                for b, (s, e) in enumerate(BLK):
                    mm(PS[:, 3 + b, 0:e - s], ones[:, :], ss[:, s:e], start=True, stop=True).then_inc(sems[f"n{r}_ps"], 1)
            norm_sum(0)

            with pe.Fori(0, KC) as j:
                for t in range(4):
                    free = [lambda b: pe.wait_ge(sems["dve_evac"], START["dve_evac"] + 6 * j - 3 + b + 1), lambda b: pe.wait_ge(sems["act_evac"], 6 * j + b + 1),
                            lambda b: pe.wait_ge(sems["dve_evac"], START["dve_evac"] + 6 * j + b + 1), lambda b: pe.wait_ge(sems["act_evac"], 6 * j + 3 + b + 1)][t]
                    tile(4 * j + t, t % 2, 0, free, hr=0)

            def out_tiles(n0, ed0, hr):
                with pe.Fori(0, KC // 2) as i:
                    for u in range(2):
                        tile(n0 + 2 * i + u, (n0 + u) % 2, 0,
                             lambda b: pe.wait_ge(sems["dve_evac"], START["dve_evac"] + ed0 + 6 * i + 3 * u - 3 + b + 1), hr=hr)

            def feed(r, n0, ea0, ed0, hr):
                pe.wait_ge(sems[f"ple{r}_in"], 48)
                for c in range(PC):
                    for h_, src in enumerate((sA, sZ, sU)):
                        if c:
                            pe.wait_ge(sems[f"ple{r}_lo"], h_ + 1)
                        if h_ < 2:
                            for i in range(4):
                                last = tp(PS[:, 3 + h_, i * P:(i + 1) * P], src[:, i * PLE + c * P:i * PLE + (c + 1) * P], ident[:, :])
                        else:
                            last = tp(PS[:, 5, 0:NS], src[0:NS, c * P:(c + 1) * P], ident[0:NS, 0:NS])
                        last.then_inc(sems[f"ple{r}_turned"], 1)
                pe.wait_ge(sems[f"ple{r}_lo"], 6)
                pe.wait_ge(sems["dve_evac"], START["dve_evac"] + ed0)
                with pe.Fori(0, KC // 2) as i:
                    for u in range(2):
                        n, par = n0 + 2 * i + u, (n0 + u) % 2
                        tile(n, par, 0, lambda b: pe.wait_ge(sems["act_evac"], ea0 + 6 * i + 3 * u - 3 + b + 1), hr=hr)
                        tile(n, par, 3, lambda b: pe.wait_ge(sems["dve_evac"], START["dve_evac"] + ed0 + 6 * i + 3 * u - 3 + b + 1),
                             k0=KC, nk=PC, hi=PTh, lo=PTl)

            out_tiles(N_A2, ED_A2, 8)
            for c in range(2):
                for i in range(4):
                    last = tp(PS[0:18, 6 + c, i * P:(i + 1) * P], uc[:, 4 * c + i, :], ident[:, :])
                last.then_inc(sems["uc_turned"], 1)
            feed(0, N_A3, EA_A3, ED_A3, 16)
            norm_sum(1)
            pe.wait_ge(sems["act_evac"], EA_F)
            tile(N_F, N_F % 2, 0, lambda b: None, hr=24)
            pe.wait_ge(sems["s_logf"], 16 * DB * PAGES)
            for pg in range(PAGES):
                for x in range(pg, PAGES):
                    last = mm(S[:, pg * P:(pg + 1) * P], LFP[:, x, :, :].rearrange("p b h -> p (b h)"),
                              (tri if x == pg else ones)[:, :], start=(x == pg), stop=(x == PAGES - 1))
            last.then_inc(sems["s_rest"], 1)
            pe.wait_ge(sems["f_lf"], 1)
            for t in range(9):
                n = P if t < 8 else NS
                last = tp(PS[0:n, 6, t * H:(t + 1) * H], lfT[:, t * P:t * P + n], ident[0:H, 0:H])
            last.then_inc(sems["f_turned"], 1)
            pe.wait_ge(sems["s_lf8"], 1)
            mm(PS[:, 5, 0:NS], lf8[:, :, :].rearrange("p b h -> p (b h)"), same[:, :], start=True, stop=True)
            mm(PS[0:NS, 5, P:P + H], same[:, :], lfn[0:NS, 8, :], start=True, stop=True).then_inc(sems["s_cn"], 1)

            def dense_piece(j, half, p):
                i, b, k = 2 * half + p // 24, p % 24 // KC, p % KC
                g_ = 4 * j + 3 + i
                par = (N_B1 + 3 + i) % 2
                if p % 24 == 0:
                    pe.wait_ge(sems["w_split"], START["w_split"] + N_B1 + g_ + 1)
                if k == 0:
                    pe.wait_ge(sems["act_evac"], EA_B1 + 3 * g_ - 3 + b + 1)
                s, e = BLK[b]
                out = PS[:, b, 0:e - s]
                wh, wl = whi[:, par, k, :], wlo[:, par, k, :]
                mm(out, wh, Hhi[:, k, s:e], start=(k == 0), stop=False)
                mm(out, wh, Hlo[:, k, s:e], start=False, stop=False)
                last = mm(out, wl, Hhi[:, k, s:e], start=False, stop=(k == KC - 1))
                if k == KC - 1:
                    last.then_inc(sems["block_done"], 1)

            def turn_part(j, t, i):
                if i == 0:
                    pe.wait_ge(sems["staged"], 3 * j + (1, 3)[t])
                if i == 2:
                    pe.wait_ge(sems["kv_nat"], 6 * j + 3 * t + 1)
                src = (stK, stQ)[t]
                for y, x in enumerate(TURN_PARTS[i]):
                    n = P if x < 8 else NS
                    last = tp(PS[0:n, 5 + i % 2, y * P:(y + 1) * P], src[:, x * P:x * P + n], ident[:, :])
                last.then_inc(sems["kv_turned"], 1)

            def scores(j, hh, qb):
                c = 8 * hh + qb
                n = (qb + 1) * P
                pe.wait_ge(sems["exp"], START["exp"] + 16 * j + c - (1 if 0 < qb < 4 else 0))
                if qb == 0:
                    pe.wait_ge(sems["kq_lo"], 3 * j + 2 + hh)
                    pe.wait_ge(sems[f"aug_in{hh}"], 32 * j + 32)
                q = slice(qb * P, (qb + 1) * P)
                out = score_bank(qb)
                for c0 in range(0, n, 512):
                    w = min(512, n - c0)
                    mm(out[:, c0:c0 + w], QA[:, hh, q], KA[:, hh, c0:c0 + w], start=True, stop=False)
                    mm(out[:, c0:c0 + w], QB[:, hh, q], KB[:, hh, c0:c0 + w], start=False, stop=(c0 + 512 < n))
                mm(out[:, qb * P:n], identb[:, :], maskb[:, :], start=False, stop=True).then_inc(sems["score"], 1)

            def turn_p(j, hh, grp, kb, more):
                u = 12 * hh + 4 * grp + kb
                q0 = max(0, kb - QG * grp)
                if kb == 0:
                    pe.wait_ge(sems["p_norm"], 16 * j + 8 * hh + QG * (grp + 1))
                if grp == 0 and kb == 0 and (hh == 0 or more):
                    pe.wait_ge(sems["kv_nat"], 6 * j + 6 + 3 * hh)
                pe.wait_ge(sems["p_lo"], START["p_lo"] + 24 * j + u - 1)
                for qi in range(q0, QG):
                    off = P_OFF[QG * grp + qi] + kb * P
                    last = tp(PS[:, 5 + kb % 2, qi * P:(qi + 1) * P], Pb[:, off:off + P], ident[:, :])
                last.then_inc(sems["turned"], 1)

            def pv_step(j, hh, grp, kb):
                u = 12 * hh + 4 * grp + kb
                q0 = max(0, kb - QG * grp)
                nkb = QG * (grp + 1)
                if kb == 0:
                    pe.wait_ge(sems["o_done"], START["o_done"] + 4 * j + 2 * hh + grp)
                    pe.wait_ge(sems["v_lo"], j + 1)
                pe.wait_ge(sems["p_lo"], START["p_lo"] + 24 * j + u + 1)
                for x in (pTh, pTl):
                    last = mm(PS[:, 7, q0 * P:512], VS[:, kb, hh, :], x[:, kb % 2, q0 * P:512],
                              start=(kb == 0 and x is pTh), stop=(kb == nkb - 1 and x is pTl))
                last.then_inc(sems["pv"], 1)

            def half_pair(j, half, more):
                p = 0
                for step in STEPS:
                    if step[0] == "S":
                        scores(j, half, step[1])
                    if step[0] == "T":
                        turn_p(j, half, step[1], step[2], more)
                    if step[0] == "V":
                        pv_step(j, half, step[1], step[2])
                    if step[0] == "N" and (half == 0 or more):
                        turn_part(j + half, 1 - half, step[1])
                    if step[0] == "D":
                        for _ in range(step[1]):
                            if more or PIECES * half + p < 24:
                                dense_piece(j, half, p)
                            p += 1

            for p in range(24, PIECES):
                dense_piece(-1, 0, p)
            for p in range(PIECES):
                dense_piece(-1, 1, p)
                if p == 8:
                    for i in range(3):
                        turn_part(0, 0, i)
            with pe.Fori(0, NPAIR - 1) as j:
                half_pair(j, 0, True)
                half_pair(j, 1, True)
            half_pair(NPAIR - 1, 0, False)
            half_pair(NPAIR - 1, 1, False)

            pe.wait_ge(sems["act_evac"], EA_B2)
            pe.wait_ge(sems["exp"], START["exp"] + 16 * NPAIR)
            pe.wait_ge(sems["p_lo"], START["p_lo"] + 24 * NPAIR)
            pe.wait_ge(sems["o_done"], START["o_done"] + 4 * NPAIR)

            def k_turn(b, pg):
                pe.wait_ge(sems[f"k_in{pg}"], 16 * b + 16)
                for c in range(2):
                    pe.wait_ge(sems[f"s_kt{c}"], 1 + PAGES * b + pg)
                    for i in range(4 * c, 4 * c + 4):
                        last = tp(PS[:, c, (i % 4) * P:(i % 4 + 1) * P], Kr[:, pg, i * P:(i + 1) * P], ident[:, :])
                    last.then_inc(sems["s_kturn"], 1)

            def s_bank(s_, c):
                return PS[:, 2 + 2 * s_ + c, :]

            def s_bias(b, out, s_, c0, n):
                rows = slice(4 * s_, 4 * s_ + 4)
                w = lambda x: x[:, rows, :].rearrange("p i n -> p (i n)")
                mm(out, w(pick), RT[:, 0, c0:c0 + n], start=True, stop=False)
                mm(out, w(pick), RT[:, 1, c0:c0 + n], start=False, stop=False)
                mm(out, w(cqh), onesr[:, 0:n], start=False, stop=False)
                mm(out, w(cql), onesr[:, 0:n], start=False, stop=False)

            def s_scores(b, pp):
                for c in range(2):
                    pe.wait_ge(sems[f"s_kt{c}"], 1 + PAGES * b + 2 * pp + 2)
                for i in range(NPAIR):
                    r = 32 * (i % 4)
                    last = mm(s_bank(i // 4, pp // 2)[r:r + 32, 256 * (pp % 2):256 * (pp % 2) + 256], qc[:, i, :],
                              KT[:, pp % 2, i, :], start=False, stop=(pp % 2 == 1))
                last.then_inc(sems["s_score"], 1)

            def s_new(b):
                pe.wait_ge(sems["s_osb"], START["s_osb"] + b)
                for s_ in range(2):
                    out = PS[:, 6, NS * s_:NS * s_ + NS]
                    s_bias(b, out, s_, KEYS, NS)
                    mm(out, mq[:, :, :].rearrange("p g n -> p (g n)"), maskQ[:, :], start=False, stop=False)
                    for i in range(4 * s_, 4 * s_ + 4):
                        r = 32 * (i % 4)
                        last = mm(PS[r:r + 32, 6, NS * s_:NS * s_ + NS], qc[:, i, :], knT[:, i, :], start=False, stop=True)
                last.then_inc(sems["s_all"], 1)

            def s_p_turn(b):
                pe.wait_ge(sems["s_exp"], START["s_exp"] + b + 1)
                for r, (bank, s_, k0) in enumerate(P_ROUNDS):
                    if bank == 7:
                        pe.wait_ge(sems["s_out"], START["s_out"] + b)
                    if k0 == PAGES:
                        for x in range(2):
                            last = tp(PS[0:NS, bank, x * P:(x + 1) * P], Ps[:, x, KEYS:], ident[:, :])
                    else:
                        for x in range(4):
                            last = tp(PS[:, bank, x * P:(x + 1) * P], Ps[:, s_, (k0 + x) * P:(k0 + x + 1) * P], ident[:, :])
                    last.then_inc(sems["s_back"], 1)

            def s_values(b):
                for s_ in range(2):
                    pe.wait_ge(sems["s_pt0"], START["s_pt0"] + 3 * b + 2 + s_)
                    pe.wait_ge(sems["s_pt1"], START["s_pt1"] + 2 * b + 1 + s_)
                    for pg in range(PAGES + 1):
                        if s_ == 0 and pg < PAGES:
                            pe.wait_ge(sems[f"v_in{pg}"], 16 * b + 16)
                        for g_ in range(4):
                            i = 4 * s_ + g_
                            k, v = (P, Vb[:, pg, i * P:(i + 1) * P]) if pg < PAGES else (NS, vnew[:, i * P:(i + 1) * P])
                            last = mm(PS[32 * g_:32 * g_ + 32, 6, P * (1 + s_):P * (2 + s_)],
                                      PsT[0:k, s_, pg, 32 * g_:32 * g_ + 32], v, start=(pg == 0), stop=(pg == PAGES))
                last.then_inc(sems["s_pv"], 1)

            def s_y_turn(b):
                pe.wait_ge(sems["s_osb"], START["s_osb"] + b + 1)
                pe.wait_ge(sems["s_pt0"], START["s_pt0"] + 3 * b + 3)
                for s_ in range(2):
                    last = tp(PS[:, 7, s_ * P:(s_ + 1) * P], Osb[:, s_, :], ident[:, :])
                last.then_inc(sems["s_yturn"], 1)

            def sample_batch(b, more):
                pe.wait_ge(sems["s_prep"], b + 1)
                pe.wait_ge(sems["s_pt0"], START["s_pt0"] + 3 * b)
                pe.wait_ge(sems["s_pt1"], START["s_pt1"] + 2 * b)
                for s_ in range(2):
                    for c in range(2):
                        s_bias(b, s_bank(s_, c), s_, 512 * c, 512)
                k_turn(b, 3)
                s_scores(b, 0)
                for pp in range(1, 4):
                    if pp < 3:
                        k_turn(b, 2 * pp + 2)
                        k_turn(b, 2 * pp + 3)
                    s_scores(b, pp)
                s_new(b)
                if more:
                    k_turn(b + 1, 0)
                    k_turn(b + 1, 1)
                s_p_turn(b)
                s_values(b)
                if more:
                    k_turn(b + 1, 2)
                s_y_turn(b)

            pe.wait_ge(sems["s_restin"], 16)
            for pg in range(3):
                k_turn(0, pg)
            with pe.Fori(0, DB - 1) as b:
                sample_batch(b, True)
            sample_batch(DB - 1, False)

            out_tiles(N_B2, ED_B2, 32)
            feed(1, N_B3, EA_B3, ED_B3, 40)
            norm_sum(2)
            pe.wait_ge(sems["y_norm"], KC)
            pe.wait_ge(sems["dve_evac"], START["dve_evac"] + ED_END)
            pe.wait_ge(sems["act_evac"], EA_END)
            for tt in range(9):
                n = P if tt < 8 else NS
                for c in range(2):
                    if tt:
                        pe.wait_ge(sems[("y_act", "y_dve")[c]], tt)
                    for i in range(4):
                        last = tp(PS[0:n, c, i * P:(i + 1) * P], X[:, 4 * c + i, tt * P:tt * P + n], ident[:, :])
                    last.then_inc(sems["y_turned"], 1)

        @block.scalar
        def _(act):
            for k, n in LEAD["scalar"].items():
                act.sem_inc(sems[k], n)
            af = act.activation

            def w_hi(par, blocks, count=None, gained=None, nk=KC):
                if gained is None:
                    act.wait_ge(sems[f"w_in{par}"], count)
                else:
                    act.wait_ge(sems["w_gained"], gained)
                act.wait_ge(sems["block_done"], START["block_done"] + blocks)
                af(whi[:, par, 0:nk, :], raw[:, par, 0:nk, :], ACT.Copy).then_inc(sems["w_hi"], 1)

            for k in range(KC):
                act.wait_ge(sems["x_turned"], 3 * k + 1)
                af(X[:, k, 0:512], PS[:, 0, :], ACT.Copy).then_inc(sems["x_act"], 1)
            w_hi(0, -3, loaded(0))

            def squares(r, x_ok):
                for k in range(KC):
                    x_ok(k)
                    if k >= 3:
                        act.wait_ge(sems[f"n{r}_acc"], k - 2)
                    af(ss[:, :] if k == 0 else sq[k % 2][:, :], X[:, k, :], ACT.Square).then_inc(sems[f"n{r}_sq"], 1)

            def roots(r):
                for b, (s, e) in enumerate(BLK):
                    act.wait_ge(sems[f"n{r}_ps"], b + 1)
                    af(rs[:, s:e], PS[:, 3 + b, 0:e - s], ACT.Sqrt, scale=1.0 / D, bias=small[:, 31:32]).then_inc(sems[f"n{r}_rt"], 1)

            def normed_hi(r):
                for k in range(KC):
                    act.wait_ge(sems[f"n{r}_tmp"], k + 1)
                    af(Hhi[:, k, :], sq[k % 2][:, :], ACT.Copy).then_inc(sems["h_hi"], 1)

            def split_hi(src):
                for k in range(KC):
                    af(Hhi[:, k, :], src[:, k, :], ACT.Copy).then_inc(sems["h_hi"], 1)

            act.wait_ge(sems["const_ready"], 1)
            act.wait_ge(sems["x_turned"], 3 * KC)
            act.drain()
            squares(0, lambda k: act.wait_ge(sems["x_dve"], 2 * k + 2))
            roots(0)
            normed_hi(0)

            def conv_layer(j, last):
                for t in range(4):
                    act.drain()
                    if last and t == 3:
                        w_hi(N_A2 % 2, 3 * (N_A2 - 1), loaded(N_A2))
                    else:
                        w_hi((t + 1) % 2, 12 * j + 3 * t, loaded(t + 1, 4, j))
                    if t in (0, 2):
                        act.wait_ge(sems["dve_evac"], START["dve_evac"] + 6 * j)
                        for b, (s, e) in enumerate(BLK):
                            act.wait_ge(sems["block_done"], START["block_done"] + 12 * j + 3 * t + b + 1)
                            if t == 0:
                                af(sA[:, s:e], PS[:, b, 0:e - s], ACT.Copy).then_inc(sems["act_evac"], 1)
                            else:
                                af(sZ[:, s:e], PS[:, b, 0:e - s], ACT.Silu).then_inc(sems["act_evac"], 1)
            peeled(act, KC, conv_layer)
            act.wait_ge(sems["dve_evac"], START["dve_evac"] + ED_A2)
            act.wait_ge(sems["block_done"], START["block_done"] + B_A2)
            split_hi(Y)

            def out_tiles(n0, b0):
                def body(i, last):
                    for u in range(2):
                        n = n0 + u + 1
                        if last and u == 1:
                            w_hi(n % 2, b0 + 21, loaded(n, 2, 3), nk=KC + PC)
                        else:
                            w_hi(n % 2, b0 + 6 * i + 3 * u, loaded(n, 2, i))
                peeled(act, KC // 2, body)

            def feed(r, n0, b0, ed0, next_hi):
                for g_ in range(6):
                    act.wait_ge(sems[f"ple{r}_turned"], g_ + 1)
                    c, h_ = divmod(g_, 3)
                    n = 512 if h_ < 2 else NS
                    af(PTh[:, c, h_ * 512:h_ * 512 + n], PS[:, 3 + h_, 0:n], ACT.Copy).then_inc(sems[f"ple{r}_hi"], 1)
                act.wait_ge(sems["dve_evac"], START["dve_evac"] + ed0)
                act.wait_ge(sems["block_done"], START["block_done"] + b0)
                split_hi(X)

                def body(i, last):
                    for u in range(2):
                        if last and u == 1:
                            if next_hi:
                                next_hi(b0 + 42)
                        else:
                            w_hi((n0 + u + 1) % 2, b0 + 12 * i + 6 * u, loaded(n0 + u + 1, 2, i), nk=KC + PC)
                        act.wait_ge(sems["x_sum"], START["x_sum"] + 8 * r + 2 * i + u - 1)
                        for b, (s, e) in enumerate(BLK):
                            act.wait_ge(sems["block_done"], START["block_done"] + b0 + 12 * i + 6 * u + b + 1)
                            af(sg[:, u, s:e], PS[:, b, 0:e - s], ACT.Sigmoid).then_inc(sems["act_evac"], 1)
                peeled(act, KC // 2, body)

            out_tiles(N_A2, B_A2)
            for c in range(2):
                act.wait_ge(sems["uc_turned"], c + 1)
                af(sC[0:18, c * 512:(c + 1) * 512], PS[0:18, 6 + c, :], ACT.Copy).then_inc(sems["uc_act"], 1)
            act.drain()
            feed(0, N_A3, B_A3, ED_A3, lambda blocks: w_hi(N_F % 2, blocks, gained=1))
            act.drain()
            act.wait_ge(sems["uc_out"], 32)
            squares(1, lambda k: act.wait_ge(sems["x_sum"], START["x_sum"] + k + 1))
            roots(1)
            act.wait_ge(sems["block_done"], START["block_done"] + B_F)
            normed_hi(1)

            act.wait_ge(sems["x_parked"], 16 * KC)
            for b, (s, e) in enumerate(BLK):
                act.wait_ge(sems["block_done"], START["block_done"] + B_F + b + 1)
                af(fl[:, s:e], PS[0:H, b, 0:e - s], ACT.Identity, bias=bf_col[:, 0:1]).then_inc(sems["act_evac"], 1)
            act.drain().then_inc(sems["f_raw"], 1)
            act.wait_ge(sems["f_abs"], 1)
            af(fe[:, :], fu[:, :], ACT.Exp)
            act.drain()
            af(fm[:, :], fe[:, :], ACT.Ln, bias=1.0).then_inc(sems["f_ln"], 1)
            act.wait_ge(sems["f_turned"], 1)
            af(lfn[:, 0:8, :].rearrange("p t h -> p (t h)"), PS[:, 6, 0:8 * H], ACT.Copy)
            af(lfn[0:NS, 8, :], PS[0:NS, 6, 8 * H:9 * H], ACT.Copy)
            act.drain().then_inc(sems["f_nat"], 1)
            w_hi(N_B1 % 2, B_F, gained=2)

            def exp_scores(j, hh, qb):
                n = (qb + 1) * P
                act.wait_ge(sems["rowmax"], 16 * j + 8 * hh + qb + 1)
                af(Pb[:, P_OFF[qb]:P_OFF[qb + 1]], score_bank(qb)[:, 0:n], ACT.Exp, bias=small[:, qb:qb + 1],
                   accum_out=small[:, 8 + qb:9 + qb]).then_inc(sems["exp"], 1)

            def p_hi(j, hh, grp, kb):
                u = 12 * hh + 4 * grp + kb
                q0 = max(0, kb - QG * grp)
                act.wait_ge(sems["turned"], START["turned"] + 24 * j + u + 1)
                act.wait_ge(sems["pv"], START["pv"] + 24 * j + u - 1)
                af(pTh[:, kb % 2, q0 * P:512], PS[:, 5 + kb % 2, q0 * P:512], ACT.Copy).then_inc(sems["p_hi"], 1)

            def o_up(j, hh, grp):
                act.wait_ge(sems["pv"], START["pv"] + 24 * j + 12 * hh + (4, 12)[grp])
                if hh == 0 and grp == 0:
                    act.wait_ge(sems["z_done"], j + 1)
                hs = slice(64 * hh, 64 * hh + 64)
                af(yT[hs, 512 * grp:512 * grp + 512], PS[64:128, 7, :], ACT.Copy).then_inc(sems["o_up"], 1)

            def k_hi(hh):
                for half in range(2):
                    af(KA[64 * half:64 * half + 64, hh, :], stK[64 * hh:64 * hh + 64, 0:SEQ], ACT.Copy)

            def q_hi(hh):
                rows = stQ[64 * hh:64 * hh + 64, 0:SEQ]
                af(QA[64 * hh:64 * hh + 64, hh, :], rows, ACT.Copy)
                af(QB[0:HD, hh, :], rows, ACT.Copy)

            def evacuate(j, half, i, b, attend):
                g_ = 4 * j + 3 + i
                s, e = BLK[b]
                if i == 0 and b == 0:
                    act.wait_ge(sems["o_done"], START["o_done"] + 4 * j)
                if i == 1 and b == 0 and attend:
                    act.wait_ge(sems["kq_lo"], 3 * j + 3)
                if i == 2 and b == 0 and attend:
                    act.wait_ge(sems["kv_turned"], 6 * j + 6)
                if i == 3 and b == 0:
                    act.wait_ge(sems["kq_lo"], 3 * j + 6)
                act.wait_ge(sems["block_done"], START["block_done"] + B_B1 + 3 * g_ + b + 1)
                af((zf, stK, stQ, stQ)[i][:, s:e], PS[:, b, 0:e - s], ACT.Copy,
                   scale=SCALE if i == 2 else 1.0).then_inc(sems["act_evac"], 1)
                if b < NB - 1:
                    return
                if i == 0:
                    act.drain()
                    act.wait_ge(sems["y_out"], START["y_out"] + 16 * j)
                    af(yT[:, :], zf[:, :], ACT.Exp, scale=-1.0).then_inc(sems["z_exp"], 1)
                else:
                    act.drain().then_inc(sems["staged"], 1)
                if i == 2:
                    q_hi(0)
                    act.drain().then_inc(sems["kq_hi"], 1)

            leaves = [{7: (0, 0), 15: (0, 1), 23: (0, 2), 31: (1, 0), 39: (1, 1), 47: (1, 2)},
                      {7: (2, 0), 15: (2, 1), 23: (2, 2), 37: (3, 0), 39: (3, 1), 47: (3, 2)}]

            def beside(j, half, p, attend, more):
                i = 2 * half + p // 24
                if p % 24 == 16 and more:
                    w_hi((N_B1 + i) % 2, B_B1 + 3 * (4 * j + 3 + i), gained=4 * j + 3 + i + 3)
                if half == 0 and p == 4 and attend:
                    act.wait_ge(sems["kv_nat"], 6 * j + 6)
                    act.wait_ge(sems["pv"], START["pv"] + 24 * j)
                    af(VS[:, :, :, 0:HD], KN[:, 0:8, :].rearrange("p t (h n) -> p t h n", h=2), ACT.Copy).then_inc(sems["v_hi"], 1)
                if half == 1 and p == 0 and more:
                    k_hi(0)
                    act.drain().then_inc(sems["kq_hi"], 1)
                if half == 1 and p == 30 and more:
                    if attend:
                        act.wait_ge(sems["score"], START["score"] + 16 * j + 16)
                    k_hi(1)
                if half == 1 and p == 32 and more:
                    q_hi(1)
                    act.drain().then_inc(sems["kq_hi"], 1)
                if p in leaves[half] and (more or PIECES * half + p < 24):
                    evacuate(j, half, *leaves[half][p], attend)

            def half_pair(j, half, more):
                p = 0
                for step in STEPS:
                    if step[0] == "S":
                        exp_scores(j, half, step[1])
                    if step[0] == "T":
                        p_hi(j, half, step[1], step[2])
                    if step[0] == "V" and step[2] == (3, 7)[step[1]]:
                        o_up(j, half, step[1])
                    if step[0] == "D":
                        for _ in range(step[1]):
                            beside(j, half, p, True, more)
                            p += 1

            for p in range(24, PIECES):
                beside(-1, 0, p, False, True)
            for p in range(PIECES):
                beside(-1, 1, p, False, True)
            with act.Fori(0, NPAIR - 1) as j:
                half_pair(j, 0, True)
                half_pair(j, 1, True)
            half_pair(NPAIR - 1, 0, False)
            half_pair(NPAIR - 1, 1, False)

            act.drain()

            def keep_keys(b, pg):
                act.wait_ge(sems["s_kturn"], 2 * PAGES * b + 2 * pg + 1)
                act.wait_ge(sems["s_score"], START["s_score"] + 4 * b + pg // 2 - 1)
                af(KT[:, pg // 2 % 2, 0:4, pg % 2 * P:(pg % 2 + 1) * P], PS[:, 0, :].rearrange("p (i n) -> p i n", i=4),
                   ACT.Copy).then_inc(sems["s_kt0"], 1)

            def sample_batch(b, more):
                for pg in range(3, PAGES):
                    keep_keys(b, pg)
                if more:
                    keep_keys(b + 1, 0)
                act.wait_ge(sems["s_max"], b + 1)
                for s_ in range(2):
                    for col, src, dst in ((4, flat[:, 512 * (2 + 2 * s_):512 * (4 + 2 * s_)], Ps[:, s_, 0:KEYS]),
                                          (6, PS[:, 6, NS * s_:NS * s_ + NS], Ps[:, s_, KEYS:])):
                        af(dst, src, ACT.Exp, bias=small[:, s_:s_ + 1], accum_out=small[:, col + s_:col + s_ + 1])
                act.drain().then_inc(sems["s_exp"], 1)
                if more:
                    keep_keys(b + 1, 1)
                act.wait_ge(sems["s_pv"], START["s_pv"] + b)
                for r in (0, 2, 4):
                    bank, s_, k0 = P_ROUNDS[r]
                    act.wait_ge(sems["s_back"], 5 * b + r + 1)
                    if k0 == PAGES:
                        af(PsT[0:NS, :, 8, :], PS[0:NS, bank, 0:2 * P].rearrange("p (s n) -> p s n", s=2), ACT.Copy).then_inc(sems["s_pt0"], 1)
                    else:
                        af(PsT[:, s_, k0:k0 + 4, :].rearrange("p t n -> p (t n)"), PS[:, bank, :], ACT.Copy).then_inc(sems["s_pt0"], 1)
                if more:
                    keep_keys(b + 1, 2)

            for pg in range(3):
                keep_keys(0, pg)
            with act.Fori(0, DB - 1) as b:
                sample_batch(b, True)
            sample_batch(DB - 1, False)

            act.drain()
            act.wait_ge(sems["y_back"], 16 * KC)
            act.wait_ge(sems["y_merged"], 1)
            w_hi(N_B2 % 2, B_B2 - 3, loaded(N_B2))
            split_hi(Y)
            out_tiles(N_B2, B_B2)
            feed(1, N_B3, B_B3, ED_B3, None)
            act.drain()
            squares(2, lambda k: act.wait_ge(sems["x_sum"], START["x_sum"] + 8 + k + 1))
            roots(2)
            act.drain()
            for tt in range(9):
                n = P if tt < 8 else NS
                act.wait_ge(sems["y_turned"], 2 * tt + 1)
                if tt >= 2:
                    act.wait_ge(sems[f"y_dma{tt % 2}"], 16 * (tt // 2))
                af(Y[0:n, tt % 2, 0:512], PS[0:n, 0, :], ACT.Copy).then_inc(sems["y_act"], 1)

        @block.vector
        def _(ve):
            for k, n in LEAD["vector"].items():
                ve.sem_inc(sems[k], n)
            tt_, ts_, stt = ve.tensor_tensor, ve.tensor_scalar, ve.scalar_tensor_tensor

            def w_lo(par, n, nk=KC):
                ve.wait_ge(sems["w_hi"], n + 1)
                tt_(wlo[:, par, 0:nk, :], raw[:, par, 0:nk, :], f(whi[:, par, 0:nk, :]), ALU.subtract).then_inc(sems["w_split"], 1)

            ve.wait_ge(sems["g_turned"], 1)
            ve.tensor_copy(GT[:, :, :].rearrange("p k n -> p (k n)"), PS[:, 7, 0:KC * G_N]).then_inc(sems["g_ready"], 1)
            for k in range(KC):
                ve.wait_ge(sems["x_turned"], 3 * k + 2)
                ve.tensor_copy(X[:, k, 512:SEQ], PS[:, 1, :]).then_inc(sems["x_dve"], 1)
                ve.wait_ge(sems["x_turned"], 3 * k + 3)
                ve.tensor_copy(X[:, k, SEQ:], PS[:, 2, 0:NS]).then_inc(sems["x_dve"], 1)
            w_lo(0, 0)

            def sum_squares(r):
                for k in range(1, KC):
                    ve.wait_ge(sems[f"n{r}_sq"], k + 1)
                    tt_(ss[:, :], ss[:, :], sq[k % 2][:, :], ALU.add).then_inc(sems[f"n{r}_acc"], 1)
                    ve.drain()

            def reciprocals(r):
                ve.wait_ge(sems[f"n{r}_rt"], NB)
                ve.reciprocal(rs[:, :], rs[:, :])
                ve.drain()

            def h_lo(src, k, h0):
                ve.wait_ge(sems["h_hi"], h0 + k + 1)
                tt_(Hlo[:, k, :], src, f(Hhi[:, k, :]), ALU.subtract).then_inc(sems["h_ready"], 1)

            def normed(r, gain, h0):
                reciprocals(r)
                for k in range(KC + 1):
                    ve.drain()
                    if k < KC:
                        if gain is None:
                            tt_(sq[k % 2][:, :], X[:, k, :], rs[:, :], ALU.mult).then_inc(sems[f"n{r}_tmp"], 1)
                        else:
                            stt(out=sq[k % 2][:, :], in0=X[:, k, :], scalar=GT[:, k, gain:gain + 1], in1=rs[:, :],
                                op0=ALU.mult, op1=ALU.mult).then_inc(sems[f"n{r}_tmp"], 1)
                    if k:
                        ve.drain()
                        h_lo(sq[(k - 1) % 2][:, :], k - 1, h0)

            ve.memset(Up[:, 0:2], 0.0)
            ve.drain()
            sum_squares(0)
            normed(0, G_A, 0)

            def conv_layer(j, last):
                for t in range(4):
                    if last and t == 3:
                        w_lo(N_A2 % 2, N_A2)
                    else:
                        w_lo((t + 1) % 2, 4 * j + t + 1)
                    ve.drain()
                    if t == 1:
                        for b, (s, e) in enumerate(BLK):
                            ve.wait_ge(sems["act_evac"], 6 * j + b + 1)
                            ve.wait_ge(sems["block_done"], START["block_done"] + 12 * j + 3 + b + 1)
                            m = min(e, SEQ)
                            ins = tt_(Up[:, 2 + s:2 + m], PS[:, b, 0:m - s], sA[:, s:m], ALU.mult)
                            if e > SEQ:
                                ins = tt_(Us[:, :, 2:], PS[:, b, SEQ - s:e - s].rearrange("p (b t) -> p b t", b=DB),
                                          sA[:, SEQ:e].rearrange("p (b t) -> p b t", b=DB), ALU.mult)
                            ins.then_inc(sems["dve_evac"], 1)
                        g = lambda r, n=1: GT[:, bass.ds(j, 1), r:r + n].rearrange("p a n -> p (a n)")
                        ve.tensor_copy(Us[:, :, 0:2], g(G_ST, 16).rearrange("p (b w) -> p b w", b=DB))
                        ve.drain()
                        cs = sC[:, SEQ:].rearrange("p (b t) -> p b t", b=DB)
                        for w in range(CW):
                            for dst, src in ((sC[:, 0:SEQ], Up[:, w:w + SEQ]), (cs, Us[:, :, w:w + DS])):
                                if w == 0:
                                    ts_(dst, src, g(G_CW), None, ALU.mult)
                                else:
                                    stt(out=dst, in0=src, scalar=g(G_CW + w), in1=dst, op0=ALU.mult, op1=ALU.add)
                            ve.drain()
                        ucj = at_pair(uc, j).rearrange("p a n -> p (a n)")
                        ve.tensor_copy(ucj[:, 0:2], Up[:, SEQ:SEQ + 2])
                        ve.tensor_copy(ucj[:, 2:18].rearrange("p (b w) -> p b w", b=DB), Us[:, :, DS:])
                    if t == 2:
                        ve.wait_ge(sems["act_evac"], 6 * j + 6)
                        tt_(sC[:, :], sC[:, :], sZ[:, :], ALU.mult)
                        ve.drain()
                    if t == 3:
                        for b, (s, e) in enumerate(BLK):
                            ve.wait_ge(sems["block_done"], START["block_done"] + 12 * j + 9 + b + 1)
                            tt_(at_pair(Y, j).rearrange("p a n -> p (a n)")[:, s:e], PS[:, b, 0:e - s], sC[:, s:e],
                                ALU.mult).then_inc(sems["dve_evac"], 1)
            peeled(ve, KC, conv_layer)

            def split_lo(src, h0):
                for k in range(KC):
                    h_lo(src[:, k, :], k, h0)

            def add_x(m, ps_, s, e):
                x = at_pair(X, m).rearrange("p a n -> p (a n)")[:, s:e] if not isinstance(m, int) else X[:, m, s:e]
                return tt_(x, x, ps_, ALU.add)

            def out_tiles(n0, b0):
                def body(i, last):
                    for u in range(2):
                        n = n0 + u + 1
                        w_lo(n % 2, n + 2 * i, nk=KC + PC if last and u == 1 else KC)
                        for b, (s, e) in enumerate(BLK):
                            ve.wait_ge(sems["block_done"], START["block_done"] + b0 + 6 * i + 3 * u + b + 1)
                            add_x(2 * i + u, PS[:, b, 0:e - s], s, e).then_inc(sems["dve_evac"], 1)
                peeled(ve, KC // 2, body)

            def feed(r, n0, b0, ea0, h0):
                for g_ in range(6):
                    ve.wait_ge(sems[f"ple{r}_hi"], g_ + 1)
                    c, h_ = divmod(g_, 3)
                    n = 512 if h_ < 2 else NS
                    tt_(PTl[:, c, h_ * 512:h_ * 512 + n], PS[:, 3 + h_, 0:n], f(PTh[:, c, h_ * 512:h_ * 512 + n]),
                        ALU.subtract).then_inc(sems[f"ple{r}_lo"], 1)
                split_lo(X, h0)

                def body(i, last):
                    for u in range(2):
                        n = n0 + u + 1
                        if last and u == 1:
                            if r == 0:
                                w_lo(n % 2, N_F)
                        else:
                            w_lo(n % 2, n + 2 * i, nk=KC + PC)
                        for b, (s, e) in enumerate(BLK):
                            ve.wait_ge(sems["act_evac"], ea0 + 6 * i + 3 * u + b + 1)
                            ve.wait_ge(sems["block_done"], START["block_done"] + b0 + 12 * i + 6 * u + 3 + b + 1)
                            tt_(sg[:, u, s:e], sg[:, u, s:e], PS[:, 3 + b, 0:e - s], ALU.mult).then_inc(sems["dve_evac"], 1)
                        ve.drain()
                        add_x(2 * i + u, sg[:, u, :], 0, TT).then_inc(sems["x_sum"], 1)
                peeled(ve, KC // 2, body)

            split_lo(Y, 8)
            out_tiles(N_A2, B_A2)
            ve.drain()
            feed(0, N_A3, B_A3, EA_A3, 16)
            ve.drain()
            sum_squares(1)
            normed(1, None, 24)

            ve.wait_ge(sems["f_raw"], 1)
            stt(out=fu[:, :], in0=fl[:, :], scalar=-1.0, in1=fl[:, :], op0=ALU.mult, op1=ALU.min).then_inc(sems["f_abs"], 1)
            ve.memset(one16[:, :], 1.0)
            ve.wait_ge(sems["f_ln"], 1)
            stt(out=lfT[:, :], in0=fl[:, :], scalar=0.0, in1=fm[:, :], op0=ALU.min, op1=ALU.subtract)
            ve.drain().then_inc(sems["f_lf"], 1)
            ve.tensor_tensor_scan(fe[:, 0:SEQ], one16[:, :], lfT[:, 0:SEQ], 0.0, ALU.mult, ALU.add)
            ve.tensor_copy(ch[:, 4, :], one16[:, :])
            ve.drain()
            ve.tensor_copy(ch[:, 0, :], fe[:, 0:SEQ])
            ve.drain()
            tt_(ch[:, 1, :], fe[:, 0:SEQ], f(ch[:, 0, :]), ALU.subtract)
            ve.drain()
            ts_(ch[:, 2:4, :], f(ch[:, 0:2, :]), -1.0, None, ALU.mult)
            ve.drain().then_inc(sems["f_aug"], 1)
            ve.wait_ge(sems["f_nat"], 1)
            ve.tensor_copy(lf8[:, :, :], lfn[0:NS, 8, :].unsqueeze(1).to_broadcast([NS, DB, H])).then_inc(sems["s_lf8"], 1)
            ve.wait_ge(sems["s_cn"], 1)
            ve.tensor_copy(cn[:, :], PS[0:NS, 5, P:P + H])
            ve.tensor_copy(RTs[:, 0, 0:KEYS], S[:, 0:KEYS])
            ts_(RTs[:, 0, KEYS:], PS[:, 5, 0:NS], -1.0, None, ALU.mult)
            ve.drain()
            tt_(RTs[:, 1, 0:KEYS], S[:, 0:KEYS], f(RTs[:, 0, 0:KEYS]), ALU.subtract)
            stt(out=RTs[:, 1, KEYS:], in0=PS[:, 5, 0:NS], scalar=-1.0, in1=f(RTs[:, 0, KEYS:]), op0=ALU.mult, op1=ALU.subtract)
            ve.drain().then_inc(sems["s_restsb"], 1)
            w_lo(N_B1 % 2, N_B1)

            def row_max(j, hh, qb):
                n = (qb + 1) * P
                ve.wait_ge(sems["score"], START["score"] + 16 * j + 8 * hh + qb + 1)
                ve.reduce_max(small[:, qb:qb + 1], score_bank(qb)[:, 0:n], AXX, negate=True).then_inc(sems["rowmax"], 1)

            def row_sum(j, hh, qb):
                ve.wait_ge(sems["exp"], START["exp"] + 16 * j + 8 * hh + qb + 1)
                ve.reciprocal(small[:, 16 + qb:17 + qb], small[:, 8 + qb:9 + qb]).then_inc(sems["rinv"], 1)

            def p_lo(j, hh, grp, kb):
                u = 12 * hh + 4 * grp + kb
                q0 = max(0, kb - QG * grp)
                ve.wait_ge(sems["p_hi"], 24 * j + u + 1)
                tt_(pTl[:, kb % 2, q0 * P:512], PS[:, 5 + kb % 2, q0 * P:512], f(pTh[:, kb % 2, q0 * P:512]),
                    ALU.subtract).then_inc(sems["p_lo"], 1)

            def output(j, hh, grp):
                hs, cols = slice(64 * hh, 64 * hh + 64), slice(512 * grp, 512 * grp + 512)
                ve.wait_ge(sems["o_up"], 4 * j + 2 * hh + grp + 1)
                tt_(yT[hs, cols], PS[0:64, 7, :], yT[hs, cols], ALU.add)
                ve.drain()
                tt_(yT[hs, cols], yT[hs, cols], zf[hs, cols], ALU.mult).then_inc(sems["o_done"], 1)

            def keep_part(j, t, i):
                if i == 0:
                    ve.wait_ge(sems["kv_out"], START["kv_out"] + 64 * j + 32 * t)
                    if t == 0:
                        ve.wait_ge(sems["v_hi"], j)
                ve.wait_ge(sems["kv_turned"], 6 * j + 3 * t + i + 1)
                if i < 2:
                    x, n = TURN_PARTS[i][0], len(TURN_PARTS[i])
                    ve.tensor_copy(KN[:, x:x + n, :].rearrange("p t n -> p (t n)"), PS[:, 5 + i, 0:n * P]).then_inc(sems["kv_nat"], 1)
                else:
                    ve.tensor_copy(KN[:, 7, :], PS[:, 5, 0:P])
                    if t == 1:
                        ve.tensor_copy(vnew[:, bass.ds(P * j, P)], PS[0:NS, 5, P:2 * P])
                    ve.tensor_copy(KN[0:NS, 8, :], PS[0:NS, 5, P:2 * P])
                    ve.drain().then_inc(sems["kv_nat"], 1)

            def k_lo(hh):
                hs = slice(64 * hh, 64 * hh + 64)
                tt_(KB[0:HD, hh, :], stK[hs, 0:SEQ], f(KA[hs, hh, :]), ALU.subtract)

            def q_lo(hh):
                hs, other = slice(64 * hh, 64 * hh + 64), slice(64 - 64 * hh, 128 - 64 * hh)
                tt_(QA[other, hh, :], stQ[hs, 0:SEQ], f(QA[hs, hh, :]), ALU.subtract)

            def q_sample(j, hh):
                hs = slice(64 * hh, 64 * hh + 64)
                if isinstance(j, int) and hh == 0:
                    ve.wait_ge(sems["qd_zero"], 1)
                ve.tensor_copy(qd[hs, bass.ds(j, 1), :, DS * hh:DS * hh + DS].rearrange("p a b t -> p (a b) t"),
                               stQ[hs, SEQ:].rearrange("p (b t) -> p b t", b=DB))

            def beside(j, half, p, attend, more):
                i = 2 * half + p // 24
                if p % 24 == 17 and more:
                    w_lo((N_B1 + i) % 2, N_B1 + 4 * j + 3 + i + 1)
                if half == 0 and p == 6 and attend:
                    ve.wait_ge(sems["v_hi"], j + 1)
                    tt_(VS[:, :, :, HD:], KN[:, 0:8, :].rearrange("p t (h n) -> p t h n", h=2),
                        f(VS[:, :, :, 0:HD]), ALU.subtract).then_inc(sems["v_lo"], 1)
                if half == 1 and p == 2 and more:
                    ve.wait_ge(sems["kq_hi"], 3 * j + 4)
                    k_lo(0)
                    ve.tensor_copy(at_pair(knT, j + 1).rearrange("p a n -> p (a n)"), stK[:, SEQ:])
                    ve.drain().then_inc(sems["kq_lo"], 1)
                if half == 1 and p == 27 and more:
                    ve.wait_ge(sems["kq_hi"], 3 * j + 5)
                    q_lo(0)
                    q_sample(j + 1, 0)
                    ve.drain().then_inc(sems["kq_lo"], 1)
                if half == 1 and p == 34 and more:
                    ve.wait_ge(sems["kq_hi"], 3 * j + 6)
                    k_lo(1)
                    q_lo(1)
                    q_sample(j + 1, 1)
                    ve.drain().then_inc(sems["kq_lo"], 1)
                if half == 0 and attend and p == 25:
                    ve.wait_ge(sems["z_exp"], j + 1)
                    ts_(yT[:, :], yT[:, :], 1.0, None, ALU.add)
                    ve.drain()
                    ve.reciprocal(yT[:, :], yT[:, :])
                    ve.drain()
                    tt_(zf[:, :], zf[:, :], yT[:, :], ALU.mult)
                    ve.drain().then_inc(sems["z_done"], 1)
                    ve.tensor_copy(at_pair(zsS, j).rearrange("p a n -> p (a n)"), zf[:, SEQ:])

            def half_pair(j, half, more):
                p = 0
                for step in STEPS:
                    if step[0] == "S":
                        if step[1] >= 4:
                            row_sum(j, half, step[1] - 1)
                        row_max(j, half, step[1])
                        if 1 <= step[1] < 4:
                            row_sum(j, half, step[1] - 1)
                    if step == ("V", 0, 2):
                        row_sum(j, half, 7)
                    if step[0] == "N" and (half == 0 or more):
                        keep_part(j + half, 1 - half, step[1])
                    if step[0] == "T":
                        p_lo(j, half, step[1], step[2])
                    if step[0] == "V" and step[2] == (3, 7)[step[1]]:
                        output(j, half, step[1])
                    if step[0] == "D":
                        for _ in range(step[1]):
                            beside(j, half, p, True, more)
                            p += 1

            for p in range(24, PIECES):
                beside(-1, 0, p, False, True)
            for p in range(PIECES):
                beside(-1, 1, p, False, True)
                if p == 8:
                    for i in range(3):
                        keep_part(0, 0, i)
            with ve.Fori(0, NPAIR - 1) as j:
                half_pair(j, 0, True)
                half_pair(j, 1, True)
            half_pair(NPAIR - 1, 0, False)
            half_pair(NPAIR - 1, 1, False)

            ve.drain()
            ve.wait_ge(sems["y_out"], START["y_out"] + 16 * NPAIR)
            ve.wait_ge(sems["kv_out"], START["kv_out"] + 64 * NPAIR)

            def keep_keys(b, pg):
                ve.wait_ge(sems["s_kturn"], 2 * PAGES * b + 2 * pg + 2)
                ve.wait_ge(sems["s_score"], START["s_score"] + 4 * b + pg // 2 - 1)
                ve.tensor_copy(KT[:, pg // 2 % 2, 4:8, pg % 2 * P:(pg % 2 + 1) * P],
                               PS[:, 1, :].rearrange("p (i n) -> p i n", i=4)).then_inc(sems["s_kt1"], 1)

            def prepare(b):
                rows = lambda x: x[:, :, 0:16].rearrange("p i (h q) -> p i h q", h=2)
                ve.tensor_copy(qc[:, :, 0:16], qd[:, :, bass.ds(b, 1), :].rearrange("p i b n -> p i (b n)"))
                ve.tensor_copy(rows(pick), ident[:, bass.ds(H * b, H)].rearrange("p (i h) -> p i h", h=2).unsqueeze(3)
                               .to_broadcast([P, NPAIR, 2, DS]))
                own = ident[0:NS, bass.ds(DS * b, DS)]
                for hh in range(2):
                    ve.tensor_copy(mq[:, :, 8 * hh:8 * hh + 8], own.unsqueeze(1).to_broadcast([NS, 4, DS]))
                    tt_(cq[:, :, 8 * hh:8 * hh + 8], own.unsqueeze(1).to_broadcast([NS, NPAIR, DS]),
                        cn[:, :].rearrange("p (i h) -> p i h", h=2)[:, :, hh:hh + 1].to_broadcast([NS, NPAIR, DS]), ALU.mult)
                ve.drain()
                ve.tensor_copy(cqh[:, :, :], cq[:, :, :])
                ve.drain()
                tt_(cql[:, :, :], cq[:, :, :], f(cqh[:, :, :]), ALU.subtract)
                ve.drain().then_inc(sems["s_prep"], 1)

            def sample_batch(b, more):
                for pg in range(3, PAGES):
                    keep_keys(b, pg)
                ve.wait_ge(sems["s_all"], b + 1)
                ve.reduce_max(small[:, 0:2], PS[:, 2:6, :].rearrange("p (s c) n -> p s (c n)", s=2), AXX, negate=True)
                ve.reduce_max(small[:, 2:4], PS[:, 6, 0:2 * NS].rearrange("p (s n) -> p s n", s=2), AXX, negate=True)
                ve.drain()
                tt_(small[:, 0:2], small[:, 0:2], small[:, 2:4], ALU.min)
                ve.drain().then_inc(sems["s_max"], 1)
                if more:
                    keep_keys(b + 1, 0)
                    keep_keys(b + 1, 1)
                ve.wait_ge(sems["s_exp"], START["s_exp"] + b + 1)
                tt_(small[:, 8:10], small[:, 4:6], small[:, 6:8], ALU.add)
                ve.drain()
                ve.reciprocal(small[:, 8:10], small[:, 8:10])
                ve.wait_ge(sems["s_pv"], START["s_pv"] + b)
                for r in (1, 3):
                    bank, s_, k0 = P_ROUNDS[r]
                    ve.wait_ge(sems["s_back"], 5 * b + r + 1)
                    ve.tensor_copy(PsT[:, s_, k0:k0 + 4, :].rearrange("p t n -> p (t n)"), PS[:, bank, :]).then_inc(sems["s_pt1"], 1)
                if more:
                    prepare(b + 1)
                ve.drain()
                ve.wait_ge(sems["s_pv"], START["s_pv"] + b + 1)
                for s_ in range(2):
                    ts_(Osb[:, s_, :], PS[:, 6, P * (1 + s_):P * (2 + s_)], small[:, 8 + s_:9 + s_], None, ALU.mult)
                ve.drain().then_inc(sems["s_osb"], 1)
                if more:
                    keep_keys(b + 1, 2)
                ve.wait_ge(sems["s_yturn"], b + 1)
                for hh in range(2):
                    hs = slice(64 * hh, 64 * hh + 64)
                    z = zsS[hs, :, bass.ds(DS * b, DS)]
                    ins = tt_(z, PS[hs, 7, 0:2 * P].rearrange("p (i n) -> p i n", n=32)[:, :, DS * hh:DS * hh + DS], z, ALU.mult)
                ins.then_inc(sems["s_out"], 1)

            for x in (qc, cq, mq):
                ve.memset(x[:, :, :], 0.0)
            ve.drain()
            ve.tensor_copy(pick[:, :, :], qc[:, :, :])
            ve.tensor_copy(onesr[:, :], ones[0:NS, 0:1].to_broadcast([NS, 512]))
            ve.drain()
            prepare(0)
            for pg in range(3):
                keep_keys(0, pg)
            with ve.Fori(0, DB - 1) as b:
                sample_batch(b, True)
            sample_batch(DB - 1, False)

            ve.drain()
            ve.tensor_copy(Y[:, :, SEQ:], zsS[:, :, :])
            ve.drain().then_inc(sems["y_merged"], 1)
            w_lo(N_B2 % 2, N_B2)
            split_lo(Y, 32)
            ve.wait_ge(sems["x_back"], 16 * KC)
            out_tiles(N_B2, B_B2)
            ve.drain()
            feed(1, N_B3, B_B3, EA_B3, 40)
            ve.drain()
            sum_squares(2)
            reciprocals(2)
            ve.drain()
            for k in range(KC):
                stt(out=X[:, k, :], in0=X[:, k, :], scalar=GT[:, k, G_F:G_F + 1], in1=rs[:, :],
                    op0=ALU.mult, op1=ALU.mult).then_inc(sems["y_norm"], 1)
            for tt in range(9):
                n = P if tt < 8 else NS
                ve.wait_ge(sems["y_turned"], 2 * tt + 2)
                if tt >= 2:
                    ve.wait_ge(sems[f"y_dma{tt % 2}"], 16 * (tt // 2))
                ve.tensor_copy(Y[0:n, tt % 2, 512:D], PS[0:n, 1, :]).then_inc(sems["y_dve"], 1)


INS = ["x_prompt", "x_sample", "p_prompt", "p_sample", "state_conv", "cache_k", "cache_v", "cache_logf",
       "page_table", "norm_a", "w_in_a", "conv_w_a", "w_out_a", "norm_kv", "w_kv", "b_f", "norm_b",
       "w_in_b", "w_out_b", "w_ple_proj", "w_ple_gate", "norm_f"]
OUTS = [("y_prompt", (1, SEQ, D)), ("y_sample", (DB, DS, D)), ("conv_prompt", (1, 1, CW - 1, D)),
        ("k_prompt", (1, SEQ, H, HD)), ("v_prompt", (1, SEQ, H, HD)), ("logf_prompt", (1, SEQ, H)),
        ("conv_sample", (1, DB, CW - 1, D)), ("k_sample", (DB, DS, H, HD)), ("v_sample", (DB, DS, H, HD)),
        ("logf_sample", (DB, DS, H))]


def kernel(**inputs):
    import concourse.bacc as bacc
    from concourse.bass_utils import run_bass_kernel_spmd

    nc = bacc.Bacc("TRN2", target_bir_lowering=False, num_devices=1)
    arrays, a, o = {}, {}, {}
    for name in INS:
        x = np.ascontiguousarray(inputs[name])
        arrays[f"in_{name}"] = x
        a[name] = nc.dram_tensor(f"in_{name}", x.shape, mybir.dt.from_np(x.dtype), kind="ExternalInput").ap()
    for name, shape in OUTS:
        o[name] = nc.dram_tensor(f"out_{name}", shape, F32, kind="ExternalOutput").ap()
    d = {"x": nc.dram_tensor("parked_x", (KC, P, TT), F32, kind="Internal").ap(),
         "y": nc.dram_tensor("parked_y", (KC, P, SEQ), F32, kind="Internal").ap(),
         "rest": nc.dram_tensor("key_bias", (P, 2, KEYS + NS), F32, kind="Internal").ap(),
         "augk": nc.dram_tensor("aug_k", (H, AUG, SEQ), F32, kind="Internal").ap(),
         "augq": nc.dram_tensor("aug_q", (H, AUG, SEQ), F32, kind="Internal").ap()}
    program(nc, a, o, d)
    r = run_bass_kernel_spmd(nc, [arrays], core_ids=[0])
    return tuple(r.results[0][f"out_{name}"] for name, _ in OUTS)
```

```python
from contextlib import ExitStack

import numpy as np
import concourse.bass as bass
from concourse import mybir

F32 = mybir.dt.float32
F32R = mybir.dt.float32r
BF16 = mybir.dt.bfloat16
I32 = mybir.dt.int32
ALU = mybir.AluOpType
ACT = mybir.ActivationFunctionType
AXX = mybir.AxisListType.X

P = 128
D = 1024
KC = D // P
SEQ, DB, DS = 1024, 8, 8
NS = DB * DS
TT = SEQ + NS
PLE, PC = 256, 2
H, HD = 16, 64
NPAIR = H // 2
PAGES, PAGE = 8, 128
CW = 3
EPS = 1e-6
NEG = -1e30
SCALE = HD ** -0.5
BLK = [(0, 364), (364, 728), (728, TT)]
NB = len(BLK)
QG = 4
KEYS = PAGES * PAGE
AUG = 4

G_A, G_KV, G_B, G_F, G_CW, G_ST, G_N = 0, 1, 2, 3, 4, 7, 24

N_A1, N_A2, N_A3, N_F, N_B1, N_B2, N_B3 = 0, 32, 40, 48, 49, 81, 89
B_A2, B_A3 = 96, 120
B_F = B_A3 + 48
B_B1 = B_F + 3
B_B2 = B_B1 + 96
B_B3 = B_B2 + 24
EA_A3, EA_F, EA_B1, EA_B2, EA_B3, EA_END = 48, 72, 75, 171, 171, 195
ED_A2, ED_A3, ED_B2, ED_B3, ED_END = 48, 72, 96, 120, 144
STEPS = [("S", 0), ("D", 2), ("N", 0), ("N", 1), ("D", 1), ("S", 1), ("D", 2), ("N", 2), ("D", 1), ("S", 2), ("D", 3),
         ("S", 3), ("D", 3), ("S", 4), ("D", 4), ("T", 0, 0), ("T", 0, 1), ("S", 5), ("D", 5), ("V", 0, 0), ("T", 0, 2),
         ("S", 6), ("D", 6), ("V", 0, 1), ("T", 0, 3), ("S", 7), ("D", 6), ("V", 0, 2), ("D", 1), ("V", 0, 3), ("D", 5),
         ("T", 1, 0), ("T", 1, 1)]
for _kb in range(8):
    STEPS += [("D", 1 if _kb < 7 else 2), ("V", 1, _kb)] + ([("T", 1, _kb + 2)] if _kb < 6 else [])
TURN_PARTS = [(0, 1, 2, 3), (4, 5, 6), (7, 8)]
PIECES = 48
assert sum(x[1] for x in STEPS if x[0] == "D") == PIECES
P_OFF = [sum((x + 1) * P for x in range(qb)) for qb in range(2 * QG + 1)]
P_ROUNDS = [(2, 0, 0), (3, 0, 4), (5, 1, 0), (7, 1, 4), (4, 0, PAGES)]
LEAD = {
    "tensor": {"block_done": 6, "score": 1, "turned": 1, "pv": 1, "s_score": 2, "s_pv": 1},
    "vector": {"n0_acc": 2, "n1_acc": 2, "n2_acc": 2, "w_split": 2, "x_sum": 2, "dve_evac": 6, "o_free": 1, "o_done": 1,
               "p_lo": 1, "s_kt1": 1, "s_pt1": 1, "s_osb": 1, "s_out": 1},
    "scalar": {"exp": 1, "s_kt0": 1, "s_exp": 1, "s_pt0": 1},
    "sync": {"kv_out": 16, "y_out": 16},
}
START = {name: n for per in LEAD.values() for name, n in per.items()}


def f(x):
    return x.bitcast(F32)


def program(nc, a, o, d):
    es = ExitStack()
    with es:
        def sb(ctx, name, shape, dt=F32):
            return ctx.enter_context(nc.sbuf_tensor(name, shape, dt))

        def sem(name):
            return es.enter_context(nc.semaphore(name))

        raw = sb(es, "w_raw", [P, 2, KC + PC, P])
        whi = sb(es, "w_hi", [P, 2, KC + PC, P], F32R)
        wlo = sb(es, "w_lo", [P, 2, KC + PC, P], F32R)
        ident = sb(es, "ident", [P, P])
        ones = sb(es, "ones", [P, P])
        tri = sb(es, "tri", [P, P])
        identb = sb(es, "identb", [P, P], BF16)
        maskb = sb(es, "maskb", [P, P], BF16)
        same = sb(es, "same", [NS, NS])
        maskQ = sb(es, "maskQ", [NS, NS], BF16)
        GT = sb(es, "GT", [P, KC, G_N])
        bf_col = sb(es, "bf_col", [H, 1])
        pt = sb(es, "pt", [1, DB * PAGES], I32)
        rt = sb(es, "rt", [P, 9])
        small = sb(es, "small", [P, 32])
        sl = ExitStack()
        LFP = sb(sl, "LFP", [P, PAGES, DB, H])
        sl.close()
        qd = sb(es, "qd", [P, NPAIR, DB, 2 * DS])
        knT = sb(es, "knT", [P, NPAIR, NS])
        zsS = sb(es, "zsS", [P, NPAIR, NS])
        vnew = sb(es, "vnew", [NS, D])
        lfn = sb(es, "lfn", [P, 9, H])
        cn = sb(es, "cn", [NS, H])

        sh = ExitStack()
        Hhi = sb(sh, "Hhi", [P, KC, TT], F32R)
        Hlo = sb(sh, "Hlo", [P, KC, TT], F32R)

        sa = ExitStack()
        sA = sb(sa, "scrA", [P, TT])
        sU = sb(sa, "scrU", [P, 2 + SEQ + DB * (DS + 2)])
        sC = sb(sa, "scrC", [P, TT])
        sZ = sb(sa, "scrZ", [P, TT])
        uc = sb(sa, "uc", [P, KC, 18])
        X = sb(sa, "X", [P, KC, TT])
        sy = ExitStack()
        Y = sb(sy, "Y", [P, KC, TT])
        sy.close()
        sp_ = ExitStack()
        PTh = sb(sp_, "PTh", [P, PC, TT], F32R)
        PTl = sb(sp_, "PTl", [P, PC, TT], F32R)
        sg = sb(sp_, "sg", [P, 2, TT])
        sp_.close()
        sa.close()
        Up = sU[:, 0:2 + SEQ]
        Us = sU[:, 2 + SEQ:].rearrange("p (b t) -> p b t", b=DB)
        ss, rs = sC, sC
        sq = [[sU[:, 0:TT], sZ[:, :]], [sA[:, :], sZ[:, :]], [sA[:, :], sZ[:, :]]]

        s1 = ExitStack()
        KA = sb(s1, "KA", [P, 2, SEQ], F32R)
        KB = sb(s1, "KB", [HD + AUG, 2, SEQ], F32R)
        QA = sb(s1, "QA", [P, 2, SEQ], F32R)
        QB = sb(s1, "QB", [HD + AUG, 2, SEQ], F32R)
        VS = sb(s1, "VS", [P, PAGES, 2, P], F32R)
        Pb = sb(s1, "Pb", [P, P_OFF[-1]])
        pTh = sb(s1, "pTh", [P, 2, 512], F32R)
        pTl = sb(s1, "pTl", [P, 2, 512], F32R)
        stK = sb(s1, "stageK", [P, TT])
        stQ = sb(s1, "stageQ", [P, TT])
        zf = sb(s1, "zf", [P, TT])
        yT = sb(s1, "yT", [P, TT])
        KN = sb(s1, "KN", [P, 9, P])
        s1.close()
        s0 = ExitStack()
        fl = sb(s0, "fl", [H, TT])
        fe = sb(s0, "fe", [H, TT])
        fu = sb(s0, "fu", [H, TT])
        fm = sb(s0, "fm", [H, TT])
        lfT = sb(s0, "lfT", [H, TT])
        one16 = sb(s0, "one16", [H, SEQ])
        ch = sb(s0, "ch", [H, 5, SEQ], F32R)
        RTs = sb(s0, "RT_first", [P, 2, KEYS + NS], F32R)
        lf8 = sb(s0, "lf8", [NS, DB, H])
        s0.close()
        sh.close()

        s2 = ExitStack()
        Kr = sb(s2, "Kpages", [P, PAGES, D])
        RT = sb(s2, "RT", [P, 2, KEYS + NS], F32R)
        KT = sb(s2, "KT", [P, 2, NPAIR, 2 * PAGE])
        pick = sb(s2, "pick", [P, NPAIR, 32], F32R)
        qc = sb(s2, "qc", [P, NPAIR, 32])
        cq = sb(s2, "cq", [NS, NPAIR, 32])
        cqh = sb(s2, "cqh", [NS, NPAIR, 32], F32R)
        cql = sb(s2, "cql", [NS, NPAIR, 32], F32R)
        mq = sb(s2, "mq", [NS, 4, 32], BF16)
        onesr = sb(s2, "onesr", [NS, 512], F32R)
        Vb = sb(s2, "Vpages", [P, PAGES, D])
        Ps = sb(s2, "Ps", [P, 2, KEYS + NS])
        PsT = sb(s2, "PsT", [P, 2, 9, P])
        Osb = sb(s2, "Osb", [P, 2, P])
        s2.close()

        PS = es.enter_context(nc.psum_tensor("PS", [P, 8, 512], F32))
        flat = PS[:, :, :].rearrange("p b n -> p (b n)")
        S = flat[:, 3 * 512:6 * 512]

        uc_rows = Y[0:18, 6, 0:D]

        def y_rows(tt):
            return Y[:, tt, 0:D] if tt < 8 else sU[0:NS, 0:D]

        def score_bank(qb):
            return PS[:, 3 + qb % 2, :] if qb < 4 else S

        names = (
            "const_ready sp_step in_rows in_bf in_x0 in_x1 in_x2 w_in0 w_in1 w_gained w_hi w_split block_done act_evac dve_evac "
            "h_hi h_ready g_turned g_ready x_turned x_first x_act x_dve x_sum x_parked x_back y_back y_merged out_dma "
            "uc_turned uc_act uc_out f_raw f_abs f_ln f_lf f_turned f_nat f_aug f_augdma "
            "staged kv_turned kv_nat kv_out kq_hi kq_lo v_hi v_lo z_done "
            "score rowmax exp rinv p_begun p_norm turned p_hi p_lo pv o_up o_free o_done y_out "
            "s_table s_logf s_rest s_lf8 s_cn s_restsb s_restout s_restin qd_zero s_prep s_kturn s_kt0 s_kt1 s_score "
            "s_all s_max s_exp s_back s_pt0 s_pt1 s_pv s_osb s_yturn s_out aug_in0 aug_in1 "
            "y_norm y_turned y_act y_dve y_dma y_sq y_root y_inv").split()
        names += [f"{k}{i}" for i in range(PAGES) for k in ("k_in", "v_in")]
        names += [f"n{r}_{k}" for r in range(2) for k in ("sq", "acc", "ps", "rt", "inv", "even", "odd")] + ["n2_sq", "n2_acc"]
        names += [f"ple{r}_{k}" for r in range(2) for k in ("in", "turned", "hi", "lo")]
        sems = {k: sem(k) for k in names}

        def loaded(n0, per=2, i=0):
            return 32 * (n0 // 2 + 1) + 16 * per * i

        block = es.enter_context(nc.Block())

        wv = lambda w: w.rearrange("(k p) n -> p k n", p=P)
        row = lambda w: w.rearrange("(a n) -> a n", a=1)
        w_in_a, w_out_a = wv(a["w_in_a"][0]), wv(a["w_out_a"][0])
        w_kv, w_in_b, w_out_b = wv(a["w_kv"]), wv(a["w_in_b"][0]), wv(a["w_out_b"][0])
        w_gate = [wv(a["w_ple_gate"][i]) for i in range(2)]
        w_proj = [wv(a["w_ple_proj"][i]) for i in range(2)]
        x_p = a["x_prompt"][0].rearrange("(t p) c -> p t c", p=P)
        x_s = a["x_sample"].rearrange("b t c -> (b t) c")
        p_p = [a["p_prompt"][i, 0].rearrange("(t p) c -> p t c", p=P) for i in range(2)]
        p_s = [a["p_sample"][i].rearrange("b t c -> (b t) c") for i in range(2)]
        ck = a["cache_k"].rearrange("n s h d -> (n s) (h d)")
        cv = a["cache_v"].rearrange("n s h d -> (n s) (h d)")
        cl = a["cache_logf"].rearrange("n s h -> (n s) h")
        last_page = a["cache_k"].shape[0] - 1
        o_yp = o["y_prompt"][0].rearrange("(t p) c -> p t c", p=P)
        o_ys = o["y_sample"].rearrange("b t c -> (b t) c")
        o_kv = [(o[f"{x}_prompt"][0].rearrange("(t p) h d -> p t (h d)", p=P),
                 o[f"{x}_sample"].rearrange("b t h d -> (b t) (h d)")) for x in "kv"]
        A1_COLS = [D, 2 * D, 3 * D, 0]

        def peeled(eng, n, body):
            with eng.Fori(0, n - 1) as i:
                body(i, False)
            body(n - 1, True)

        def at_pair(t, j):
            return t[:, bass.ds(j, 1)]

        @block.sync
        def _(sp):
            for k, n in LEAD["sync"].items():
                sp.sem_inc(sems[k], n)
            for src, r, n in ((a["norm_a"][0:1, :], G_A, 1), (row(a["norm_kv"]), G_KV, 1),
                              (a["norm_b"][0:1, :], G_B, 1), (row(a["norm_f"]), G_F, 1),
                              (a["conv_w_a"][0], G_CW, CW), (a["state_conv"][0].rearrange("b w c -> (b w) c"), G_ST, 16),
                              (row(a["norm_f"]), G_N - 1, 1)):
                sp.dma_start(sZ[r:r + n, 0:D], src).then_inc(sems["in_rows"], 16)
            sp.dma_start(Y[:, 0:4, 0:D], x_p[:, 0:4, :]).then_inc(sems["in_x0"], 16)
            sp.dma_start(Y[:, 4:8, 0:D], x_p[:, 4:8, :]).then_inc(sems["in_x1"], 16)
            sp.dma_start(sA[0:NS, 0:D], x_s).then_inc(sems["in_x2"], 16)
            with nc.allow_non_contiguous_dma(reason="16 values, one per partition"):
                sp.dma_start(bf_col[:, :], a["b_f"].rearrange("(n a) -> n a", a=1)).then_inc(sems["in_bf"], 16)
            sp.dma_start(pt[:, :], a["page_table"].rearrange("b (a n) -> a b n", a=1)).then_inc(sems["s_table"], 16)
            sp.wait_ge(sems["s_table"], 16)

            def page(b, pg):
                v = sp.value_load(pt[0:1, bass.ds(PAGES * b + pg, 1)], min_val=0, max_val=last_page)
                return bass.ds(v * PAGE, PAGE)

            def load(n, par, src, proj=None, cols=P):
                sp.wait_ge(sems["w_split"], START["w_split"] + n - 1)
                sp.sem_inc(sems["sp_step"], 1)
                if proj is None:
                    for c in (0, 4):
                        sp.dma_start(raw[:, par, c:c + 4, 0:cols], src[:, c:c + 4, :]).then_inc(sems[f"w_in{par}"], 16)
                else:
                    sp.dma_start(raw[:, par, 0:KC, :], src).then_inc(sems[f"w_in{par}"], 16)
                    sp.dma_start(raw[:, par, KC:, :], proj).then_inc(sems[f"w_in{par}"], 16)

            def load_out(n0, w, first=0):
                with sp.Fori(first, KC // 2) as i:
                    for u in range(2):
                        load(n0 + 2 * i + u, (n0 + u) % 2, w[:, :, bass.ds(2 * P * i + P * u, P)])

            def load_feed(n0, r):
                for dst, src in ((sA[:, 0:D], p_p[r][:, 0:4, :]), (sZ[:, 0:D], p_p[r][:, 4:8, :])):
                    sp.dma_start(dst.rearrange("p (t c) -> p t c", c=PLE), src).then_inc(sems[f"ple{r}_in"], 16)
                sp.dma_start(sU[0:NS, 0:PLE], p_s[r]).then_inc(sems[f"ple{r}_in"], 16)
                with sp.Fori(0, KC // 2) as i:
                    for u in range(2):
                        c = bass.ds(2 * P * i + P * u, P)
                        load(n0 + 2 * i + u, (n0 + u) % 2, w_gate[r][:, :, c], w_proj[r][:, :, c])

            with sp.Fori(0, KC) as j:
                for t in range(4):
                    load(4 * j + t, t % 2, w_in_a[:, :, bass.ds(A1_COLS[t] + P * j, P)])
                    with nc.allow_non_contiguous_dma(reason="16 log forget values per row"):
                        for pg in (2 * t, 2 * t + 1):
                            sp.dma_start(at_pair(LFP[:, pg], j).rearrange("p b h -> p (b h)"), cl[page(j, pg), :]).then_inc(sems["s_logf"], 16)
            load_out(N_A2, w_out_a)
            sp.wait_ge(sems["dve_evac"], START["dve_evac"] + ED_A2)
            load_feed(N_A3, 0)
            sp.wait_ge(sems["uc_act"], 2)
            sp.dma_start(o["conv_prompt"][0, 0], uc_rows[0:2, :]).then_inc(sems["uc_out"], 16)
            sp.dma_start(o["conv_sample"][0].rearrange("b w c -> (b w) c"), uc_rows[2:18, :]).then_inc(sems["uc_out"], 16)
            with nc.allow_non_contiguous_dma(reason="the last 16 columns of w_kv"):
                load(N_F, N_F % 2, w_kv[:, :, 2 * D:2 * D + H], cols=H)
            sp.wait_ge(sems["x_sum"], START["x_sum"] + 8)
            for k in range(KC):
                sp.dma_start(d["x"][k], X[:, k, :]).then_inc(sems["x_parked"], 16)
            load(N_B1, N_B1 % 2, w_kv[:, :, 0:P])
            sp.wait_ge(sems["f_nat"], 1)
            sp.dma_start(o["logf_prompt"][0].rearrange("(t p) h -> p t h", p=P), lfn[:, 0:8, :]).then_inc(sems["out_dma"], 16)
            sp.dma_start(o["logf_sample"].rearrange("b t h -> (b t) h"), lfn[0:NS, 8, :]).then_inc(sems["out_dma"], 16)
            sp.wait_ge(sems["f_aug"], 1)
            for r, (sk, sq_) in enumerate(((2, 4), (3, 4), (4, 0), (4, 1))):
                sp.dma_start(d["augk"][:, r, :], f(ch[:, sk, :])).then_inc(sems["f_augdma"], 16)
                sp.dma_start(d["augq"][:, r, :], f(ch[:, sq_, :])).then_inc(sems["f_augdma"], 16)
            sp.wait_ge(sems["f_augdma"], 128)

            def load_b1(j, t, back=0):
                w, c0 = ((w_kv, 0), (w_in_b, 0), (w_kv, D), (w_in_b, D))[t]
                n = N_B1 + 4 * (j + back) + t
                load(n, (N_B1 + t) % 2, w[:, :, bass.ds(c0 + P * (j + back), P)])

            def load_aug(j, hh):
                for dst, src in ((KB, d["augk"]), (QB, d["augq"])):
                    sp.dma_start(f(dst[HD:, hh, :]), src[bass.ds(2 * j + hh, 1)].rearrange("a r n -> (a r) n")).then_inc(sems[f"aug_in{hh}"], 16)

            def store_kv(j, t):
                sp.wait_ge(sems["kv_nat"], 6 * j + 3 * t + 3)
                sp.sem_inc(sems["sp_step"], 1)
                o_p, o_s = o_kv[t]
                sp.dma_start(o_p[:, :, bass.ds(P * j, P)], KN[:, 0:8, :]).then_inc(sems["kv_out"], 16)
                sp.dma_start(o_s[:, bass.ds(P * j, P)], KN[0:NS, 8, :]).then_inc(sems["kv_out"], 16)

            def half0(j, more):
                if more:
                    load_b1(j, 0, 1)
                store_kv(j, 1)
                if more:
                    load_b1(j, 1, 1)
                    load_b1(j, 2, 1)
                    sp.wait_ge(sems["score"], START["score"] + 16 * j + 8)
                    sp.sem_inc(sems["sp_step"], 1)
                    load_aug(j + 1, 0)
                    load_b1(j, 3, 1)

            def half1(j, more):
                if more:
                    store_kv(j + 1, 0)
                    sp.wait_ge(sems["score"], START["score"] + 16 * j + 16)
                    sp.sem_inc(sems["sp_step"], 1)
                    load_aug(j + 1, 1)
                if not more:
                    sp.wait_ge(sems["block_done"], START["block_done"] + B_B2)
                    for pg in range(PAGES):
                        sp.dma_start(Kr[:, pg, :], ck[page(0, pg), :]).then_inc(sems[f"k_in{pg}"], 16)
                    sp.dma_start(f(RT[:, :, :]), d["rest"]).then_inc(sems["s_restin"], 16)
                sp.wait_ge(sems["o_done"], START["o_done"] + 4 * j + 4)
                sp.sem_inc(sems["sp_step"], 1)
                sp.dma_start(d["y"][bass.ds(j, 1)].rearrange("a p n -> (a p) n"), yT[:, 0:SEQ]).then_inc(sems["y_out"], 16)

            load_b1(0, 1)
            sp.wait_ge(sems["s_restsb"], 1)
            sp.dma_start(d["rest"], f(RTs[:, :, :])).then_inc(sems["s_restout"], 16)
            sp.wait_ge(sems["s_restout"], 16)
            load_aug(0, 0)
            load_aug(0, 1)
            load_b1(0, 2)
            load_b1(0, 3)
            store_kv(0, 0)
            with sp.Fori(0, NPAIR - 1) as j:
                half0(j, True)
                half1(j, True)
            half0(NPAIR - 1, False)
            half1(NPAIR - 1, False)

            sp.wait_ge(sems["y_out"], START["y_out"] + 16 * NPAIR)
            sp.wait_ge(sems["kv_out"], START["kv_out"] + 64 * NPAIR)

            def value_pages(b):
                for pg in range(PAGES):
                    rows = page(b, pg)
                    if pg == 0:
                        sp.wait_ge(sems["s_pv"], START["s_pv"] + b)
                        sp.sem_inc(sems["sp_step"], 1)
                    sp.dma_start(Vb[:, pg, :], cv[rows, :]).then_inc(sems[f"v_in{pg}"], 16)

            with sp.Fori(0, DB - 1) as b:
                value_pages(b)
                for pg in range(PAGES):
                    rows = page(b + 1, pg)
                    sp.wait_ge(sems["s_kturn"], 16 * b + 2 * pg + 2)
                    sp.sem_inc(sems["sp_step"], 1)
                    sp.dma_start(Kr[:, pg, :], ck[rows, :]).then_inc(sems[f"k_in{pg}"], 16)
            for u in range(2):
                load(N_B2 + u, (N_B2 + u) % 2, w_out_b[:, :, P * u:P * u + P])
            value_pages(DB - 1)
            for k in range(KC):
                sp.dma_start(Y[:, k, 0:SEQ], d["y"][k]).then_inc(sems["y_back"], 16)

            sp.wait_ge(sems["s_out"], START["s_out"] + DB)
            for k in range(KC):
                sp.dma_start(X[:, k, :], d["x"][k]).then_inc(sems["x_back"], 16)
            load_out(N_B2, w_out_b, 1)
            load_feed(N_B3, 1)
            for tt in range(9):
                sp.wait_ge(sems["y_act"], tt + 1)
                sp.wait_ge(sems["y_dve"], tt + 1)
                sp.dma_start(o_yp[:, tt, :] if tt < 8 else o_ys, y_rows(tt)).then_inc(sems["y_dma"], 16)
            sp.wait_ge(sems["y_dma"], 16 * 9)
            sp.wait_ge(sems["out_dma"], 32)
            sp.wait_ge(sems["uc_out"], 32)

        @block.gpsimd
        def _(g):
            g.memset(ones[:, :], 1.0)
            g.memset(ident[:, :], 0.0)
            g.memset(tri[:, :], 0.0)
            g.memset(maskb[:, :], 0.0)
            g.memset(same[:, :], 1.0)
            g.memset(maskQ[:, :], 0.0)
            g.memset(small[:, 31:32], EPS)
            g.drain()
            g.affine_select(out=ident[:, :], in_=ident[:, :], compare_op=ALU.not_equal, fill=1.0, base=0,
                            pattern=[[-1, P]], channel_multiplier=1)
            g.affine_select(out=tri[:, :], in_=tri[:, :], compare_op=ALU.is_ge, fill=1.0, base=0,
                            pattern=[[1, P]], channel_multiplier=-1)
            g.affine_select(out=maskb[:, :], in_=maskb[:, :], compare_op=ALU.is_ge, fill=NEG, base=0,
                            pattern=[[-1, P]], channel_multiplier=1)
            g.affine_select(out=same[:, :], in_=same[:, :], compare_op=ALU.is_ge, fill=0.0, base=0,
                            pattern=[[1, NS]], channel_multiplier=-1)
            g.affine_select(out=maskQ[:, :], in_=maskQ[:, :], compare_op=ALU.is_ge, fill=NEG, base=0,
                            pattern=[[-1, NS]], channel_multiplier=1)
            g.drain()
            v = same[:, :].rearrange("p (b t) -> p b t", b=DB)
            g.affine_select(out=v, in_=v, compare_op=ALU.is_ge, fill=0.0, base=0,
                            pattern=[[-DS, DB], [0, DS]], channel_multiplier=1)
            v = maskQ[:, :].rearrange("p (b t) -> p b t", b=DB)
            g.affine_select(out=v, in_=v, compare_op=ALU.is_ge, fill=NEG, base=DS - 1,
                            pattern=[[DS, DB], [0, DS]], channel_multiplier=-1)
            g.tensor_copy(identb[:, :], ident[:, :])
            g.drain().then_inc(sems["const_ready"], 1)

            def gain(par, r, count, done=None):
                g.wait_ge(sems[f"w_in{par}"], count)
                w = raw[:, par, 0:KC, :]
                g.tensor_tensor(w, w, GT[:, :, r:r + 1].to_broadcast([P, KC, P]), ALU.mult).then_inc(sems["w_gained"], 1)
            def norm_odd(r, h0):
                g.wait_ge(sems[f"n{r}_inv"], 1)
                for k in range(1, KC, 2):
                    if k > 1:
                        g.wait_ge(sems["h_ready"], h0 + k - 1)
                    g.tensor_tensor(sq[r][1], X[:, k, :], rs[:, :], ALU.mult).then_inc(sems[f"n{r}_odd"], 1)

            g.wait_ge(sems["g_ready"], 1)
            gain(0, G_A, loaded(0))
            norm_odd(0, 0)
            for t in range(1, 4):
                gain(t % 2, G_A, loaded(t))
            with g.Fori(1, KC) as j:
                for t in range(4):
                    gain(t % 2, G_A, loaded(t, 4, j))
            gain(N_F % 2, G_KV, loaded(N_F))
            norm_odd(1, 24)
            def gain_b1(j, t, back=0):
                gain((N_B1 + t) % 2, (G_KV, G_B, G_KV, G_B)[t], loaded(N_B1 + 4 * back + t, 4, j))

            def normalise(c, j):
                qb = c % 8
                g.wait_ge(sems["rinv"], 16 * j + c + 1)
                g.sem_inc(sems["p_begun"], 1)
                pb = Pb[:, P_OFF[qb]:P_OFF[qb + 1]]
                g.tensor_scalar(pb, pb, small[:, 16 + qb:17 + qb], 1.0, ALU.mult, ALU.mult).then_inc(sems["p_norm"], 1)

            def iteration(j, more):
                for hh in range(2):
                    if more and hh == 0:
                        gain_b1(j, 0, 1)
                    for qb in range(4):
                        normalise(8 * hh + qb, j)
                    if more:
                        gain_b1(j, (1, 3)[hh], 1)
                    for qb in range(4, 8):
                        normalise(8 * hh + qb, j)
                    if more and hh == 0:
                        gain_b1(j, 2, 1)

            gain_b1(0, 0)
            g.wait_ge(sems["s_rest"], 1)
            g.memset(qd[:, :, :, :].rearrange("p a b c -> p (a b c)"), 0.0).then_inc(sems["qd_zero"], 1)
            for t in range(1, 4):
                gain_b1(0, t)
            with g.Fori(0, NPAIR - 1) as j:
                iteration(j, True)
            iteration(NPAIR - 1, False)
            for k in range(KC):
                g.wait_ge(sems["n2_sq"], k + 1)
                g.tensor_scalar(X[:, k, :], X[:, k, :], GT[:, k, G_F:G_F + 1], 1.0, ALU.mult, ALU.mult).then_inc(sems["y_norm"], 1)

        @block.tensor
        def _(pe):
            for k, n in LEAD["tensor"].items():
                pe.sem_inc(sems[k], n)
            mm, tp = pe.matmul, pe.transpose

            def tile(n, par, bank, free, hr=None, k0=0, nk=KC, hi=Hhi, lo=Hlo):
                pe.wait_ge(sems["w_split"], START["w_split"] + n + 1)
                def products(b, k):
                    s, e = BLK[b]
                    out = PS[:, bank + b, 0:e - s]
                    wh, wl = whi[:, par, k0 + k, :], wlo[:, par, k0 + k, :]
                    mm(out, wh, hi[:, k, s:e], start=(k == 0), stop=False)
                    mm(out, wh, lo[:, k, s:e], start=False, stop=False)
                    last = mm(out, wl, hi[:, k, s:e], start=False, stop=(k == nk - 1))
                    if k == nk - 1:
                        last.then_inc(sems["block_done"], 1)
                if hr is not None:
                    for k in range(nk):
                        pe.wait_ge(sems["h_ready"], hr + k + 1)
                        for b in range(NB):
                            if k == 0:
                                free(b)
                            products(b, k)
                else:
                    for b in range(NB):
                        free(b)
                        for k in range(nk):
                            products(b, k)

            pe.wait_ge(sems["const_ready"], 1)
            pe.wait_ge(sems["in_rows"], 112)
            for k in range(KC):
                last = tp(PS[:, 7, k * G_N:(k + 1) * G_N], sZ[0:G_N, k * P:(k + 1) * P], ident[0:G_N, 0:G_N])
            last.then_inc(sems["g_turned"], 1)
            pe.wait_ge(sems["in_x0"], 16)
            for k in range(KC):
                if k >= 2:
                    pe.wait_ge(sems["x_first"], k - 1)
                for i in range(4):
                    last = tp(PS[:, 3 * (k % 2), i * P:(i + 1) * P], Y[:, i, k * P:(k + 1) * P], ident[:, :])
                last.then_inc(sems["x_turned"], 1)
            pe.wait_ge(sems["in_x1"], 16)
            pe.wait_ge(sems["in_x2"], 16)
            for k in range(KC):
                if k >= 2:
                    pe.wait_ge(sems["x_act"], k - 1)
                for i in range(4):
                    last = tp(PS[:, 1 + 3 * (k % 2), i * P:(i + 1) * P], Y[:, 4 + i, k * P:(k + 1) * P], ident[:, :])
                last.then_inc(sems["x_turned"], 1)
                if k >= 2:
                    pe.wait_ge(sems["x_dve"], k - 1)
                tp(PS[:, 2 + 3 * (k % 2), 0:NS], sA[0:NS, k * P:(k + 1) * P], ident[0:NS, 0:NS]).then_inc(sems["x_turned"], 1)

            def norm_sum(r):
                pe.wait_ge(sems[f"n{r}_acc"], START[f"n{r}_acc"] + KC)
                for b, (s, e) in enumerate(BLK):
                    mm(PS[:, 3 + b, 0:e - s], ones[:, :], ss[:, s:e], start=True, stop=True).then_inc(sems[f"n{r}_ps"], 1)
            norm_sum(0)

            with pe.Fori(0, KC) as j:
                for t in range(4):
                    free = [lambda b: pe.wait_ge(sems["dve_evac"], START["dve_evac"] + 6 * j - 3 + b + 1), lambda b: pe.wait_ge(sems["act_evac"], 6 * j + b + 1),
                            lambda b: pe.wait_ge(sems["dve_evac"], START["dve_evac"] + 6 * j + b + 1), lambda b: pe.wait_ge(sems["act_evac"], 6 * j + 3 + b + 1)][t]
                    tile(4 * j + t, t % 2, 0, free, hr=0 if t == 0 else None)

            def out_tiles(n0, ed0, hr):
                with pe.Fori(0, KC // 2) as i:
                    for u in range(2):
                        tile(n0 + 2 * i + u, (n0 + u) % 2, 0,
                             lambda b: pe.wait_ge(sems["dve_evac"], START["dve_evac"] + ed0 + 6 * i + 3 * u - 3 + b + 1), hr=hr if u == 0 else None)

            def feed(r, n0, ea0, ed0, hr):
                pe.wait_ge(sems[f"ple{r}_in"], 48)
                for c in range(PC):
                    for h_, src in enumerate((sA, sZ, sU)):
                        if c:
                            pe.wait_ge(sems[f"ple{r}_lo"], h_ + 1)
                        if h_ < 2:
                            for i in range(4):
                                last = tp(PS[:, 3 + h_, i * P:(i + 1) * P], src[:, i * PLE + c * P:i * PLE + (c + 1) * P], ident[:, :])
                        else:
                            last = tp(PS[:, 5, 0:NS], src[0:NS, c * P:(c + 1) * P], ident[0:NS, 0:NS])
                        last.then_inc(sems[f"ple{r}_turned"], 1)
                pe.wait_ge(sems[f"ple{r}_lo"], 6)
                pe.wait_ge(sems["dve_evac"], START["dve_evac"] + ed0)
                with pe.Fori(0, KC // 2) as i:
                    for u in range(2):
                        n, par = n0 + 2 * i + u, (n0 + u) % 2
                        tile(n, par, 0, lambda b: pe.wait_ge(sems["act_evac"], ea0 + 6 * i + 3 * u - 3 + b + 1), hr=hr if u == 0 else None)
                        tile(n, par, 3, lambda b: pe.wait_ge(sems["dve_evac"], START["dve_evac"] + ed0 + 6 * i + 3 * u - 3 + b + 1),
                             k0=KC, nk=PC, hi=PTh, lo=PTl)

            out_tiles(N_A2, ED_A2, 8)
            for c in range(2):
                for i in range(4):
                    last = tp(PS[0:18, 6 + c, i * P:(i + 1) * P], uc[:, 4 * c + i, :], ident[:, :])
                last.then_inc(sems["uc_turned"], 1)
            feed(0, N_A3, EA_A3, ED_A3, 16)
            norm_sum(1)
            pe.wait_ge(sems["act_evac"], EA_F)
            tile(N_F, N_F % 2, 0, lambda b: None, hr=24)
            pe.wait_ge(sems["s_logf"], 16 * DB * PAGES)
            for pg in range(PAGES):
                for x in range(pg, PAGES):
                    last = mm(S[:, pg * P:(pg + 1) * P], LFP[:, x, :, :].rearrange("p b h -> p (b h)"),
                              (tri if x == pg else ones)[:, :], start=(x == pg), stop=(x == PAGES - 1))
            last.then_inc(sems["s_rest"], 1)
            pe.wait_ge(sems["f_lf"], 1)
            for t in range(9):
                n = P if t < 8 else NS
                last = tp(PS[0:n, 6, t * H:(t + 1) * H], lfT[:, t * P:t * P + n], ident[0:H, 0:H])
            last.then_inc(sems["f_turned"], 1)
            pe.wait_ge(sems["s_lf8"], 1)
            mm(PS[:, 5, 0:NS], lf8[:, :, :].rearrange("p b h -> p (b h)"), same[:, :], start=True, stop=True)
            mm(PS[0:NS, 5, P:P + H], same[:, :], lfn[0:NS, 8, :], start=True, stop=True).then_inc(sems["s_cn"], 1)

            def dense_piece(j, half, p):
                i, b, k = 2 * half + p // 24, p % 24 // KC, p % KC
                g_ = 4 * j + 3 + i
                par = (N_B1 + 3 + i) % 2
                if p % 24 == 0:
                    pe.wait_ge(sems["w_split"], START["w_split"] + N_B1 + g_ + 1)
                if k == 0:
                    pe.wait_ge(sems["act_evac"], EA_B1 + 3 * g_ - 3 + b + 1)
                s, e = BLK[b]
                out = PS[:, b, 0:e - s]
                wh, wl = whi[:, par, k, :], wlo[:, par, k, :]
                mm(out, wh, Hhi[:, k, s:e], start=(k == 0), stop=False)
                mm(out, wh, Hlo[:, k, s:e], start=False, stop=False)
                last = mm(out, wl, Hhi[:, k, s:e], start=False, stop=(k == KC - 1))
                if k == KC - 1:
                    last.then_inc(sems["block_done"], 1)

            def turn_part(j, t, i):
                if i == 0:
                    pe.wait_ge(sems["staged"], 3 * j + (1, 3)[t])
                if i == 2:
                    pe.wait_ge(sems["kv_nat"], 6 * j + 3 * t + 1)
                src = (stK, stQ)[t]
                for y, x in enumerate(TURN_PARTS[i]):
                    n = P if x < 8 else NS
                    last = tp(PS[0:n, 5 + i % 2, y * P:(y + 1) * P], src[:, x * P:x * P + n], ident[:, :])
                last.then_inc(sems["kv_turned"], 1)

            def scores(j, hh, qb):
                c = 8 * hh + qb
                n = (qb + 1) * P
                pe.wait_ge(sems["exp"], START["exp"] + 16 * j + c - (1 if 0 < qb < 4 else 0))
                if qb == 0:
                    pe.wait_ge(sems["kq_lo"], 3 * j + 2 + hh)
                    pe.wait_ge(sems[f"aug_in{hh}"], 32 * j + 32)
                q = slice(qb * P, (qb + 1) * P)
                out = score_bank(qb)
                for c0 in range(0, n, 512):
                    w = min(512, n - c0)
                    mm(out[:, c0:c0 + w], QA[:, hh, q], KA[:, hh, c0:c0 + w], start=True, stop=False)
                    mm(out[:, c0:c0 + w], QB[:, hh, q], KB[:, hh, c0:c0 + w], start=False, stop=(c0 + 512 < n))
                mm(out[:, qb * P:n], identb[:, :], maskb[:, :], start=False, stop=True).then_inc(sems["score"], 1)

            def turn_p(j, hh, grp, kb, more):
                u = 12 * hh + 4 * grp + kb
                q0 = max(0, kb - QG * grp)
                if kb == 0:
                    pe.wait_ge(sems["p_norm"], 16 * j + 8 * hh + QG * (grp + 1))
                if grp == 0 and kb == 0 and (hh == 0 or more):
                    pe.wait_ge(sems["kv_nat"], 6 * j + 6 + 3 * hh)
                pe.wait_ge(sems["p_lo"], START["p_lo"] + 24 * j + u - 1)
                for qi in range(q0, QG):
                    off = P_OFF[QG * grp + qi] + kb * P
                    last = tp(PS[:, 5 + kb % 2, qi * P:(qi + 1) * P], Pb[:, off:off + P], ident[:, :])
                last.then_inc(sems["turned"], 1)

            def pv_step(j, hh, grp, kb):
                u = 12 * hh + 4 * grp + kb
                q0 = max(0, kb - QG * grp)
                nkb = QG * (grp + 1)
                if kb == 0:
                    pe.wait_ge(sems["o_free"], START["o_free"] + 4 * j + 2 * hh + grp)
                    pe.wait_ge(sems["v_lo"], j + 1)
                pe.wait_ge(sems["p_lo"], START["p_lo"] + 24 * j + u + 1)
                for x in (pTh, pTl):
                    last = mm(PS[:, 7, q0 * P:512], VS[:, kb, hh, :], x[:, kb % 2, q0 * P:512],
                              start=(kb == 0 and x is pTh), stop=(kb == nkb - 1 and x is pTl))
                last.then_inc(sems["pv"], 1)

            def half_pair(j, half, more):
                p = 0
                for step in STEPS:
                    if step[0] == "S":
                        scores(j, half, step[1])
                    if step[0] == "T":
                        turn_p(j, half, step[1], step[2], more)
                    if step[0] == "V":
                        pv_step(j, half, step[1], step[2])
                    if step[0] == "N" and (half == 0 or more):
                        turn_part(j + half, 1 - half, step[1])
                    if step[0] == "D":
                        for _ in range(step[1]):
                            if more or PIECES * half + p < 24:
                                dense_piece(j, half, p)
                            p += 1

            for p in range(24, PIECES):
                dense_piece(-1, 0, p)
            for p in range(PIECES):
                dense_piece(-1, 1, p)
                if p == 8:
                    for i in range(3):
                        turn_part(0, 0, i)
            with pe.Fori(0, NPAIR - 1) as j:
                half_pair(j, 0, True)
                half_pair(j, 1, True)
            half_pair(NPAIR - 1, 0, False)
            half_pair(NPAIR - 1, 1, False)

            pe.wait_ge(sems["act_evac"], EA_B2)
            pe.wait_ge(sems["exp"], START["exp"] + 16 * NPAIR)
            pe.wait_ge(sems["p_lo"], START["p_lo"] + 24 * NPAIR)
            pe.wait_ge(sems["o_done"], START["o_done"] + 4 * NPAIR)

            def k_turn(b, pg):
                pe.wait_ge(sems[f"k_in{pg}"], 16 * b + 16)
                for c in range(2):
                    pe.wait_ge(sems[f"s_kt{c}"], 1 + PAGES * b + pg)
                    for i in range(4 * c, 4 * c + 4):
                        last = tp(PS[:, c, (i % 4) * P:(i % 4 + 1) * P], Kr[:, pg, i * P:(i + 1) * P], ident[:, :])
                    last.then_inc(sems["s_kturn"], 1)

            def s_bank(s_, c):
                return PS[:, 2 + 2 * s_ + c, :]

            def s_bias(b, out, s_, c0, n):
                rows = slice(4 * s_, 4 * s_ + 4)
                w = lambda x: x[:, rows, :].rearrange("p i n -> p (i n)")
                mm(out, w(pick), RT[:, 0, c0:c0 + n], start=True, stop=False)
                mm(out, w(pick), RT[:, 1, c0:c0 + n], start=False, stop=False)
                mm(out, w(cqh), onesr[:, 0:n], start=False, stop=False)
                mm(out, w(cql), onesr[:, 0:n], start=False, stop=False)

            def s_scores(b, pp, pairs=range(NPAIR)):
                for c in range(2):
                    pe.wait_ge(sems[f"s_kt{c}"], 1 + PAGES * b + 2 * pp + 2)
                for i in pairs:
                    r = 32 * (i % 4)
                    last = mm(s_bank(i // 4, pp // 2)[r:r + 32, 256 * (pp % 2):256 * (pp % 2) + 256], qc[:, i, :],
                              KT[:, pp % 2, i, :], start=False, stop=(pp % 2 == 1))
                if pairs[-1] == NPAIR - 1:
                    last.then_inc(sems["s_score"], 1)

            def s_new(b):
                pe.wait_ge(sems["s_osb"], START["s_osb"] + b)
                for s_ in range(2):
                    out = PS[:, 6, NS * s_:NS * s_ + NS]
                    s_bias(b, out, s_, KEYS, NS)
                    mm(out, mq[:, :, :].rearrange("p g n -> p (g n)"), maskQ[:, :], start=False, stop=False)
                    for i in range(4 * s_, 4 * s_ + 4):
                        r = 32 * (i % 4)
                        last = mm(PS[r:r + 32, 6, NS * s_:NS * s_ + NS], qc[:, i, :], knT[:, i, :], start=False, stop=True)
                last.then_inc(sems["s_all"], 1)

            def s_p_turn(b):
                for r, (bank, s_, k0) in enumerate(P_ROUNDS):
                    if r in (0, 2):
                        pe.wait_ge(sems["s_exp"], START["s_exp"] + 2 * b + 1 + r // 2)
                    if bank == 7:
                        pe.wait_ge(sems["s_out"], START["s_out"] + b)
                    if k0 == PAGES:
                        for x in range(2):
                            last = tp(PS[0:NS, bank, x * P:(x + 1) * P], Ps[:, x, KEYS:], ident[:, :])
                    else:
                        for x in range(4):
                            last = tp(PS[:, bank, x * P:(x + 1) * P], Ps[:, s_, (k0 + x) * P:(k0 + x + 1) * P], ident[:, :])
                    last.then_inc(sems["s_back"], 1)

            def s_values(b):
                for s_ in range(2):
                    pe.wait_ge(sems["s_pt0"], START["s_pt0"] + 3 * b + 1 + s_)
                    pe.wait_ge(sems["s_pt1"], START["s_pt1"] + 2 * b + 1 + s_)
                    for pg in range(PAGES + 1):
                        if s_ == 0 and pg == PAGES - 1:
                            pe.wait_ge(sems["s_pt0"], START["s_pt0"] + 3 * b + 3)
                        if s_ == 0 and pg < PAGES:
                            pe.wait_ge(sems[f"v_in{pg}"], 16 * b + 16)
                        for g_ in range(4):
                            i = 4 * s_ + g_
                            k, v = (P, Vb[:, pg, i * P:(i + 1) * P]) if pg < PAGES else (NS, vnew[:, i * P:(i + 1) * P])
                            last = mm(PS[32 * g_:32 * g_ + 32, 6, P * (1 + s_):P * (2 + s_)],
                                      PsT[0:k, s_, pg, 32 * g_:32 * g_ + 32], v, start=(pg == 0), stop=(pg == PAGES))
                last.then_inc(sems["s_pv"], 1)

            def s_y_turn(b):
                pe.wait_ge(sems["s_osb"], START["s_osb"] + b + 1)
                pe.wait_ge(sems["s_pt1"], START["s_pt1"] + 2 * b + 2)
                for s_ in range(2):
                    last = tp(PS[:, 7, s_ * P:(s_ + 1) * P], Osb[:, s_, :], ident[:, :])
                last.then_inc(sems["s_yturn"], 1)

            def s_biases(b):
                pe.wait_ge(sems["s_prep"], b + 1)
                pe.wait_ge(sems["s_pt0"], START["s_pt0"] + 3 * b)
                pe.wait_ge(sems["s_pt1"], START["s_pt1"] + 2 * b)
                for s_ in range(2):
                    for c in range(2):
                        s_bias(b, s_bank(s_, c), s_, 512 * c, 512)

            def sample_batch(b, more):
                k_turn(b, 3)
                s_scores(b, 0)
                for pp in range(1, 3):
                    for x in range(2):
                        k_turn(b, 2 * pp + 2 + x)
                        s_scores(b, pp, range(4 * x, 4 * x + 4))
                s_scores(b, 3)
                s_new(b)
                if more:
                    k_turn(b + 1, 0)
                    k_turn(b + 1, 1)
                s_p_turn(b)
                s_values(b)
                if more:
                    k_turn(b + 1, 2)
                    s_biases(b + 1)
                s_y_turn(b)

            pe.wait_ge(sems["s_restin"], 16)
            for pg in range(3):
                k_turn(0, pg)
            s_biases(0)
            with pe.Fori(0, DB - 1) as b:
                sample_batch(b, True)
            sample_batch(DB - 1, False)

            out_tiles(N_B2, ED_B2, 32)
            feed(1, N_B3, EA_B3, ED_B3, 40)
            pe.wait_ge(sems["dve_evac"], START["dve_evac"] + ED_END)
            pe.wait_ge(sems["act_evac"], EA_END)
            pe.wait_ge(sems["n2_acc"], START["n2_acc"] + KC)
            for tt in range(9):
                n = P if tt < 8 else NS
                last = mm(PS[0:n, 7, tt:tt + 1], ss[:, tt * P:tt * P + n], ones[:, 0:1], start=True, stop=True)
            last.then_inc(sems["y_sq"], 1)
            pe.wait_ge(sems["y_norm"], KC)
            for tt in range(9):
                n = P if tt < 8 else NS
                for c in range(2):
                    if tt >= 2:
                        pe.wait_ge(sems[("y_act", "y_dve")[c]], tt - 1)
                    for i in range(4):
                        last = tp(PS[0:n, 2 * (tt % 2) + c, i * P:(i + 1) * P], X[:, 4 * c + i, tt * P:tt * P + n], ident[:, :])
                    last.then_inc(sems["y_turned"], 1)

        @block.scalar
        def _(act):
            for k, n in LEAD["scalar"].items():
                act.sem_inc(sems[k], n)
            af = act.activation

            def w_hi(par, blocks, count=None, gained=None, nk=KC):
                if gained is None:
                    act.wait_ge(sems[f"w_in{par}"], count)
                else:
                    act.wait_ge(sems["w_gained"], gained)
                act.wait_ge(sems["block_done"], START["block_done"] + blocks)
                af(whi[:, par, 0:nk, :], raw[:, par, 0:nk, :], ACT.Copy).then_inc(sems["w_hi"], 1)

            def square(r, k, par):
                act.wait_ge(sems[f"n{r}_acc"], START[f"n{r}_acc"] + k - 1)
                af(sq[r][par], at_pair(X, k).rearrange("p a n -> p (a n)"), ACT.Square).then_inc(sems[f"n{r}_sq"], 1)

            act.wait_ge(sems["const_ready"], 1)
            for k in range(KC + 1):
                if k < KC:
                    act.wait_ge(sems["x_turned"], KC + 2 * k + 1)
                    af(X[:, k, 512:SEQ], PS[:, 1 + 3 * (k % 2), :], ACT.Copy).then_inc(sems["x_act"], 1)
                    act.drain()
                if k:
                    act.wait_ge(sems["x_dve"], k)
                    square(0, k - 1, (k - 1) % 2)
            w_hi(0, -3, gained=1)

            def roots(r):
                for b, (s, e) in enumerate(BLK):
                    act.wait_ge(sems[f"n{r}_ps"], b + 1)
                    af(rs[:, s:e], PS[:, 3 + b, 0:e - s], ACT.Sqrt, scale=1.0 / D, bias=small[:, 31:32]).then_inc(sems[f"n{r}_rt"], 1)

            def normed_hi(r):
                for k in range(KC):
                    act.wait_ge(sems[f"n{r}_{('even', 'odd')[k % 2]}"], k // 2 + 1)
                    af(Hhi[:, k, :], sq[r][k % 2], ACT.Copy).then_inc(sems["h_hi"], 1)

            def split_hi(src):
                for k in range(KC):
                    af(Hhi[:, k, :], src[:, k, :], ACT.Copy).then_inc(sems["h_hi"], 1)

            roots(0)
            normed_hi(0)

            def conv_layer(j, last):
                for t in range(4):
                    act.drain()
                    if last and t == 3:
                        w_hi(N_A2 % 2, 3 * (N_A2 - 1), loaded(N_A2))
                    else:
                        w_hi((t + 1) % 2, 12 * j + 3 * t, gained=4 * j + t + 2)
                    if t in (0, 2):
                        act.wait_ge(sems["dve_evac"], START["dve_evac"] + 6 * j)
                        for b, (s, e) in enumerate(BLK):
                            act.wait_ge(sems["block_done"], START["block_done"] + 12 * j + 3 * t + b + 1)
                            if t == 0:
                                af(sA[:, s:e], PS[:, b, 0:e - s], ACT.Copy).then_inc(sems["act_evac"], 1)
                            else:
                                af(sZ[:, s:e], PS[:, b, 0:e - s], ACT.Silu).then_inc(sems["act_evac"], 1)
            peeled(act, KC, conv_layer)
            act.wait_ge(sems["dve_evac"], START["dve_evac"] + ED_A2)
            act.wait_ge(sems["block_done"], START["block_done"] + B_A2)
            split_hi(Y)

            def out_tiles(n0, b0):
                def body(i, last):
                    for u in range(2):
                        n = n0 + u + 1
                        if last and u == 1:
                            w_hi(n % 2, b0 + 21, loaded(n, 2, 3), nk=KC + PC)
                        else:
                            w_hi(n % 2, b0 + 6 * i + 3 * u, loaded(n, 2, i))
                peeled(act, KC // 2, body)

            def feed(r, n0, b0, ed0, next_hi):
                for g_ in range(6):
                    act.wait_ge(sems[f"ple{r}_turned"], g_ + 1)
                    c, h_ = divmod(g_, 3)
                    n = 512 if h_ < 2 else NS
                    af(PTh[:, c, h_ * 512:h_ * 512 + n], PS[:, 3 + h_, 0:n], ACT.Copy).then_inc(sems[f"ple{r}_hi"], 1)
                act.wait_ge(sems["dve_evac"], START["dve_evac"] + ed0)
                act.wait_ge(sems["block_done"], START["block_done"] + b0)
                split_hi(X)

                def body(i, last):
                    for u in range(2):
                        if last and u == 1:
                            if next_hi:
                                next_hi(b0 + 42)
                        else:
                            w_hi((n0 + u + 1) % 2, b0 + 12 * i + 6 * u, loaded(n0 + u + 1, 2, i), nk=KC + PC)
                        act.wait_ge(sems["x_sum"], START["x_sum"] + 8 * r + 2 * i + u - 1)
                        for b, (s, e) in enumerate(BLK):
                            act.wait_ge(sems["block_done"], START["block_done"] + b0 + 12 * i + 6 * u + b + 1)
                            af(sg[:, u, s:e], PS[:, b, 0:e - s], ACT.Sigmoid).then_inc(sems["act_evac"], 1)
                        act.wait_ge(sems["x_sum"], START["x_sum"] + 8 * r + 2 * i + u + 1)
                        square(r + 1, 2 * i + u, u)
                peeled(act, KC // 2, body)

            out_tiles(N_A2, B_A2)
            for c in range(2):
                act.wait_ge(sems["uc_turned"], c + 1)
                af(uc_rows[:, c * 512:(c + 1) * 512], PS[0:18, 6 + c, :], ACT.Copy).then_inc(sems["uc_act"], 1)
            act.drain()
            feed(0, N_A3, B_A3, ED_A3, lambda blocks: w_hi(N_F % 2, blocks, gained=33))
            act.drain()
            roots(1)
            act.wait_ge(sems["block_done"], START["block_done"] + B_F)
            normed_hi(1)

            act.wait_ge(sems["in_bf"], 16)
            act.wait_ge(sems["x_parked"], 16 * KC)
            for b, (s, e) in enumerate(BLK):
                act.wait_ge(sems["block_done"], START["block_done"] + B_F + b + 1)
                af(fl[:, s:e], PS[0:H, b, 0:e - s], ACT.Identity, bias=bf_col[:, 0:1]).then_inc(sems["act_evac"], 1)
            act.drain().then_inc(sems["f_raw"], 1)
            act.wait_ge(sems["f_abs"], 1)
            af(fe[:, :], fu[:, :], ACT.Exp)
            act.drain()
            af(fm[:, :], fe[:, :], ACT.Ln, bias=1.0).then_inc(sems["f_ln"], 1)
            w_hi(N_B1 % 2, B_F, gained=34)
            act.wait_ge(sems["f_turned"], 1)
            af(lfn[:, 0:8, :].rearrange("p t h -> p (t h)"), PS[:, 6, 0:8 * H], ACT.Copy)
            af(lfn[0:NS, 8, :], PS[0:NS, 6, 8 * H:9 * H], ACT.Copy)
            act.drain().then_inc(sems["f_nat"], 1)

            def exp_scores(j, hh, qb):
                n = (qb + 1) * P
                act.wait_ge(sems["rowmax"], 16 * j + 8 * hh + qb + 1)
                af(Pb[:, P_OFF[qb]:P_OFF[qb + 1]], score_bank(qb)[:, 0:n], ACT.Exp, bias=small[:, qb:qb + 1],
                   accum_out=small[:, 8 + qb:9 + qb]).then_inc(sems["exp"], 1)

            def p_hi(j, hh, grp, kb):
                u = 12 * hh + 4 * grp + kb
                q0 = max(0, kb - QG * grp)
                act.wait_ge(sems["turned"], START["turned"] + 24 * j + u + 1)
                act.wait_ge(sems["pv"], START["pv"] + 24 * j + u - 1)
                af(pTh[:, kb % 2, q0 * P:512], PS[:, 5 + kb % 2, q0 * P:512], ACT.Copy).then_inc(sems["p_hi"], 1)

            def o_up(j, hh, grp):
                act.wait_ge(sems["pv"], START["pv"] + 24 * j + 12 * hh + (4, 12)[grp])
                if hh == 0 and grp == 0:
                    act.wait_ge(sems["y_out"], START["y_out"] + 16 * j)
                hs = slice(64 * hh, 64 * hh + 64)
                af(yT[hs, 512 * grp:512 * grp + 512], PS[64:128, 7, :], ACT.Copy).then_inc(sems["o_up"], 1)

            def k_hi(hh, half):
                af(KA[64 * half:64 * half + 64, hh, :], stK[64 * hh:64 * hh + 64, 0:SEQ], ACT.Copy)

            def q_hi(hh, part):
                af(QB[0:HD, hh, :] if part else QA[64 * hh:64 * hh + 64, hh, :], stQ[64 * hh:64 * hh + 64, 0:SEQ], ACT.Copy)

            def evacuate(j, half, i, b, attend):
                g_ = 4 * j + 3 + i
                s, e = BLK[b]
                if i == 0 and b == 0:
                    act.wait_ge(sems["o_done"], START["o_done"] + 4 * j)
                if i == 1 and b == 0 and attend:
                    act.wait_ge(sems["kq_lo"], 3 * j + 3)
                if i == 2 and b == 0 and attend:
                    act.wait_ge(sems["kv_turned"], 6 * j + 6)
                if i == 3 and b == 0:
                    act.wait_ge(sems["kq_lo"], 3 * j + 6)
                act.wait_ge(sems["block_done"], START["block_done"] + B_B1 + 3 * g_ + b + 1)
                af((zf, stK, stQ, stQ)[i][:, s:e], PS[:, b, 0:e - s], ACT.Copy,
                   scale=SCALE if i == 2 else 1.0).then_inc(sems["act_evac"], 1)
                if b < NB - 1:
                    return
                if i == 0:
                    act.drain()
                    af(zf[:, :], zf[:, :], ACT.Silu).then_inc(sems["z_done"], 1)
                else:
                    act.drain().then_inc(sems["staged"], 1)
                if i == 2:
                    q_hi(0, 0)
                    q_hi(0, 1)
                    act.drain().then_inc(sems["kq_hi"], 1)

            leaves = [{7: (0, 0), 15: (0, 1), 23: (0, 2), 31: (1, 0), 39: (1, 1), 47: (1, 2)},
                      {7: (2, 0), 15: (2, 1), 23: (2, 2), 45: (3, 0), 46: (3, 1), 47: (3, 2)}]

            def beside(j, half, p, attend, more):
                i = 2 * half + p // 24
                if p % 24 == 16 and more:
                    w_hi((N_B1 + i) % 2, B_B1 + 3 * (4 * j + 3 + i), gained=32 + 4 * j + 3 + i + 3)
                if half == 0 and p == 4 and attend:
                    act.wait_ge(sems["kv_nat"], 6 * j + 6)
                    act.wait_ge(sems["pv"], START["pv"] + 24 * j)
                    af(VS[:, :, :, 0:HD], KN[:, 0:8, :].rearrange("p t (h n) -> p t h n", h=2), ACT.Copy).then_inc(sems["v_hi"], 1)
                if half == 1 and p in (7, 10) and more:
                    k_hi(0, (7, 10).index(p))
                if half == 1 and p == 28 and attend:
                    act.wait_ge(sems["score"], START["score"] + 16 * j + 16)
                if half == 1 and p in (28, 35) and more:
                    k_hi(1, (28, 35).index(p))
                if half == 1 and p in (10, 35) and more:
                    act.drain().then_inc(sems["kq_hi"], 1)
                if half == 1 and p in (40, 43) and more:
                    q_hi(1, (40, 43).index(p))
                    if p == 43:
                        act.drain().then_inc(sems["kq_hi"], 1)
                if p in leaves[half] and (more or PIECES * half + p < 24):
                    evacuate(j, half, *leaves[half][p], attend)

            def half_pair(j, half, more):
                p = 0
                for step in STEPS:
                    if step[0] == "S":
                        exp_scores(j, half, step[1])
                    if step[0] == "T":
                        p_hi(j, half, step[1], step[2])
                    if step[0] == "V" and step[2] == (3, 7)[step[1]]:
                        o_up(j, half, step[1])
                    if step[0] == "D":
                        for _ in range(step[1]):
                            beside(j, half, p, True, more)
                            p += 1

            for p in range(24, PIECES):
                beside(-1, 0, p, False, True)
            for p in range(PIECES):
                beside(-1, 1, p, False, True)
            with act.Fori(0, NPAIR - 1) as j:
                half_pair(j, 0, True)
                half_pair(j, 1, True)
            half_pair(NPAIR - 1, 0, False)
            half_pair(NPAIR - 1, 1, False)

            act.drain()

            def keep_keys(b, pg):
                act.wait_ge(sems["s_kturn"], 2 * PAGES * b + 2 * pg + 1)
                act.wait_ge(sems["s_score"], START["s_score"] + 4 * b + pg // 2 - 1)
                af(KT[:, pg // 2 % 2, 0:4, pg % 2 * P:(pg % 2 + 1) * P], PS[:, 0, :].rearrange("p (i n) -> p i n", i=4),
                   ACT.Copy).then_inc(sems["s_kt0"], 1)

            def sample_batch(b, more):
                for pg in range(3, PAGES):
                    keep_keys(b, pg)
                if more:
                    keep_keys(b + 1, 0)
                else:
                    w_hi(N_B2 % 2, B_B2 - 3, loaded(N_B2))
                for s_ in range(2):
                    act.wait_ge(sems["s_max"], 2 * b + 1 + s_)
                    for col, src, dst in ((4, flat[:, 512 * (2 + 2 * s_):512 * (4 + 2 * s_)], Ps[:, s_, 0:KEYS]),
                                          (6, PS[:, 6, NS * s_:NS * s_ + NS], Ps[:, s_, KEYS:])):
                        af(dst, src, ACT.Exp, bias=small[:, s_:s_ + 1], accum_out=small[:, col + s_:col + s_ + 1])
                    act.drain().then_inc(sems["s_exp"], 1)
                if more:
                    keep_keys(b + 1, 1)
                act.wait_ge(sems["s_pv"], START["s_pv"] + b)
                for r in (0, 2, 4):
                    bank, s_, k0 = P_ROUNDS[r]
                    act.wait_ge(sems["s_back"], 5 * b + r + 1)
                    if k0 == PAGES:
                        af(PsT[0:NS, :, 8, :], PS[0:NS, bank, 0:2 * P].rearrange("p (s n) -> p s n", s=2), ACT.Copy).then_inc(sems["s_pt0"], 1)
                    else:
                        af(PsT[:, s_, k0:k0 + 4, :].rearrange("p t n -> p (t n)"), PS[:, bank, :], ACT.Copy).then_inc(sems["s_pt0"], 1)
                if more:
                    keep_keys(b + 1, 2)

            for pg in range(3):
                keep_keys(0, pg)
            act.wait_ge(sems["y_out"], START["y_out"] + 16 * NPAIR)
            act.wait_ge(sems["kv_out"], START["kv_out"] + 64 * NPAIR)
            with act.Fori(0, DB - 1) as b:
                sample_batch(b, True)
            sample_batch(DB - 1, False)

            act.drain()
            act.wait_ge(sems["y_back"], 16 * KC)
            act.wait_ge(sems["y_merged"], 1)
            split_hi(Y)
            out_tiles(N_B2, B_B2)
            feed(1, N_B3, B_B3, ED_B3, None)
            act.drain()
            act.wait_ge(sems["y_sq"], 1)
            for n, c in ((P, slice(0, 8)), (NS, slice(8, 9))):
                af(rt[0:n, c], PS[0:n, 7, c], ACT.Sqrt, scale=1.0 / D, bias=small[0:n, 31:32]).then_inc(sems["y_root"], 1)
            act.wait_ge(sems["y_inv"], 1)
            for tt in range(9):
                n = P if tt < 8 else NS
                act.wait_ge(sems["y_turned"], 2 * tt + 1)
                af(y_rows(tt)[:, 0:512], PS[0:n, 2 * (tt % 2), :], ACT.Copy, scale=rt[0:n, tt:tt + 1]).then_inc(sems["y_act"], 1)

        @block.vector
        def _(ve):
            for k, n in LEAD["vector"].items():
                ve.sem_inc(sems[k], n)
            tt_, ts_, stt = ve.tensor_tensor, ve.tensor_scalar, ve.scalar_tensor_tensor

            def w_lo(par, n, nk=KC):
                ve.wait_ge(sems["w_hi"], n + 1)
                tt_(wlo[:, par, 0:nk, :], raw[:, par, 0:nk, :], f(whi[:, par, 0:nk, :]), ALU.subtract).then_inc(sems["w_split"], 1)

            def add_square(r, k, par):
                ve.wait_ge(sems[f"n{r}_sq"], k + 1)
                tt_(ss[:, :], ss[:, :], sq[r][par], ALU.add)
                ve.drain().then_inc(sems[f"n{r}_acc"], 1)

            ve.memset(ss[:, :], 0.0)
            ve.wait_ge(sems["g_turned"], 1)
            ve.tensor_copy(GT[:, :, :].rearrange("p k n -> p (k n)"), PS[:, 7, 0:KC * G_N]).then_inc(sems["g_ready"], 1)
            for k in range(KC):
                ve.wait_ge(sems["x_turned"], k + 1)
                ve.tensor_copy(X[:, k, 0:512], PS[:, 3 * (k % 2), :]).then_inc(sems["x_first"], 1)
            for k in range(KC):
                ve.wait_ge(sems["x_turned"], KC + 2 * k + 2)
                ve.tensor_copy(X[:, k, SEQ:], PS[:, 2 + 3 * (k % 2), 0:NS]).then_inc(sems["x_dve"], 1)
                if k:
                    add_square(0, k - 1, (k - 1) % 2)
            add_square(0, KC - 1, 1)
            w_lo(0, 0)

            def reciprocals(r):
                ve.wait_ge(sems[f"n{r}_rt"], NB)
                ve.reciprocal(rs[:, :], rs[:, :])
                ve.drain().then_inc(sems[f"n{r}_inv"], 1)

            def h_lo(src, k, h0):
                ve.wait_ge(sems["h_hi"], h0 + k + 1)
                tt_(Hlo[:, k, :], src, f(Hhi[:, k, :]), ALU.subtract).then_inc(sems["h_ready"], 1)

            def normed(r, h0):
                reciprocals(r)
                for k in range(KC):
                    if k % 2 == 0:
                        ve.drain()
                        tt_(sq[r][0], X[:, k, :], rs[:, :], ALU.mult).then_inc(sems[f"n{r}_even"], 1)
                        if k:
                            h_lo(sq[r][1], k - 1, h0)
                        ve.drain()
                        h_lo(sq[r][0], k, h0)
                h_lo(sq[r][1], KC - 1, h0)

            normed(0, 0)
            ve.drain()
            ve.memset(Up[:, 0:2], 0.0)
            ve.drain()

            def conv_layer(j, last):
                for t in range(4):
                    if last and t == 3:
                        w_lo(N_A2 % 2, N_A2)
                    else:
                        w_lo((t + 1) % 2, 4 * j + t + 1)
                    ve.drain()
                    if t == 1:
                        for b, (s, e) in enumerate(BLK):
                            ve.wait_ge(sems["act_evac"], 6 * j + b + 1)
                            ve.wait_ge(sems["block_done"], START["block_done"] + 12 * j + 3 + b + 1)
                            m = min(e, SEQ)
                            ins = tt_(Up[:, 2 + s:2 + m], PS[:, b, 0:m - s], sA[:, s:m], ALU.mult)
                            if e > SEQ:
                                ins = tt_(Us[:, :, 2:], PS[:, b, SEQ - s:e - s].rearrange("p (b t) -> p b t", b=DB),
                                          sA[:, SEQ:e].rearrange("p (b t) -> p b t", b=DB), ALU.mult)
                            ins.then_inc(sems["dve_evac"], 1)
                        g = lambda r, n=1: GT[:, bass.ds(j, 1), r:r + n].rearrange("p a n -> p (a n)")
                        ve.tensor_copy(Us[:, :, 0:2], g(G_ST, 16).rearrange("p (b w) -> p b w", b=DB))
                        ve.drain()
                        cs = sC[:, SEQ:].rearrange("p (b t) -> p b t", b=DB)
                        for w in range(CW):
                            for dst, src in ((sC[:, 0:SEQ], Up[:, w:w + SEQ]), (cs, Us[:, :, w:w + DS])):
                                if w == 0:
                                    ts_(dst, src, g(G_CW), None, ALU.mult)
                                else:
                                    stt(out=dst, in0=src, scalar=g(G_CW + w), in1=dst, op0=ALU.mult, op1=ALU.add)
                            ve.drain()
                        ucj = at_pair(uc, j).rearrange("p a n -> p (a n)")
                        ve.tensor_copy(ucj[:, 0:2], Up[:, SEQ:SEQ + 2])
                        ve.tensor_copy(ucj[:, 2:18].rearrange("p (b w) -> p b w", b=DB), Us[:, :, DS:])
                    if t == 2:
                        ve.wait_ge(sems["act_evac"], 6 * j + 6)
                        tt_(sC[:, :], sC[:, :], sZ[:, :], ALU.mult)
                        ve.drain()
                    if t == 3:
                        for b, (s, e) in enumerate(BLK):
                            ve.wait_ge(sems["block_done"], START["block_done"] + 12 * j + 9 + b + 1)
                            tt_(at_pair(Y, j).rearrange("p a n -> p (a n)")[:, s:e], PS[:, b, 0:e - s], sC[:, s:e],
                                ALU.mult).then_inc(sems["dve_evac"], 1)
            peeled(ve, KC, conv_layer)

            def split_lo(src, h0):
                for k in range(KC):
                    h_lo(src[:, k, :], k, h0)

            def add_x(m, ps_, s, e):
                x = at_pair(X, m).rearrange("p a n -> p (a n)")[:, s:e] if not isinstance(m, int) else X[:, m, s:e]
                return tt_(x, x, ps_, ALU.add)

            def out_tiles(n0, b0, x_back=False):
                def body(i, last):
                    for u in range(2):
                        n = n0 + u + 1
                        w_lo(n % 2, n + 2 * i, nk=KC + PC if last and u == 1 else KC)
                        if x_back:
                            ve.wait_ge(sems["x_back"], 16 * KC)
                        for b, (s, e) in enumerate(BLK):
                            ve.wait_ge(sems["block_done"], START["block_done"] + b0 + 6 * i + 3 * u + b + 1)
                            add_x(2 * i + u, PS[:, b, 0:e - s], s, e).then_inc(sems["dve_evac"], 1)
                peeled(ve, KC // 2, body)

            def feed(r, n0, b0, ea0, h0):
                for g_ in range(6):
                    ve.wait_ge(sems[f"ple{r}_hi"], g_ + 1)
                    c, h_ = divmod(g_, 3)
                    n = 512 if h_ < 2 else NS
                    tt_(PTl[:, c, h_ * 512:h_ * 512 + n], PS[:, 3 + h_, 0:n], f(PTh[:, c, h_ * 512:h_ * 512 + n]),
                        ALU.subtract).then_inc(sems[f"ple{r}_lo"], 1)
                split_lo(X, h0)
                ve.memset(ss[:, :], 0.0)
                ve.drain()

                def body(i, last):
                    for u in range(2):
                        n = n0 + u + 1
                        if last and u == 1:
                            if r == 0:
                                w_lo(n % 2, N_F)
                        else:
                            w_lo(n % 2, n + 2 * i, nk=KC + PC)
                        for b, (s, e) in enumerate(BLK):
                            ve.wait_ge(sems["act_evac"], ea0 + 6 * i + 3 * u + b + 1)
                            ve.wait_ge(sems["block_done"], START["block_done"] + b0 + 12 * i + 6 * u + 3 + b + 1)
                            tt_(sg[:, u, s:e], sg[:, u, s:e], PS[:, 3 + b, 0:e - s], ALU.mult).then_inc(sems["dve_evac"], 1)
                        ve.drain()
                        add_x(2 * i + u, sg[:, u, :], 0, TT).then_inc(sems["x_sum"], 1)
                        add_square(r + 1, 2 * i + u, u)
                peeled(ve, KC // 2, body)

            split_lo(Y, 8)
            out_tiles(N_A2, B_A2)
            ve.drain()
            feed(0, N_A3, B_A3, EA_A3, 16)
            ve.drain()
            normed(1, 24)

            ve.wait_ge(sems["f_raw"], 1)
            stt(out=fu[:, :], in0=fl[:, :], scalar=-1.0, in1=fl[:, :], op0=ALU.mult, op1=ALU.min).then_inc(sems["f_abs"], 1)
            ve.memset(one16[:, :], 1.0)
            ve.wait_ge(sems["f_ln"], 1)
            stt(out=lfT[:, :], in0=fl[:, :], scalar=0.0, in1=fm[:, :], op0=ALU.min, op1=ALU.subtract)
            ve.drain().then_inc(sems["f_lf"], 1)
            ve.tensor_tensor_scan(fe[:, 0:SEQ], one16[:, :], lfT[:, 0:SEQ], 0.0, ALU.mult, ALU.add)
            ve.tensor_copy(ch[:, 4, :], one16[:, :])
            ve.drain()
            ve.tensor_copy(ch[:, 0, :], fe[:, 0:SEQ])
            ve.drain()
            tt_(ch[:, 1, :], fe[:, 0:SEQ], f(ch[:, 0, :]), ALU.subtract)
            ve.drain()
            ts_(ch[:, 2:4, :], f(ch[:, 0:2, :]), -1.0, None, ALU.mult)
            ve.drain().then_inc(sems["f_aug"], 1)
            ve.wait_ge(sems["f_nat"], 1)
            ve.tensor_copy(lf8[:, :, :], lfn[0:NS, 8, :].unsqueeze(1).to_broadcast([NS, DB, H])).then_inc(sems["s_lf8"], 1)
            w_lo(N_B1 % 2, N_B1)
            ve.wait_ge(sems["s_cn"], 1)
            ve.tensor_copy(cn[:, :], PS[0:NS, 5, P:P + H])
            ve.tensor_copy(RTs[:, 0, 0:KEYS], S[:, 0:KEYS])
            ts_(RTs[:, 0, KEYS:], PS[:, 5, 0:NS], -1.0, None, ALU.mult)
            ve.drain()
            tt_(RTs[:, 1, 0:KEYS], S[:, 0:KEYS], f(RTs[:, 0, 0:KEYS]), ALU.subtract)
            stt(out=RTs[:, 1, KEYS:], in0=PS[:, 5, 0:NS], scalar=-1.0, in1=f(RTs[:, 0, KEYS:]), op0=ALU.mult, op1=ALU.subtract)
            ve.drain().then_inc(sems["s_restsb"], 1)

            def row_max(j, hh, qb):
                n = (qb + 1) * P
                ve.wait_ge(sems["score"], START["score"] + 16 * j + 8 * hh + qb + 1)
                ve.reduce_max(small[:, qb:qb + 1], score_bank(qb)[:, 0:n], AXX, negate=True).then_inc(sems["rowmax"], 1)

            def row_sum(j, hh, qb):
                ve.wait_ge(sems["exp"], START["exp"] + 16 * j + 8 * hh + qb + 1)
                ve.reciprocal(small[:, 16 + qb:17 + qb], small[:, 8 + qb:9 + qb]).then_inc(sems["rinv"], 1)

            def p_lo(j, hh, grp, kb):
                u = 12 * hh + 4 * grp + kb
                q0 = max(0, kb - QG * grp)
                ve.wait_ge(sems["p_hi"], 24 * j + u + 1)
                tt_(pTl[:, kb % 2, q0 * P:512], PS[:, 5 + kb % 2, q0 * P:512], f(pTh[:, kb % 2, q0 * P:512]),
                    ALU.subtract).then_inc(sems["p_lo"], 1)

            def output(j, hh, grp):
                hs, cols = slice(64 * hh, 64 * hh + 64), slice(512 * grp, 512 * grp + 512)
                ve.wait_ge(sems["o_up"], 4 * j + 2 * hh + grp + 1)
                tt_(yT[hs, cols], PS[0:64, 7, :], yT[hs, cols], ALU.add)
                ve.drain().then_inc(sems["o_free"], 1)
                tt_(yT[hs, cols], yT[hs, cols], zf[hs, cols], ALU.mult).then_inc(sems["o_done"], 1)

            def keep_part(j, t, i):
                if i == 0:
                    ve.wait_ge(sems["kv_out"], START["kv_out"] + 64 * j + 32 * t)
                    if t == 0:
                        ve.wait_ge(sems["v_hi"], j)
                ve.wait_ge(sems["kv_turned"], 6 * j + 3 * t + i + 1)
                if i < 2:
                    x, n = TURN_PARTS[i][0], len(TURN_PARTS[i])
                    ve.tensor_copy(KN[:, x:x + n, :].rearrange("p t n -> p (t n)"), PS[:, 5 + i, 0:n * P]).then_inc(sems["kv_nat"], 1)
                else:
                    ve.tensor_copy(KN[:, 7, :], PS[:, 5, 0:P])
                    if t == 1:
                        ve.tensor_copy(vnew[:, bass.ds(P * j, P)], PS[0:NS, 5, P:2 * P])
                    ve.tensor_copy(KN[0:NS, 8, :], PS[0:NS, 5, P:2 * P])
                    ve.drain().then_inc(sems["kv_nat"], 1)

            def k_lo(hh):
                hs = slice(64 * hh, 64 * hh + 64)
                tt_(KB[0:HD, hh, :], stK[hs, 0:SEQ], f(KA[hs, hh, :]), ALU.subtract)

            def q_lo(hh):
                hs, other = slice(64 * hh, 64 * hh + 64), slice(64 - 64 * hh, 128 - 64 * hh)
                tt_(QA[other, hh, :], stQ[hs, 0:SEQ], f(QA[hs, hh, :]), ALU.subtract)

            def q_sample(j, hh):
                hs = slice(64 * hh, 64 * hh + 64)
                if isinstance(j, int) and hh == 0:
                    ve.wait_ge(sems["qd_zero"], 1)
                ve.tensor_copy(qd[hs, bass.ds(j, 1), :, DS * hh:DS * hh + DS].rearrange("p a b t -> p (a b) t"),
                               stQ[hs, SEQ:].rearrange("p (b t) -> p b t", b=DB))

            def beside(j, half, p, attend, more):
                i = 2 * half + p // 24
                if p % 24 == 17 and more:
                    w_lo((N_B1 + i) % 2, N_B1 + 4 * j + 3 + i + 1)
                if half == 0 and p == 6 and attend:
                    ve.wait_ge(sems["v_hi"], j + 1)
                    tt_(VS[:, :, :, HD:], KN[:, 0:8, :].rearrange("p t (h n) -> p t h n", h=2),
                        f(VS[:, :, :, 0:HD]), ALU.subtract).then_inc(sems["v_lo"], 1)
                if half == 1 and p == 14 and more:
                    ve.wait_ge(sems["kq_hi"], 4 * j + 5)
                    k_lo(0)
                    ve.tensor_copy(at_pair(knT, j + 1).rearrange("p a n -> p (a n)"), stK[:, SEQ:])
                    ve.drain().then_inc(sems["kq_lo"], 1)
                if half == 1 and p == 29 and more:
                    ve.wait_ge(sems["kq_hi"], 4 * j + 6)
                    q_lo(0)
                    q_sample(j + 1, 0)
                    ve.drain().then_inc(sems["kq_lo"], 1)
                if half == 1 and p == 37 and more:
                    ve.wait_ge(sems["kq_hi"], 4 * j + 7)
                    k_lo(1)
                if half == 1 and p == 44 and more:
                    ve.wait_ge(sems["kq_hi"], 4 * j + 8)
                    q_lo(1)
                    q_sample(j + 1, 1)
                    ve.drain().then_inc(sems["kq_lo"], 1)
                if half == 0 and attend and p == 25:
                    ve.wait_ge(sems["z_done"], j + 1)
                    ve.tensor_copy(at_pair(zsS, j).rearrange("p a n -> p (a n)"), zf[:, SEQ:])

            def half_pair(j, half, more):
                p = 0
                for step in STEPS:
                    if step[0] == "S":
                        if step[1] >= 4:
                            row_sum(j, half, step[1] - 1)
                        row_max(j, half, step[1])
                        if 1 <= step[1] < 4:
                            row_sum(j, half, step[1] - 1)
                    if step[0] == "N" and (half == 0 or more):
                        keep_part(j + half, 1 - half, step[1])
                    if step[0] == "T":
                        p_lo(j, half, step[1], step[2])
                    if step[0] == "V" and step[2] == (3, 7)[step[1]]:
                        output(j, half, step[1])
                    if step[0] == "D":
                        for _ in range(step[1]):
                            beside(j, half, p, True, more)
                            if p == 29:
                                row_sum(j, half, 7)
                            p += 1

            for p in range(24, PIECES):
                beside(-1, 0, p, False, True)
            for p in range(PIECES):
                beside(-1, 1, p, False, True)
                if p == 8:
                    for i in range(3):
                        keep_part(0, 0, i)
            with ve.Fori(0, NPAIR - 1) as j:
                half_pair(j, 0, True)
                half_pair(j, 1, True)
            half_pair(NPAIR - 1, 0, False)
            half_pair(NPAIR - 1, 1, False)

            ve.drain()
            ve.wait_ge(sems["block_done"], START["block_done"] + B_B2)

            def keep_keys(b, pg):
                ve.wait_ge(sems["s_kturn"], 2 * PAGES * b + 2 * pg + 2)
                ve.wait_ge(sems["s_score"], START["s_score"] + 4 * b + pg // 2 - 1)
                ve.tensor_copy(KT[:, pg // 2 % 2, 4:8, pg % 2 * P:(pg % 2 + 1) * P],
                               PS[:, 1, :].rearrange("p (i n) -> p i n", i=4)).then_inc(sems["s_kt1"], 1)

            def prepare(b):
                rows = lambda x: x[:, :, 0:16].rearrange("p i (h q) -> p i h q", h=2)
                ve.tensor_copy(qc[:, :, 0:16], qd[:, :, bass.ds(b, 1), :].rearrange("p i b n -> p i (b n)"))
                ve.tensor_copy(rows(pick), ident[:, bass.ds(H * b, H)].rearrange("p (i h) -> p i h", h=2).unsqueeze(3)
                               .to_broadcast([P, NPAIR, 2, DS]))
                own = ident[0:NS, bass.ds(DS * b, DS)]
                for hh in range(2):
                    ve.tensor_copy(mq[:, :, 8 * hh:8 * hh + 8], own.unsqueeze(1).to_broadcast([NS, 4, DS]))
                    tt_(cq[:, :, 8 * hh:8 * hh + 8], own.unsqueeze(1).to_broadcast([NS, NPAIR, DS]),
                        cn[:, :].rearrange("p (i h) -> p i h", h=2)[:, :, hh:hh + 1].to_broadcast([NS, NPAIR, DS]), ALU.mult)
                ve.drain()
                ve.tensor_copy(cqh[:, :, :], cq[:, :, :])
                ve.drain()
                tt_(cql[:, :, :], cq[:, :, :], f(cqh[:, :, :]), ALU.subtract)
                ve.drain().then_inc(sems["s_prep"], 1)

            def sample_batch(b, more):
                for pg in range(3, PAGES):
                    keep_keys(b, pg)
                ve.wait_ge(sems["s_all"], b + 1)
                ve.reduce_max(small[:, 2:4], PS[:, 6, 0:2 * NS].rearrange("p (s n) -> p s n", s=2), AXX, negate=True)
                for s_ in range(2):
                    ve.reduce_max(small[:, s_:s_ + 1], flat[:, 512 * (2 + 2 * s_):512 * (4 + 2 * s_)], AXX, negate=True)
                    ve.drain()
                    tt_(small[:, s_:s_ + 1], small[:, s_:s_ + 1], small[:, 2 + s_:3 + s_], ALU.min).then_inc(sems["s_max"], 1)
                    if more:
                        keep_keys(b + 1, s_)
                ve.wait_ge(sems["s_exp"], START["s_exp"] + 2 * b + 2)
                tt_(small[:, 8:10], small[:, 4:6], small[:, 6:8], ALU.add)
                ve.drain()
                ve.reciprocal(small[:, 8:10], small[:, 8:10])
                ve.wait_ge(sems["s_pv"], START["s_pv"] + b)
                for r in (1, 3):
                    bank, s_, k0 = P_ROUNDS[r]
                    ve.wait_ge(sems["s_back"], 5 * b + r + 1)
                    ve.tensor_copy(PsT[:, s_, k0:k0 + 4, :].rearrange("p t n -> p (t n)"), PS[:, bank, :]).then_inc(sems["s_pt1"], 1)
                if more:
                    prepare(b + 1)
                else:
                    w_lo(N_B2 % 2, N_B2)
                ve.drain()
                ve.wait_ge(sems["s_pv"], START["s_pv"] + b + 1)
                for s_ in range(2):
                    ts_(Osb[:, s_, :], PS[:, 6, P * (1 + s_):P * (2 + s_)], small[:, 8 + s_:9 + s_], None, ALU.mult)
                ve.drain().then_inc(sems["s_osb"], 1)
                if more:
                    keep_keys(b + 1, 2)
                ve.wait_ge(sems["s_yturn"], b + 1)
                for hh in range(2):
                    hs = slice(64 * hh, 64 * hh + 64)
                    z = zsS[hs, :, bass.ds(DS * b, DS)]
                    ins = tt_(z, PS[hs, 7, 0:2 * P].rearrange("p (i n) -> p i n", n=32)[:, :, DS * hh:DS * hh + DS], z, ALU.mult)
                ins.then_inc(sems["s_out"], 1)

            for x in (qc, cq, mq):
                ve.memset(x[:, :, :], 0.0)
            ve.drain()
            ve.tensor_copy(pick[:, :, :], qc[:, :, :])
            ve.tensor_copy(onesr[:, :], ones[0:NS, 0:1].to_broadcast([NS, 512]))
            ve.drain()
            prepare(0)
            for pg in range(3):
                keep_keys(0, pg)
            ve.wait_ge(sems["y_out"], START["y_out"] + 16 * NPAIR)
            ve.wait_ge(sems["kv_out"], START["kv_out"] + 64 * NPAIR)
            with ve.Fori(0, DB - 1) as b:
                sample_batch(b, True)
            sample_batch(DB - 1, False)

            ve.drain()
            ve.tensor_copy(Y[:, :, SEQ:], zsS[:, :, :])
            ve.drain().then_inc(sems["y_merged"], 1)
            split_lo(Y, 32)
            out_tiles(N_B2, B_B2, x_back=True)
            ve.drain()
            feed(1, N_B3, B_B3, EA_B3, 40)
            ve.drain()
            ve.wait_ge(sems["y_root"], 2)
            ve.reciprocal(rt[:, 0:8], rt[:, 0:8])
            ve.reciprocal(rt[0:NS, 8:9], rt[0:NS, 8:9])
            ve.drain().then_inc(sems["y_inv"], 1)
            for tt in range(9):
                n = P if tt < 8 else NS
                ve.wait_ge(sems["y_turned"], 2 * tt + 2)
                ts_(y_rows(tt)[:, 512:D], PS[0:n, 2 * (tt % 2) + 1, :], rt[0:n, tt:tt + 1], None, ALU.mult).then_inc(sems["y_dve"], 1)


INS = ["x_prompt", "x_sample", "p_prompt", "p_sample", "state_conv", "cache_k", "cache_v", "cache_logf",
       "page_table", "norm_a", "w_in_a", "conv_w_a", "w_out_a", "norm_kv", "w_kv", "b_f", "norm_b",
       "w_in_b", "w_out_b", "w_ple_proj", "w_ple_gate", "norm_f"]
OUTS = [("y_prompt", (1, SEQ, D)), ("y_sample", (DB, DS, D)), ("conv_prompt", (1, 1, CW - 1, D)),
        ("k_prompt", (1, SEQ, H, HD)), ("v_prompt", (1, SEQ, H, HD)), ("logf_prompt", (1, SEQ, H)),
        ("conv_sample", (1, DB, CW - 1, D)), ("k_sample", (DB, DS, H, HD)), ("v_sample", (DB, DS, H, HD)),
        ("logf_sample", (DB, DS, H))]


def kernel(**inputs):
    import concourse.bacc as bacc
    from concourse.bass_utils import run_bass_kernel_spmd

    nc = bacc.Bacc("TRN2", target_bir_lowering=False, num_devices=1)
    arrays, a, o = {}, {}, {}
    for name in INS:
        x = np.ascontiguousarray(inputs[name])
        arrays[f"in_{name}"] = x
        a[name] = nc.dram_tensor(f"in_{name}", x.shape, mybir.dt.from_np(x.dtype), kind="ExternalInput").ap()
    for name, shape in OUTS:
        o[name] = nc.dram_tensor(f"out_{name}", shape, F32, kind="ExternalOutput").ap()
    d = {"x": nc.dram_tensor("parked_x", (KC, P, TT), F32, kind="Internal").ap(),
         "y": nc.dram_tensor("parked_y", (KC, P, SEQ), F32, kind="Internal").ap(),
         "rest": nc.dram_tensor("key_bias", (P, 2, KEYS + NS), F32, kind="Internal").ap(),
         "augk": nc.dram_tensor("aug_k", (H, AUG, SEQ), F32, kind="Internal").ap(),
         "augq": nc.dram_tensor("aug_q", (H, AUG, SEQ), F32, kind="Internal").ap()}
    program(nc, a, o, d)
    r = run_bass_kernel_spmd(nc, [arrays], core_ids=[0])
    return tuple(r.results[0][f"out_{name}"] for name, _ in OUTS)
```
